# Optimizing a Trainium2 kernel written in Bass

```python
import math
import jax
import jax.numpy as jnp
from jax import lax
import numpy as np
import jax, jax.numpy as jnp

D_MODEL = 2048
BATCH = 1
SEQ = 256
DEPTH = 1

HEAD_DIM = 128
NSA_HEADS = 8
NSA_KV_HEADS = 2
CMP_LEN = 32
CMP_STRIDE = 16
CMP_HIDDEN = 2 * HEAD_DIM
SEL_BLOCK = 64
SEL_TOP_N = 16
NSA_WINDOW = 512
NSA_Q_CHUNK = 64
SWA_HEADS = 8
SWA_KV_HEADS = 2
SWA_WINDOW = 128
MOBA_HEADS = 8
MOBA_KV_HEADS = 2
MOBA_BLOCK = 256
MOBA_TOP_K = 3
MOBA_Q_CHUNK = 16
BAND_BLOCK = 128
N_BUCKETS = 32
BUCKET_MAX_DIST = 128
TOTAL_HEADS = NSA_HEADS + SWA_HEADS + MOBA_HEADS
N_BRANCHES = 3
MIX_WIDTH = NSA_HEADS * HEAD_DIM
D_FF = 4 * D_MODEL
RMS_EPS = 1e-6
NEG_INF = -1e30
FORCE_SCORE = 1e30
TINY = 1e-30

SPLIT_SIZES = (
    NSA_HEADS * HEAD_DIM,
    NSA_KV_HEADS * HEAD_DIM,
    NSA_KV_HEADS * HEAD_DIM,
    NSA_KV_HEADS * HEAD_DIM,
    NSA_KV_HEADS * HEAD_DIM,
    NSA_KV_HEADS * HEAD_DIM,
    NSA_KV_HEADS * HEAD_DIM,
    NSA_HEADS * 3,
    SWA_HEADS * HEAD_DIM,
    SWA_KV_HEADS * HEAD_DIM,
    SWA_KV_HEADS * HEAD_DIM,
    MOBA_HEADS * HEAD_DIM,
    MOBA_KV_HEADS * HEAD_DIM,
    MOBA_KV_HEADS * HEAD_DIM,
    N_BRANCHES * D_MODEL,
)
SPLIT_POINTS = tuple(int(v) for v in np.cumsum(SPLIT_SIZES)[:-1])
D_IN = sum(SPLIT_SIZES)


def rms_norm(x, gain):
    x32 = x.astype(jnp.float32)
    y = x32 * lax.rsqrt(jnp.mean(x32 * x32, axis=-1, keepdims=True) + RMS_EPS)
    return (y * gain.astype(jnp.float32)).astype(x.dtype)

def t5_bucket(dist):
    n = jnp.maximum(dist, 0)
    exact = N_BUCKETS // 2
    log_ratio = jnp.log(jnp.maximum(n, 1).astype(jnp.float32) / exact) / math.log(BUCKET_MAX_DIST / exact)
    large = jnp.minimum(exact + (log_ratio * (N_BUCKETS - exact)).astype(jnp.int32), N_BUCKETS - 1)
    return jnp.where(n < exact, n, large)

def masked_softmax(logits, mask, sink=None):
    logits = jnp.where(mask, logits, NEG_INF)
    m = jnp.max(logits, axis=-1, keepdims=True)
    if sink is not None:
        m = jnp.maximum(m, sink)
    p = jnp.where(mask, jnp.exp(logits - m), 0.0)
    denom = jnp.sum(p, axis=-1, keepdims=True)
    if sink is not None:
        denom = denom + jnp.exp(sink - m)
    return p / jnp.maximum(denom, TINY)

def split_heads(t, n_heads):
    return t.reshape(t.shape[0], t.shape[1], n_heads, HEAD_DIM)

def banded_attention(q, k, v, bias_tbl, window, sinks=None):
    b, s, h, d = q.shape
    n_kv = k.shape[2]
    g = h // n_kv
    nb = s // BAND_BLOCK
    pad = -(-(window - 1) // BAND_BLOCK) * BAND_BLOCK
    span = BAND_BLOCK + pad
    key_idx = jnp.arange(nb)[:, None] * BAND_BLOCK + jnp.arange(span)[None, :]
    padding = ((0, 0), (pad, 0), (0, 0), (0, 0))
    kp = jnp.pad(k, padding)[:, key_idx]
    vp = jnp.pad(v, padding)[:, key_idx]
    qb = q.reshape(b, nb, BAND_BLOCK, n_kv, g, d)
    logits = jnp.einsum('bnqkgd,bnlkd->bnkgql', qb, kp, preferred_element_type=jnp.float32) * (d ** -0.5)
    dist = (jnp.arange(BAND_BLOCK)[:, None] + pad) - jnp.arange(span)[None, :]
    bias = jnp.transpose(bias_tbl[t5_bucket(dist)], (2, 0, 1)).reshape(n_kv, g, BAND_BLOCK, span)
    logits = logits + bias.astype(jnp.float32)
    mask = ((dist >= 0) & (dist < window))[None] & (key_idx >= pad)[:, None, :]
    mask = mask[None, :, None, None]
    sink = None
    if sinks is not None:
        sink = sinks.astype(jnp.float32).reshape(n_kv, g, 1, 1)
    p = masked_softmax(logits, mask, sink)
    out = jnp.einsum('bnkgql,bnlkd->bnqkgd', p.astype(v.dtype), vp)
    return out.reshape(b, s, h, d)

def nsa_compress(kv, pos_emb, w1, w2):
    b, s, n_kv, d = kv.shape
    n_cmp = (s - CMP_LEN) // CMP_STRIDE + 1
    idx = jnp.arange(n_cmp)[:, None] * CMP_STRIDE + jnp.arange(CMP_LEN)[None, :]
    blocks = kv[:, idx] + pos_emb[None, None, :, None, :]
    blocks = jnp.moveaxis(blocks, 3, 2).reshape(b, n_cmp, n_kv, CMP_LEN * d)
    return jax.nn.gelu(blocks @ w1) @ w2

def selection_weights(n_cmp, n_sel):
    starts = np.arange(n_cmp)[:, None] * CMP_STRIDE
    blk = np.arange(n_sel)[None, :] * SEL_BLOCK
    shared = np.clip(np.minimum(starts + CMP_LEN, blk + SEL_BLOCK) - np.maximum(starts, blk), 0, None)
    return (shared / CMP_STRIDE).astype(np.float32)

def nsa_selected_attention(qg, k_sel, v_sel, sel_idx, bias_tbl):
    b, s, n_kv, g, d = qg.shape
    n_top = sel_idx.shape[-1]
    n_sel = s // SEL_BLOCK
    n_keys = n_top * SEL_BLOCK
    scale = d ** -0.5
    kb = jnp.moveaxis(k_sel.reshape(b, n_sel, SEL_BLOCK, n_kv, d), 3, 1)
    vb = jnp.moveaxis(v_sel.reshape(b, n_sel, SEL_BLOCK, n_kv, d), 3, 1)
    tbl = jnp.moveaxis(bias_tbl.reshape(N_BUCKETS, n_kv, g), 0, 1)
    n_chunk = s // NSA_Q_CHUNK
    q_chunks = jnp.moveaxis(qg.reshape(b, n_chunk, NSA_Q_CHUNK, n_kv, g, d), 1, 0)
    idx_chunks = jnp.moveaxis(sel_idx.reshape(b, n_kv, n_chunk, NSA_Q_CHUNK, n_top), 2, 0)
    starts = jnp.arange(n_chunk) * NSA_Q_CHUNK
    bi = jnp.arange(b)[:, None, None, None]
    kvi = jnp.arange(n_kv)[None, :, None, None]
    pos_in_blk = jnp.arange(SEL_BLOCK)

    def chunk(xs):
        q_c, idx_c, start = xs
        t_c = start + jnp.arange(NSA_Q_CHUNK)
        k_c = kb[bi, kvi, idx_c]
        v_c = vb[bi, kvi, idx_c]
        dist = t_c[:, None, None] - (idx_c[..., None] * SEL_BLOCK + pos_in_blk)
        bias = jnp.moveaxis(tbl[kvi[..., None], t5_bucket(dist)], -1, 2)
        logits = jnp.einsum('bqkgd,bkqnld->bkgqnl', q_c, k_c, preferred_element_type=jnp.float32) * scale + bias
        mask = (dist >= 0)[:, :, None]
        p = masked_softmax(logits.reshape(b, n_kv, g, NSA_Q_CHUNK, n_keys),
                           mask.reshape(b, n_kv, 1, NSA_Q_CHUNK, n_keys))
        return jnp.einsum('bkgqm,bkqmd->bqkgd', p.astype(v_sel.dtype),
                          v_c.reshape(b, n_kv, NSA_Q_CHUNK, n_keys, d))

    out = lax.map(chunk, (q_chunks, idx_chunks, starts))
    return jnp.moveaxis(out, 0, 1).reshape(b, s, n_kv * g, d)

def nsa_attention(q, k_cmp, v_cmp, k_sel, v_sel, k_win, v_win, gate_logits, cmp_pos, cmp_w1, cmp_w2, bias_tbl):
    b, s, h, d = q.shape
    n_kv = k_cmp.shape[2]
    g = h // n_kv
    scale = d ** -0.5
    qg = q.reshape(b, s, n_kv, g, d)
    t = jnp.arange(s)
    kc = nsa_compress(k_cmp, cmp_pos[0], cmp_w1[0], cmp_w2[0])
    vc = nsa_compress(v_cmp, cmp_pos[1], cmp_w1[1], cmp_w2[1])
    n_cmp = kc.shape[1]
    dist_c = t[:, None] - (jnp.arange(n_cmp) * CMP_STRIDE + CMP_LEN - 1)[None, :]
    bias_c = jnp.moveaxis(bias_tbl[t5_bucket(dist_c)], -1, 0).reshape(n_kv, g, s, n_cmp)
    logits_c = jnp.einsum('bskgd,bckd->bkgsc', qg, kc, preferred_element_type=jnp.float32) * scale + bias_c
    p_cmp = masked_softmax(logits_c, dist_c >= 0)
    o_cmp = jnp.einsum('bkgsc,bckd->bskgd', p_cmp.astype(vc.dtype), vc).reshape(b, s, h, d)
    n_sel = s // SEL_BLOCK
    n_top = min(SEL_TOP_N, n_sel)
    share = jnp.asarray(selection_weights(n_cmp, n_sel))
    importance = jnp.einsum('bkgsc,cj->bksj', p_cmp, share)
    blk = jnp.arange(n_sel)[None, :]
    cur = (t // SEL_BLOCK)[:, None]
    forced = (blk == 0) | (blk == cur) | (blk == cur - 1)
    score = jnp.where(forced, FORCE_SCORE, jnp.where(blk <= cur, importance, NEG_INF))
    _, sel_idx = lax.top_k(score, n_top)
    o_sel = nsa_selected_attention(qg, k_sel, v_sel, sel_idx, bias_tbl)
    o_win = banded_attention(q, k_win, v_win, bias_tbl, NSA_WINDOW)
    gate = jax.nn.sigmoid(gate_logits.astype(jnp.float32)).reshape(b, s, h, 3).astype(q.dtype)
    out = gate[..., 0:1] * o_cmp + gate[..., 1:2] * o_sel + gate[..., 2:3] * o_win
    return out.reshape(b, s, h * d)

def moba_attention(q, k, v, bias_tbl):
    b, s, h, d = q.shape
    n_kv = k.shape[2]
    g = h // n_kv
    scale = d ** -0.5
    n_blk = -(-s // MOBA_BLOCK)
    padding = ((0, 0), (0, n_blk * MOBA_BLOCK - s), (0, 0), (0, 0))
    kb = jnp.moveaxis(jnp.pad(k, padding).reshape(b, n_blk, MOBA_BLOCK, n_kv, d), 3, 1)
    vb = jnp.moveaxis(jnp.pad(v, padding).reshape(b, n_blk, MOBA_BLOCK, n_kv, d), 3, 1)
    qg = q.reshape(b, s, n_kv, g, d)
    tbl = jnp.transpose(bias_tbl.reshape(N_BUCKETS, n_kv, g), (1, 2, 0))
    n_top = min(MOBA_TOP_K, n_blk - 1)
    n_chunk = s // MOBA_Q_CHUNK
    q_chunks = jnp.moveaxis(qg.reshape(b, n_chunk, MOBA_Q_CHUNK, n_kv, g, d), 1, 0)
    starts = jnp.arange(n_chunk) * MOBA_Q_CHUNK
    pos_in_blk = jnp.arange(MOBA_BLOCK)
    bi = jnp.arange(b)[:, None, None, None, None]
    kvi = jnp.arange(n_kv)[None, :, None, None, None]
    gi = jnp.arange(g)[None, None, :, None, None]

    def own_block(q_c, start):
        t_c = start + jnp.arange(MOBA_Q_CHUNK)
        blk = start // MOBA_BLOCK
        k_own = lax.dynamic_index_in_dim(kb, blk, axis=2, keepdims=False)
        v_own = lax.dynamic_index_in_dim(vb, blk, axis=2, keepdims=False)
        dist = t_c[:, None] - (blk * MOBA_BLOCK + pos_in_blk)[None, :]
        logits = jnp.einsum('bqkgd,bkld->bkgql', q_c, k_own, preferred_element_type=jnp.float32) * scale
        logits = logits + tbl[:, :, t5_bucket(dist)]
        mask = jnp.broadcast_to(dist >= 0, logits.shape)
        return logits, mask, v_own, t_c

    if n_top > 0:
        t = jnp.arange(s)
        q_blk = t // MOBA_BLOCK
        k_mean = jnp.mean(kb, axis=3)
        gate = jnp.einsum('bskgd,bknd->bkgsn', qg, k_mean, preferred_element_type=jnp.float32)
        gate = jnp.where(jnp.arange(n_blk)[None, :] < q_blk[:, None], gate, NEG_INF)
        _, sel_idx = lax.top_k(gate, n_top)
        valid = sel_idx < q_blk[:, None]
        idx_chunks = jnp.moveaxis(sel_idx.reshape(b, n_kv, g, n_chunk, MOBA_Q_CHUNK, n_top), 3, 0)
        valid_chunks = jnp.moveaxis(valid.reshape(b, n_kv, g, n_chunk, MOBA_Q_CHUNK, n_top), 3, 0)
        n_sel_keys = n_top * MOBA_BLOCK

        def chunk(xs):
            q_c, start, idx_c, valid_c = xs
            logits_own, mask_own, v_own, t_c = own_block(q_c, start)
            k_sel = kb[bi, kvi, idx_c]
            v_sel = vb[bi, kvi, idx_c]
            dist = t_c[:, None, None] - (idx_c[..., None] * MOBA_BLOCK + pos_in_blk)
            bias = tbl[kvi[..., None], gi[..., None], t5_bucket(dist)]
            logits_sel = jnp.einsum('bqkgd,bkgqnld->bkgqnl', q_c, k_sel, preferred_element_type=jnp.float32) * scale + bias
            logits_sel = logits_sel.reshape(b, n_kv, g, MOBA_Q_CHUNK, n_sel_keys)
            mask_sel = jnp.broadcast_to(valid_c[..., None], dist.shape).reshape(logits_sel.shape)
            p = masked_softmax(jnp.concatenate([logits_sel, logits_own], axis=-1),
                               jnp.concatenate([mask_sel, mask_own], axis=-1)).astype(v.dtype)
            o_sel = jnp.einsum('bkgqm,bkgqmd->bqkgd', p[..., :n_sel_keys],
                               v_sel.reshape(b, n_kv, g, MOBA_Q_CHUNK, n_sel_keys, d))
            o_own = jnp.einsum('bkgql,bkld->bqkgd', p[..., n_sel_keys:], v_own)
            return o_sel + o_own

        out = lax.map(chunk, (q_chunks, starts, idx_chunks, valid_chunks))
    else:
        def chunk(xs):
            q_c, start = xs
            logits_own, mask_own, v_own, _ = own_block(q_c, start)
            p = masked_softmax(logits_own, mask_own).astype(v.dtype)
            return jnp.einsum('bkgql,bkld->bqkgd', p, v_own)

        out = lax.map(chunk, (q_chunks, starts))
    return jnp.moveaxis(out, 0, 1).reshape(b, s, h, d)

def first_inputs(seed: int = 0) -> dict:
    key = jax.random.key(seed)
    ks = jax.random.split(key, 14)

    def nrm(k, shape, scale):
        return jax.random.normal(k, shape, jnp.float32) * scale

    out_scale = (2 * DEPTH) ** -0.5
    return {
        'x': nrm(ks[0], (BATCH, SEQ, D_MODEL), 1.0),
        'w_in': nrm(ks[1], (DEPTH, D_MODEL, D_IN), D_MODEL ** -0.5),
        'cmp_pos': nrm(ks[2], (DEPTH, 2, CMP_LEN, HEAD_DIM), 0.1),
        'cmp_w1': nrm(ks[3], (DEPTH, 2, CMP_LEN * HEAD_DIM, CMP_HIDDEN), (CMP_LEN * HEAD_DIM) ** -0.5),
        'cmp_w2': nrm(ks[4], (DEPTH, 2, CMP_HIDDEN, HEAD_DIM), CMP_HIDDEN ** -0.5),
        'swa_sinks': nrm(ks[5], (DEPTH, SWA_HEADS), 1.0),
        'w_branch': nrm(ks[6], (DEPTH, N_BRANCHES, MIX_WIDTH, D_MODEL), MIX_WIDTH ** -0.5),
        'w_out': nrm(ks[7], (DEPTH, D_MODEL, D_MODEL), D_MODEL ** -0.5 * out_scale),
        'w_mlp_in': nrm(ks[8], (DEPTH, D_MODEL, D_FF), D_MODEL ** -0.5),
        'w_mlp_out': nrm(ks[9], (DEPTH, D_FF, D_MODEL), D_FF ** -0.5 * out_scale),
        'norm_mix': 1.0 + nrm(ks[10], (DEPTH, D_MODEL), 0.02),
        'norm_mlp': 1.0 + nrm(ks[11], (DEPTH, D_MODEL), 0.02),
        'norm_final': 1.0 + nrm(ks[12], (D_MODEL,), 0.02),
        'rel_bias': nrm(ks[13], (N_BUCKETS, TOTAL_HEADS), 0.5),
    }

def first_block(x, w_in, cmp_pos, cmp_w1, cmp_w2, swa_sinks, w_branch, w_out, w_mlp_in, w_mlp_out,
              norm_mix, norm_mlp, norm_final, rel_bias):
    b, s, _ = x.shape
    bias_a = rel_bias[:, :NSA_HEADS]
    bias_b = rel_bias[:, NSA_HEADS:NSA_HEADS + SWA_HEADS]
    bias_c = rel_bias[:, NSA_HEADS + SWA_HEADS:]
    for layer in range(DEPTH):
        h = rms_norm(x, norm_mix[layer])
        (a_q, a_kc, a_vc, a_ks, a_vs, a_kw, a_vw, a_gate,
         b_q, b_k, b_v, c_q, c_k, c_v, merge_gate) = jnp.split(h @ w_in[layer], SPLIT_POINTS, axis=-1)
        o_a = nsa_attention(split_heads(a_q, NSA_HEADS),
                            split_heads(a_kc, NSA_KV_HEADS), split_heads(a_vc, NSA_KV_HEADS),
                            split_heads(a_ks, NSA_KV_HEADS), split_heads(a_vs, NSA_KV_HEADS),
                            split_heads(a_kw, NSA_KV_HEADS), split_heads(a_vw, NSA_KV_HEADS),
                            a_gate, cmp_pos[layer], cmp_w1[layer], cmp_w2[layer], bias_a)
        o_b = banded_attention(split_heads(b_q, SWA_HEADS), split_heads(b_k, SWA_KV_HEADS),
                               split_heads(b_v, SWA_KV_HEADS), bias_b, SWA_WINDOW,
                               swa_sinks[layer]).reshape(b, s, MIX_WIDTH)
        o_c = moba_attention(split_heads(c_q, MOBA_HEADS), split_heads(c_k, MOBA_KV_HEADS),
                             split_heads(c_v, MOBA_KV_HEADS), bias_c).reshape(b, s, MIX_WIDTH)
        branches = jnp.stack([o_a, o_b, o_c], axis=2)
        y = jnp.einsum('bsmc,mcd->bsmd', branches, w_branch[layer])
        gate = jax.nn.sigmoid(merge_gate.reshape(b, s, N_BRANCHES, D_MODEL))
        x = x + jnp.sum(gate * y, axis=2) @ w_out[layer]
        h = rms_norm(x, norm_mlp[layer])
        x = x + jnp.square(jax.nn.relu(h @ w_mlp_in[layer])) @ w_mlp_out[layer]
    return rms_norm(x, norm_final)


DEPTH_2 = 2

GRID_W = 64
CTX_LEN = 256
Q_BLOCK = 128
ROPE_BASE = 10000.0
EPS = 1e-6
NEG_INF_2 = -1e30

A_HEADS = 8
A_QK_DIM = 64
A_V_DIM = 128
B_HEADS = 8
B_KV_HEADS = 2
WINDOW = 128
NBAND = (WINDOW + Q_BLOCK - 1) // Q_BLOCK
PAD = NBAND * Q_BLOCK
BAND = (2 * NBAND + 1) * Q_BLOCK
C_HEADS = 8
C_KV_HEADS = 2
D_HEADS = 8
D_Q_RANK = 512
D_KV_RANK = 256
D_NOPE = 128
D_ROPE = 64
D_V = 128

A_Q = A_HEADS * 2 * A_QK_DIM
A_K = A_HEADS * 2 * A_QK_DIM
A_V = A_HEADS * A_V_DIM
A_IN = A_Q + A_K + A_V
B_Q = B_HEADS * HEAD_DIM
B_K = B_KV_HEADS * HEAD_DIM
B_V = B_KV_HEADS * HEAD_DIM
B_IN = B_Q + B_K + B_V
C_Q = C_HEADS * HEAD_DIM
C_K = C_KV_HEADS * HEAD_DIM
C_V = C_KV_HEADS * HEAD_DIM
C_IN = C_Q + C_K + C_V
D_IN_2 = D_Q_RANK + D_KV_RANK + D_ROPE
MIX_WIDTH_2 = A_HEADS * A_V_DIM + B_HEADS * HEAD_DIM
EVEN_IN = A_IN + B_IN + MIX_WIDTH_2
ODD_IN = C_IN + D_IN_2 + MIX_WIDTH_2
N_EVEN = (DEPTH_2 + 1) // 2
N_ODD = DEPTH_2 // 2


def rmsnorm(x, g):
    xf = x.astype(jnp.float32)
    y = xf * lax.rsqrt(jnp.mean(xf * xf, axis=-1, keepdims=True) + EPS)
    return (y * g.astype(jnp.float32)).astype(x.dtype)

def axial_angles(n_tok, dim):
    rows = n_tok // GRID_W
    row = jnp.repeat(jnp.arange(rows), GRID_W).astype(jnp.float32)
    col = jnp.tile(jnp.arange(GRID_W), rows).astype(jnp.float32)
    n_freq = dim // 4
    inv = ROPE_BASE ** (-jnp.arange(n_freq, dtype=jnp.float32) / n_freq)
    ang = jnp.concatenate([row[:, None] * inv[None], col[:, None] * inv[None]], axis=-1)
    return jnp.cos(ang), jnp.sin(ang)

def apply_rope(x, cs):
    cos, sin = cs
    shape = (1, cos.shape[0]) + (1,) * (x.ndim - 3) + (cos.shape[1],)
    cos = cos.reshape(shape).astype(x.dtype)
    sin = sin.reshape(shape).astype(x.dtype)
    x1, x2 = jnp.split(x, 2, axis=-1)
    return jnp.concatenate([x1 * cos - x2 * sin, x1 * sin + x2 * cos], axis=-1)

def softmax_with_sink(s, sink):
    full = jnp.concatenate([s, jnp.broadcast_to(sink, s.shape[:-1] + (1,)).astype(jnp.float32)], axis=-1)
    return jax.nn.softmax(full, axis=-1)[..., :-1]

def attend(q, k, v, scale):
    b, lq, hq, dk = q.shape
    hk = k.shape[2]
    qg = q.reshape(b, lq, hk, hq // hk, dk)
    s = jnp.einsum('bqhgd,bkhd->bhgqk', qg, k).astype(jnp.float32) * scale
    p = jax.nn.softmax(s, axis=-1).astype(v.dtype)
    o = jnp.einsum('bhgqk,bkhd->bqhgd', p, v)
    return o.reshape(b, lq, hq, v.shape[-1])

def diff_attend(q1, q2, k1, k2, v, lam, scale):
    p1 = jax.nn.softmax(jnp.einsum('bqhd,bkhd->bhqk', q1, k1).astype(jnp.float32) * scale, axis=-1)
    p2 = jax.nn.softmax(jnp.einsum('bqhd,bkhd->bhqk', q2, k2).astype(jnp.float32) * scale, axis=-1)
    p = (p1 - lam * p2).astype(v.dtype)
    return jnp.einsum('bhqk,bkhd->bqhd', p, v)

def over_query_blocks(fn, *qs):
    b, s = qs[0].shape[:2]
    nb = s // Q_BLOCK
    blocks = tuple(jnp.moveaxis(q.reshape((b, nb, Q_BLOCK) + q.shape[2:]), 1, 0) for q in qs)
    out = lax.map(lambda args: fn(*args), blocks)
    return jnp.moveaxis(out, 0, 1).reshape((b, s) + out.shape[3:])

def band_mask(nb, s):
    qpos = jnp.arange(nb)[:, None, None] * Q_BLOCK + jnp.arange(Q_BLOCK)[None, :, None]
    kpos = jnp.arange(nb)[:, None, None] * Q_BLOCK - PAD + jnp.arange(BAND)[None, None, :]
    return (jnp.abs(kpos - qpos) <= WINDOW) & (kpos >= 0) & (kpos < s)

def mixer_a(u_lat, u_ctx, cs64, lam, lam_init, sub_g, with_ctx):
    def heads(u):
        b, l = u.shape[:2]
        q, k, v = jnp.split(u, [A_Q, A_Q + A_K], axis=-1)
        q = q.reshape(b, l, A_HEADS, 2 * A_QK_DIM)
        k = k.reshape(b, l, A_HEADS, 2 * A_QK_DIM)
        v = v.reshape(b, l, A_HEADS, A_V_DIM)
        return q[..., :A_QK_DIM], q[..., A_QK_DIM:], k[..., :A_QK_DIM], k[..., A_QK_DIM:], v

    q1, q2, k1, k2, v = heads(u_lat)
    q1, q2, k1, k2 = (apply_rope(t, cs64) for t in (q1, q2, k1, k2))
    cq1, cq2, ck1, ck2, cv = heads(u_ctx)
    k1a = jnp.concatenate([ck1, k1], axis=1)
    k2a = jnp.concatenate([ck2, k2], axis=1)
    va = jnp.concatenate([cv, v], axis=1)
    scale = A_QK_DIM ** -0.5

    def post(o):
        b, l = o.shape[:2]
        return (rmsnorm(o, sub_g) * (1.0 - lam_init)).reshape(b, l, A_HEADS * A_V_DIM)

    o = over_query_blocks(lambda a1, a2: diff_attend(a1, a2, k1a, k2a, va, lam, scale), q1, q2)
    y = post(o)
    yc = post(diff_attend(cq1, cq2, ck1, ck2, cv, lam, scale)) if with_ctx else None
    return y, yc

def mixer_b(u_lat, u_ctx, cs128, sink, with_ctx):
    g = B_HEADS // B_KV_HEADS

    def heads(u):
        b, l = u.shape[:2]
        q, k, v = jnp.split(u, [B_Q, B_Q + B_K], axis=-1)
        return (q.reshape(b, l, B_KV_HEADS, g, HEAD_DIM),
                k.reshape(b, l, B_KV_HEADS, HEAD_DIM),
                v.reshape(b, l, B_KV_HEADS, HEAD_DIM))

    q, k, v = heads(u_lat)
    q, k = apply_rope(q, cs128), apply_rope(k, cs128)
    cq, ck, cv = heads(u_ctx)
    b, s = q.shape[:2]
    lc = ck.shape[1]
    nb = s // Q_BLOCK
    scale = HEAD_DIM ** -0.5
    sink_hg = sink.reshape(B_KV_HEADS, g)

    def band(t):
        tp = jnp.pad(t, ((0, 0), (PAD, PAD), (0, 0), (0, 0)))
        tp = tp.reshape((b, nb + 2 * NBAND, Q_BLOCK) + t.shape[2:])
        return jnp.concatenate([tp[:, i:i + nb] for i in range(2 * NBAND + 1)], axis=2)

    qb = q.reshape(b, nb, Q_BLOCK, B_KV_HEADS, g, HEAD_DIM)
    kb, vb = band(k), band(v)
    s_win = jnp.einsum('bnqhgd,bnkhd->bnhgqk', qb, kb).astype(jnp.float32) * scale
    s_win = jnp.where(band_mask(nb, s)[None, :, None, None], s_win, NEG_INF_2)
    s_ctx = jnp.einsum('bnqhgd,bkhd->bnhgqk', qb, ck).astype(jnp.float32) * scale
    p = softmax_with_sink(jnp.concatenate([s_ctx, s_win], axis=-1),
                          sink_hg[None, None, :, :, None, None]).astype(v.dtype)
    o = (jnp.einsum('bnhgqk,bkhd->bnqhgd', p[..., :lc], cv)
         + jnp.einsum('bnhgqk,bnkhd->bnqhgd', p[..., lc:], vb))
    y = o.reshape(b, s, B_HEADS * HEAD_DIM)
    yc = None
    if with_ctx:
        sc = jnp.einsum('bqhgd,bkhd->bhgqk', cq, ck).astype(jnp.float32) * scale
        pc = softmax_with_sink(sc, sink_hg[None, :, :, None, None]).astype(cv.dtype)
        yc = jnp.einsum('bhgqk,bkhd->bqhgd', pc, cv).reshape(b, lc, B_HEADS * HEAD_DIM)
    return y, yc

def mixer_c(u_lat, u_ctx, cs128, q_g, k_g, with_ctx):
    def heads(u):
        b, l = u.shape[:2]
        q, k, v = jnp.split(u, [C_Q, C_Q + C_K], axis=-1)
        q = rmsnorm(q.reshape(b, l, C_HEADS, HEAD_DIM), q_g)
        k = rmsnorm(k.reshape(b, l, C_KV_HEADS, HEAD_DIM), k_g)
        return q, k, v.reshape(b, l, C_KV_HEADS, HEAD_DIM)

    q, k, v = heads(u_lat)
    q, k = apply_rope(q, cs128), apply_rope(k, cs128)
    cq, ck, cv = heads(u_ctx)
    ka = jnp.concatenate([ck, k], axis=1)
    va = jnp.concatenate([cv, v], axis=1)
    scale = HEAD_DIM ** -0.5
    b, s = q.shape[:2]
    y = over_query_blocks(lambda qb: attend(qb, ka, va, scale), q).reshape(b, s, C_HEADS * HEAD_DIM)
    yc = attend(cq, ck, cv, scale).reshape(b, ck.shape[1], C_HEADS * HEAD_DIM) if with_ctx else None
    return y, yc

def mixer_d(u_lat, u_ctx, cs64, q_a_g, kv_a_g, w_q_b, w_kv_b, with_ctx):
    def heads(u, rope):
        b, l = u.shape[:2]
        cq, ckv, kpe = jnp.split(u, [D_Q_RANK, D_Q_RANK + D_KV_RANK], axis=-1)
        q = (rmsnorm(cq, q_a_g) @ w_q_b).reshape(b, l, D_HEADS, D_NOPE + D_ROPE)
        kv = (rmsnorm(ckv, kv_a_g) @ w_kv_b).reshape(b, l, D_HEADS, D_NOPE + D_V)
        q_nope, q_pe = q[..., :D_NOPE], q[..., D_NOPE:]
        k_nope, v = kv[..., :D_NOPE], kv[..., D_NOPE:]
        kpe = kpe.reshape(b, l, 1, D_ROPE)
        if rope:
            q_pe, kpe = apply_rope(q_pe, cs64), apply_rope(kpe, cs64)
        q = jnp.concatenate([q_nope, q_pe], axis=-1)
        k = jnp.concatenate([k_nope, jnp.broadcast_to(kpe, (b, l, D_HEADS, D_ROPE))], axis=-1)
        return q, k, v

    q, k, v = heads(u_lat, True)
    cq, ck, cv = heads(u_ctx, False)
    ka = jnp.concatenate([ck, k], axis=1)
    va = jnp.concatenate([cv, v], axis=1)
    scale = (D_NOPE + D_ROPE) ** -0.5
    b, s = q.shape[:2]
    y = over_query_blocks(lambda qb: attend(qb, ka, va, scale), q).reshape(b, s, D_HEADS * D_V)
    yc = attend(cq, ck, cv, scale).reshape(b, ck.shape[1], D_HEADS * D_V) if with_ctx else None
    return y, yc

def second_inputs(seed: int = 0) -> dict:
    key = jax.random.key(seed)
    ks = jax.random.split(key, 23)
    n = lambda k, shape, s: jax.random.normal(k, shape, jnp.float32) * s
    gain = lambda k, shape: 1.0 + 0.02 * jax.random.normal(k, shape, jnp.float32)
    return {
        "x": n(ks[0], (BATCH, SEQ, D_MODEL), 1.0),
        "c": n(ks[1], (BATCH, D_MODEL), 1.0),
        "ctx": n(ks[2], (BATCH, CTX_LEN, D_MODEL), 1.0),
        "c_ctx": n(ks[3], (D_MODEL,), 1.0),
        "w_mod": n(ks[4], (DEPTH_2, D_MODEL, 3 * D_MODEL), 0.5 * D_MODEL ** -0.5),
        "b_mod": n(ks[5], (DEPTH_2, 3 * D_MODEL), 0.01),
        "norm_g": gain(ks[6], (DEPTH_2, D_MODEL)),
        "w_o": n(ks[7], (DEPTH_2, MIX_WIDTH_2, D_MODEL), MIX_WIDTH_2 ** -0.5),
        "final_g": gain(ks[8], (D_MODEL,)),
        "e_w_in": n(ks[9], (N_EVEN, D_MODEL, EVEN_IN), D_MODEL ** -0.5),
        "a_lam_q1": n(ks[10], (N_EVEN, A_QK_DIM), 0.1),
        "a_lam_k1": n(ks[11], (N_EVEN, A_QK_DIM), 0.1),
        "a_lam_q2": n(ks[12], (N_EVEN, A_QK_DIM), 0.1),
        "a_lam_k2": n(ks[13], (N_EVEN, A_QK_DIM), 0.1),
        "a_sub_g": gain(ks[14], (N_EVEN, A_V_DIM)),
        "b_sink": n(ks[15], (N_EVEN, B_HEADS), 1.0),
        "o_w_in": n(ks[16], (N_ODD, D_MODEL, ODD_IN), D_MODEL ** -0.5),
        "c_q_g": gain(ks[17], (N_ODD, HEAD_DIM)),
        "c_k_g": gain(ks[18], (N_ODD, HEAD_DIM)),
        "d_q_a_g": gain(ks[19], (N_ODD, D_Q_RANK)),
        "d_kv_a_g": gain(ks[20], (N_ODD, D_KV_RANK)),
        "d_w_q_b": n(ks[21], (N_ODD, D_Q_RANK, D_HEADS * (D_NOPE + D_ROPE)), D_Q_RANK ** -0.5),
        "d_w_kv_b": n(ks[22], (N_ODD, D_KV_RANK, D_HEADS * (D_NOPE + D_V)), D_KV_RANK ** -0.5),
    }

def second_block(x, c, ctx, c_ctx, w_mod, b_mod, norm_g, w_o, final_g,
              e_w_in, a_lam_q1, a_lam_k1, a_lam_q2, a_lam_k2, a_sub_g, b_sink,
              o_w_in, c_q_g, c_k_g, d_q_a_g, d_kv_a_g, d_w_q_b, d_w_kv_b):
    s = x.shape[1]
    cs128 = axial_angles(s, HEAD_DIM)
    cs64 = axial_angles(s, A_QK_DIM)
    silu_c = jax.nn.silu(c)
    silu_cc = jax.nn.silu(c_ctx)
    cx = ctx
    for l in range(DEPTH_2):
        with_ctx = l < DEPTH_2 - 1
        i = l // 2
        mod = silu_c @ w_mod[l] + b_mod[l]
        shift, scale, gate = jnp.split(mod[:, None, :], 3, axis=-1)
        cmod = silu_cc @ w_mod[l] + b_mod[l]
        cshift, cscale, cgate = jnp.split(cmod, 3)
        h = rmsnorm(x, norm_g[l]) * (1.0 + scale) + shift
        hc = rmsnorm(cx, norm_g[l]) * (1.0 + cscale) + cshift
        if l % 2 == 0:
            u = h @ e_w_in[i]
            uc = hc @ e_w_in[i]
            ua, ub, ug = jnp.split(u, [A_IN, A_IN + B_IN], axis=-1)
            uca, ucb, ucg = jnp.split(uc, [A_IN, A_IN + B_IN], axis=-1)
            lam_init = 0.8 - 0.6 * math.exp(-0.3 * l)
            lam = (jnp.exp(jnp.sum(a_lam_q1[i].astype(jnp.float32) * a_lam_k1[i].astype(jnp.float32)))
                   - jnp.exp(jnp.sum(a_lam_q2[i].astype(jnp.float32) * a_lam_k2[i].astype(jnp.float32)))
                   + lam_init)
            y1, yc1 = mixer_a(ua, uca, cs64, lam, lam_init, a_sub_g[i], with_ctx)
            y2, yc2 = mixer_b(ub, ucb, cs128, b_sink[i], with_ctx)
        else:
            u = h @ o_w_in[i]
            uc = hc @ o_w_in[i]
            ucc_, ud, ug = jnp.split(u, [C_IN, C_IN + D_IN_2], axis=-1)
            ucc2, ucd, ucg = jnp.split(uc, [C_IN, C_IN + D_IN_2], axis=-1)
            y1, yc1 = mixer_c(ucc_, ucc2, cs128, c_q_g[i], c_k_g[i], with_ctx)
            y2, yc2 = mixer_d(ud, ucd, cs64, d_q_a_g[i], d_kv_a_g[i], d_w_q_b[i], d_w_kv_b[i], with_ctx)
        y = jnp.concatenate([y1, y2], axis=-1) * jax.nn.silu(ug)
        x = x + gate * (y @ w_o[l])
        if with_ctx:
            yc = jnp.concatenate([yc1, yc2], axis=-1) * jax.nn.silu(ucg)
            cx = cx + cgate * (yc @ w_o[l])
    return rmsnorm(x, final_g)


def setup_inputs(seed=0):
    out = dict(first_inputs(seed))
    for name, value in second_inputs(seed + 1).items():
        if name != "x":
            out[name + "_2"] = value
    return out


def reference(
    x, w_in, cmp_pos, cmp_w1, cmp_w2, swa_sinks, w_branch, w_out, w_mlp_in, w_mlp_out, norm_mix,
    norm_mlp, norm_final, rel_bias, c_2, ctx_2, c_ctx_2, w_mod_2, b_mod_2, norm_g_2, w_o_2,
    final_g_2, e_w_in_2, a_lam_q1_2, a_lam_k1_2, a_lam_q2_2, a_lam_k2_2, a_sub_g_2, b_sink_2,
    o_w_in_2, c_q_g_2, c_k_g_2, d_q_a_g_2, d_kv_a_g_2, d_w_q_b_2, d_w_kv_b_2,
):
    x = first_block(
        x, w_in, cmp_pos, cmp_w1, cmp_w2, swa_sinks, w_branch, w_out, w_mlp_in, w_mlp_out,
        norm_mix, norm_mlp, norm_final, rel_bias,
    )
    return second_block(
        x, c_2, ctx_2, c_ctx_2, w_mod_2, b_mod_2, norm_g_2, w_o_2, final_g_2, e_w_in_2,
        a_lam_q1_2, a_lam_k1_2, a_lam_q2_2, a_lam_k2_2, a_sub_g_2, b_sink_2, o_w_in_2, c_q_g_2,
        c_k_g_2, d_q_a_g_2, d_kv_a_g_2, d_w_q_b_2, d_w_kv_b_2,
    )


_drawn_inputs = setup_inputs


def setup_inputs(seed=0):
    import zlib

    import numpy as np

    out = dict(_drawn_inputs(seed))
    spreads = {}
    factors = {'cmp_pos': 5.284,
     'swa_sinks': 8.0,
     'norm_mix': 8.0,
     'norm_mlp': 3.857,
     'norm_final': 2.892,
     'b_mod_2': 8.0,
     'norm_g_2': 8.0,
     'final_g_2': 2.741,
     'a_lam_q1_2': 8.0,
     'a_lam_k1_2': 8.0,
     'a_lam_q2_2': 7.866,
     'a_lam_k2_2': 5.105,
     'a_sub_g_2': 8.0,
     'b_sink_2': 8.0,
     'c_q_g_2': 8.0,
     'c_k_g_2': 8.0,
     'd_q_a_g_2': 8.0,
     'd_kv_a_g_2': 8.0,
     'd_w_q_b_2': 4.755}
    for name, (base, spread) in spreads.items():
        noise = np.random.default_rng([zlib.crc32(name.encode()), seed]).standard_normal(out[name].shape)
        drawn = base * np.exp(spread * noise) if base else spread * noise
        out[name] = jnp.asarray(drawn.astype(out[name].dtype))
    for name, factor in factors.items():
        out[name] = (out[name] * factor).astype(out[name].dtype)
    return out
```

```python
from contextlib import ExitStack

import numpy as np

import concourse.bass as bass
from concourse import mybir

F32 = mybir.dt.float32
F32R = mybir.dt.float32r
ACT = mybir.ActivationFunctionType
ALU = mybir.AluOpType
AX = mybir.AxisListType

P = 128
DM = 2048
KT = DM // P
SEQ = 256
CTX = 256
HD = 128
G = 512
CH = 2048
QKV1 = 5656
GATE0 = 2560
NCMP = (SEQ - 32) // 16 + 1
NM = 3 * DM // P
BANK = [0, 1, 2, 3, 0]
RAWS, SPLITS = 4, 2
NEG = -1e30
EPS = 1e-6
TINY = 1e-30
GELU_C = float(np.sqrt(2.0 / np.pi))
SCALE = HD ** -0.5
BUCKETS = 32
LAM_INIT = 0.2


class Step:

    def __init__(self, chunks, tiles, lhs, evac, width=G, wtiles=4):
        self.chunks, self.tiles, self.lhs, self.evac = chunks, tiles, lhs, evac
        self.width, self.wtiles = width, wtiles


class Stage:

    def __init__(self, steps, times=1):
        self.steps, self.times = steps, times


def count_stages(stages):
    total = {("fill", 4): 1, ("put", 4): 1, "relu2": 1}
    for st in stages:
        st.base = dict(total)
        local = {}
        for s in st.steps:
            s.chunk0 = local.get("chunk", 0)
            local["chunk"] = s.chunk0 + len(s.chunks)
            s.fill, s.put = {}, {}
            s.done = {}
            for bank, _ in s.tiles[:-1]:
                s.done[bank] = local.get(("done", bank), 0)
                local[("done", bank)] = s.done[bank] + 1
            for bank, _ in s.tiles:
                s.fill[bank] = local.get(("fill", bank), 0)
                local[("fill", bank)] = s.fill[bank] + 1
                if s.evac["kind"] == "store":
                    s.put[bank] = local.get(("put", bank), 0)
                    local[("put", bank)] = s.put[bank] + 1
            for kind in ("relu2", "branch"):
                if s.evac["kind"] == kind:
                    s.nth = local.get(kind, 0)
                    local[kind] = s.nth + 1
        st.per = local
        assert st.times == 1 or local["chunk"] % RAWS == 0
        for k, v in local.items():
            total[k] = total.get(k, 0) + v * st.times
    return total


def at(st, kind, local, it):
    return st.base.get(kind, 0) + local + (st.per.get(kind, 0) * it if st.times > 1 else 0)


class Unit:

    def __init__(self, q, k, v, keys, out, bias=None, sink=None, coeff=None, add=False):
        self.q, self.k, self.v, self.keys, self.out = q, k, v, keys, out
        self.bias, self.sink, self.coeff, self.add = bias, sink, coeff, add


def two_blocks(nc, A, C, out):
    ctx = ExitStack()
    with ctx:
        here = [nc.sbuf_base + (-nc.sbuf_base) % 64]
        fence = ctx.enter_context(nc.sbuf_tensor("fence", [P, (nc.sbuf_bytes_remaining - 256) // 4], F32))

        def place(name, shape, offset, dt=F32):
            return nc.alloc_sbuf_tensor_at(name, shape, dt, offset=offset)

        def take(n):
            o = here[0]
            here[0] += n + (-n) % 32
            assert here[0] <= nc.sbuf_usable_end, here
            return o

        def sb(name, shape, dt=F32):
            return place(name, shape, take(4 * int(np.prod(shape[1:]))), dt)

        def sem(name):
            return ctx.enter_context(nc.semaphore(name))

        def dram(name, shape):
            return nc.dram_tensor(name, shape, F32, kind="Internal").ap()

        raw = sb("raw", [P, RAWS, CH])
        w_hi = sb("w_hi", [P, SPLITS, CH], F32R)
        w_lo = sb("w_lo", [P, SPLITS, CH], F32R)
        act_hi_at, act_lo_at = take(32768), take(32768)
        a_hi = place("a_hi", [P, 8192], act_hi_at, F32R)
        a_lo = place("a_lo", [P, 8192], act_lo_at, F32R)
        XR = sb("XR", [P, 2, DM])
        CX = sb("CX", [P, 2, DM])
        MIX = CX
        stage = sb("stage", [P, 4, G])
        ident = sb("ident", [P, P])
        small = sb("small", [P, 64])
        half = sb("half", [P, 2])
        scr_at = take(0)
        

        class Arena:

            def __init__(self, regions):
                self.regions = [list(r) for r in regions]

            def __call__(self, name, shape, dt=F32):
                n = 4 * int(np.prod(shape[1:]))
                n += (-n) % 32
                for r in self.regions:
                    if r[0] + n <= r[1]:
                        r[0] += n
                        return place(name, shape, r[0] - n, dt)
                raise AssertionError((name, n, self.regions))

        AHI, ALO = (act_hi_at, act_hi_at + 32768), (act_lo_at, act_lo_at + 32768)

        acc = ctx.enter_context(nc.psum_tensor("acc", [P, 8, G], F32))

        U1 = dram("U1", (SEQ, QKV1))
        AG = dram("AG", (SEQ, 24))
        GT = dram("GT", (SEQ, 3 * DM))
        OB = dram("OB", (SEQ, 3 * 1024))
        MODP = dram("MODP", (4, 2 * 3 * DM))
        BREV = dram("BREV", (24, G))
        BROW = dram("BROW", (24, P, G))
        CMPK = dram("CMPK", (HD, 2 * NCMP))
        CMPV = dram("CMPV", (2 * NCMP, HD))
        MODF = dram("MODF", (2, 2 * 3 * DM))
        U2 = dram("U2", (CTX + SEQ, 6656))
        O2 = dram("O2", (CTX + SEQ, DM))
        U3 = dram("U3", (CTX + SEQ, 4416))
        QB = dram("QB", (CTX + SEQ, 1536))
        KVB = dram("KVB", (CTX + SEQ, DM))
        O3 = dram("O3", (CTX + SEQ, DM))

        def tok(ap, tt):
            return ap[tt * P:(tt + 1) * P, :]

        def lhs_act(T, off=0):
            def f(part, kt, tt):
                o = off + kt * T + tt * P
                return (a_hi, a_lo)[part][:, o:o + P]
            return f

        MV = sb("MV", [P, KT * 4 + P], F32R)

        def lhs_mod(part, kt, tt):
            return MV[:, kt * 4:kt * 4 + P]

        def wcols(W, k0, n0, width=G, nk=4):
            def f(it):
                c = n0(it) if callable(n0) else n0
                kk = k0(it) if callable(k0) else k0
                return W.rearrange("(k p) n -> p k n", p=P)[:, bass.ds(kk, nk), bass.ds(c, width)]
            return f

        def group(W, n0, tiles, lhs, evac, kts=KT, k0=0, width=G):
            ch = [wcols(W, (lambda it, j=j: (k0(it) if callable(k0) else k0) + j), n0, width)
                  for j in range(0, kts, 4)]
            return Step(ch, tiles, lhs, evac, width)

        def store(dst, func=ACT.Copy, scale=1.0, rows=P):
            return dict(kind="store", dst=dst, func=func, scale=scale, rows=rows)

        T2 = [(0, 0), (1, 1)]
        T4 = [(0, 0), (1, 1), (2, 2), (3, 3)]
        TX = [(2, 2), (3, 3)]

        def to(D, n0, t0=0):
            return lambda it, tt, w: D[tt * P:(tt + 1) * P, bass.ds(n0(it) if callable(n0) else n0, w)]

        x256, x512 = lhs_act(256), lhs_act(512)
        win = A["w_in"][0]
        stages = {}
        GQ = -(-QKV1 // (12 * 8)) * 8
        gg = GATE0 // GQ
        assert gg == 5 and GATE0 + 24 <= (gg + 1) * GQ and QKV1 > 11 * GQ
        stages["qkv0"] = Stage([group(win, gg * GQ, T2, x256, dict(store(to(U1, gg * GQ)), gates=GATE0 - gg * GQ),
                                      width=GQ),
                                group(win, 11 * GQ, T2, x256, store(to(U1, 11 * GQ)), width=QKV1 - 11 * GQ)])
        stages["qkv"] = Stage([group(win, lambda it, j=j: (it * 6 + j) * GQ, T2, x256,
                                     store(to(U1, lambda it, j=j: (it * 6 + j) * GQ)), width=GQ)
                               for j in range(5)], 2)
        stages["gates"] = Stage([group(win, lambda it, j=j: QKV1 + (it * 4 + j) * G, T2, x256,
                                       store(to(GT, lambda it, j=j: (it * 4 + j) * G), ACT.Tanh, 0.5))
                                 for j in range(4)], 3)
        def lhs_cmp(which):
            def f(part, kt, tt):
                o = which * 1024 + kt * 30
                return (a_hi, a_lo)[part][:, 4096 + o:4096 + o + P]
            return f

        def w1chunk(which, c):
            return lambda it: A["cmp_w1"][0, which].rearrange("(k p) n -> p k n", p=P)[:, c * 8:c * 8 + 8, :]

        stages["cmp1"] = Stage([Step([w1chunk(w, c) for c in range(4)], [(w, 0)], lhs_cmp(w),
                                     dict(kind="hold"), 256, 8) for w in range(2)])

        def branch_steps():
            steps = []
            for n in range(4):
                for m in range(3):
                    steps.append(group(A["w_branch"][0, m], n * G, T2, (lambda part, kt, tt, m=m:
                                 x256(part, m * 8 + kt, tt)), dict(kind="branch", n=n, m=m), kts=8))
            return steps
        stages["branch"] = Stage(branch_steps())
        stages["out1"] = Stage([group(A["w_out"][0], n * G, T2, x256,
                                      dict(kind="resid", n=n, scale=0.5)) for n in range(4)])

        h256 = lhs_act(256, 4096)

        def mod_steps(layer, n, first=0):
            def col(r):
                return lambda it: (first + it * n + r) * G
            return [group(A["w_mod_2"][layer], col(r), [(4, 0)], lhs_mod,
                          store(lambda it, tt, w, r=r: MODP[:, bass.ds(layer * 3 * DM + col(r)(it), w)], rows=4))
                    for r in range(n)]
        stages["mod1"] = Stage(mod_steps(0, 6), 2)
        stages["modA"] = Stage(mod_steps(1, 2), 4)
        stages["modB"] = Stage(mod_steps(1, 2, 8), 2)

        def mlp_steps():
            ins = [group(A["w_mlp_in"][0], lambda it, j=j: it * DM + j * G, T2, x256,
                         dict(kind="relu2", j=j)) for j in range(4)]
            outs = [group(A["w_mlp_out"][0], n * G, T2, h256, dict(kind="resid", n=n, scale=1.0),
                          k0=lambda it: it * KT) for n in range(4)]
            return ins + outs
        stages["mlp"] = Stage(mlp_steps(), 4)
        ew = A["e_w_in_2"][0]
        stages["in2"] = Stage([group(ew, lambda it, j=j: (it * 4 + j) * G, T4, x512,
                                     store(to(U2, lambda it, j=j: (it * 4 + j) * G))) for j in range(4)], 3)
        stages["in2_end"] = Stage([group(ew, 12 * G, T4, x512, store(to(U2, 12 * G)))])
        stages["out2"] = Stage([group(A["w_o_2"][0], n * G, T4, x512, dict(kind="gresid", n=n))
                                for n in range(4)])
        ow = A["o_w_in_2"][0]
        cols3 = [(0, TX, G), (G, TX, G), (2 * G, T4, G), (3 * G, TX, G), (4 * G, T4, 320)] + \
                [(2368 + j * G, TX, G) for j in range(4)]
        stages["in3"] = Stage([group(ow, c, tl, x512, store(to(U3, c)), width=w) for c, tl, w in cols3])
        q4 = lhs_act(512)
        kv2 = lhs_act(512, 2048)
        stages["qb"] = Stage([group(A["d_w_q_b_2"][0], n * G, TX, q4, store(to(QB, n * G)), kts=4)
                              for n in range(3)])
        stages["kvb"] = Stage([Step([wcols(A["d_w_kv_b_2"][0], 0, n * G, G, 2)], T4, kv2,
                                    store(to(KVB, n * G)), G, 2) for n in range(4)])
        stages["out3"] = Stage([group(A["w_o_2"][1], n * G, TX, x512, dict(kind="gresid", n=n))
                                for n in range(4)])
        order = ["qkv0", "qkv", "gates", "cmp1", "mod1", "branch", "out1", "mlp", "in2", "in2_end", "modA", "modB",
                 "out2", "in3", "qb", "kvb", "out3"]
        for name in order:
            stages[name].name = name
        totals = count_stages([stages[n] for n in order])

        held = sem("held")
        setup_gp = sem("setup_gp")
        landed = [sem(f"landed{i}") for i in range(RAWS)]
        hi_ready, lo_ready = sem("hi_ready"), sem("lo_ready")
        w_used = sem("w_used")
        acc_done = [sem(f"acc_done{b}") for b in range(3)]
        acc_free = [sem(f"acc_free{b}") for b in range(5)]
        stored = [sem(f"stored{b}") for b in range(5)]
        mod_put = sem("mod_put")
        stage_bufs = [stage[:, b, :] for b in range(4)] + [sb("stage_mod", [4, G])[:, :]]
        nsa_g = sb("nsa_g", [P, 2, 24])
        nsa_ready, nsa_out = sem("nsa_ready"), sem("nsa_out")
        mfr, mfb, mfo = sb("mfr", [P, 4, NM]), sb("mfb", [P, NM]), sb("mfo", [P, 2, NM])
        vec = sb("vec", [P, 8, KT])
        subg = sb("subg", [P, HD])
        scr_at = here[0]
        SCR = (scr_at, nc.sbuf_usable_end - 64)
        relu_done, sq_done, ht_done, hh_done, hl_done = (sem("relu_done"), sem("sq_done"), sem("ht_done"),
                                                         sem("hh_done"), sem("hl_done"))
        gate_in = [sem(f"gate_in{i}") for i in range(2)]
        gate_used = sem("gate_used")
        branch_tmp, gres_tmp = sem("branch_tmp"), sem("gres_tmp")

        ar = Arena([SCR])
        relu_t = ar("relu_t", [P, 2, G])
        gate_t = ar("gate_t", [P, 2, 2, G])
        prod_t = ar("prod_t", [P, 2, G])
        gbc_x, gbc_c = place("gbc_x", [P, DM], SCR[0] + 16384), place("gbc_c", [P, DM], SCR[0] + 24576)
        prod_g = place("prod_g", [P, 4, G], SCR[0])

        def wait_done(eng, st, s, bank, it):
            if bank in s.done:
                eng.wait_ge(acc_done[bank], at(st, ("done", bank), s.done[bank] + 1, it))
            else:
                eng.wait_ge(w_used, at(st, "chunk", s.chunk0 + len(s.chunks), it))

        def hold(eng, s, value):
            eng.wait_ge(s, value)
            if not isinstance(value, int):
                eng.sem_inc(held, 1)

        def passes(eng, st, body):
            if st.times > 1:
                with eng.Fori(0, st.times) as it:
                    body(it)
            else:
                body(0)

        def chunk_no(st, s, c, it):
            n = at(st, "chunk", s.chunk0 + c, 0)
            return n, (st.per["chunk"] * it if st.times > 1 else 0)

        def sp_chunks(sp, st, s, it):
            for c, src in enumerate(s.chunks):
                n, more = chunk_no(st, s, c, it)
                if n >= RAWS:
                    sp.wait_ge(lo_ready, n - RAWS + 1 + more)
                dst = raw[:, n % RAWS, 0:s.wtiles * s.width].rearrange("p (k n) -> p k n", k=s.wtiles)
                sp.dma_start(dst, src(it)).then_inc(landed[n % RAWS], 16)

        def sp_stream(sp, st):
            passes(sp, st, lambda it: [sp_chunks(sp, st, s, it) for s in st.steps])

        def split_hi(act, st, s, c, it):
            n, more = chunk_no(st, s, c, it)
            size = s.wtiles * s.width
            act.wait_ge(landed[n % RAWS], 16 * (n // RAWS + 1) + (16 * (st.per["chunk"] // RAWS) * it
                                                                  if st.times > 1 else 0))
            if n >= SPLITS:
                act.wait_ge(w_used, n - SPLITS + 1 + more)
            nc.scalar.activation(w_hi[:, n % SPLITS, 0:size], raw[:, n % RAWS, 0:size], ACT.Copy)\
              .then_inc(hi_ready, 1)

        def split_lo(dve, st, s, c, it):
            n, more = chunk_no(st, s, c, it)
            size = s.wtiles * s.width
            dve.wait_ge(hi_ready, n + 1 + more)
            nc.vector.tensor_tensor(w_lo[:, n % SPLITS, 0:size], raw[:, n % RAWS, 0:size],
                                    w_hi[:, n % SPLITS, 0:size].bitcast(F32), ALU.subtract)\
              .then_inc(lo_ready, 1)

        def pe_chunk(pe, st, s, c, it):
            n, more = chunk_no(st, s, c, it)
            pe.wait_ge(lo_ready, n + 1 + more)
            for bank, tt in s.tiles:
                if c == 0:
                    f = at(st, ("fill", bank), s.fill[bank], it)
                    if not (isinstance(f, int) and f == 0):
                        pe.wait_ge(acc_free[bank], f)
                o = acc[:, BANK[bank], 0:s.width]
                for k in range(s.wtiles):
                    kt = c * s.wtiles + k
                    wh = w_hi[:, n % SPLITS, k * s.width:(k + 1) * s.width]
                    wl = w_lo[:, n % SPLITS, k * s.width:(k + 1) * s.width]
                    first = kt == 0
                    end = kt == len(s.chunks) * s.wtiles - 1
                    nc.tensor.matmul(o, s.lhs(0, kt, tt), wh, start=first, stop=False)
                    if s.lhs is lhs_mod:
                        last = nc.tensor.matmul(o, s.lhs(0, kt, tt), wl, start=False, stop=end)
                    else:
                        nc.tensor.matmul(o, s.lhs(0, kt, tt), wl, start=False, stop=False)
                        last = nc.tensor.matmul(o, s.lhs(1, kt, tt), wh, start=False, stop=end)
                if end and bank in s.done:
                    last.then_inc(acc_done[bank], 1)
            last.then_inc(w_used, 1)

        def pe_stream(pe, st):
            def body(it):
                prev = None
                for s in st.steps:
                    for c in range(len(s.chunks)):
                        if st.name == "mlp" and s.evac["kind"] == "resid" and s.evac["n"] == 0 and c in (0, 3):
                            pe.wait_ge(hl_done, at(st, "relu2", 3 if c == 0 else 4, it))
                        pe_chunk(pe, st, s, c, it)
                        if c == 1 and prev is not None and prev.evac["kind"] == "relu2":
                            pe_hidden(pe, st, prev, it)
                    prev = s
            passes(pe, st, body)

        def pe_hidden(pe, st, s, it):
            r = at(st, "relu2", s.nth, it)
            pe.wait_ge(sq_done, r + 1)
            if not (isinstance(r, int) and r == 0):
                pe.wait_ge(hl_done, r)
            for tt in range(2):
                for j in range(4):
                    last = nc.tensor.transpose(acc[:, 6 + tt, j * P:(j + 1) * P],
                                               relu_t[:, tt, j * P:(j + 1) * P], ident[:, :])
            last.then_inc(ht_done, 1)

        def hid(t, s, tt):
            o = 4096 + s.evac["j"] * 4 * 256
            return t[:, o:o + 1024].rearrange("p (j t) -> p j t", j=4)[:, :, tt * P:(tt + 1) * P]

        def act_evac(act, st, s, it):
            e = s.evac
            for bank, tt in s.tiles:
                f = at(st, ("fill", bank), s.fill[bank], it)
                if e["kind"] == "store":
                    wait_done(act, st, s, bank, it)
                    p = at(st, ("put", bank), s.put[bank], it)
                    if bank == 4:
                        act.wait_ge(mod_put, p)
                    elif not (isinstance(p, int) and p == 0):
                        act.wait_ge(stored[bank], 16 * p)
                    r = e["rows"]
                    if e.get("gates"):
                        c0 = e["gates"]
                        nc.scalar.activation(nsa_g[:, tt, :], acc[:, bank, c0:c0 + 24], ACT.Tanh, scale=0.5)\
                          .then_inc(nsa_ready, 1)
                    nc.scalar.activation(stage_bufs[bank][0:r, 0:s.width], acc[0:r, BANK[bank], 0:s.width],
                                         e["func"], scale=e["scale"]).then_inc(acc_free[bank], 1)
                elif e["kind"] == "relu2":
                    wait_done(act, st, s, bank, it)
                    if tt == 0:
                        r = at(st, "relu2", s.nth, it)
                        if not (isinstance(r, int) and r == 0):
                            act.wait_ge(ht_done, r)
                    nc.scalar.activation(relu_t[:, tt, :], acc[:, bank, :], ACT.Relu)\
                      .then_inc(acc_free[bank], 1)

        def act_hidden(act, st, s, it):
            act.wait_ge(ht_done, at(st, "relu2", s.nth, it) + 1)
            for tt in range(2):
                last = nc.scalar.activation(hid(a_hi, s, tt), acc[:, 6 + tt, :].rearrange("p (j t) -> p j t", j=4),
                                            ACT.Copy)
            last.then_inc(hh_done, 1)

        def dve_hidden(dve, st, s, it):
            dve.wait_ge(hh_done, at(st, "relu2", s.nth, it) + 1)
            for tt in range(2):
                last = nc.vector.tensor_tensor(hid(a_lo, s, tt), acc[:, 6 + tt, :].rearrange("p (j t) -> p j t", j=4),
                                               hid(a_hi, s, tt).bitcast(F32), ALU.subtract)
            last.then_inc(hl_done, 1)

        def dve_evac(dve, st, s, it):
            e = s.evac
            if e["kind"] not in ("resid", "gresid", "branch"):
                return
            for bank, tt in s.tiles:
                f = at(st, ("fill", bank), s.fill[bank], it)
                wait_done(dve, st, s, bank, it)
                n = e.get("n", 0)
                if e["kind"] == "resid":
                    x = XR[:, tt, n * G:(n + 1) * G]
                    nc.vector.scalar_tensor_tensor(out=x, in0=acc[:, bank, :], scalar=e["scale"], in1=x,
                                                   op0=ALU.mult, op1=ALU.add).then_inc(acc_free[bank], 1)
                elif e["kind"] == "gresid":
                    x = (CX[:, tt, n * G:(n + 1) * G] if tt < 2 else XR[:, tt - 2, n * G:(n + 1) * G])
                    g = (gbc_c if tt < 2 else gbc_x)[:, n * G:(n + 1) * G]
                    nc.vector.tensor_tensor(prod_g[:, tt, :], acc[:, bank, :], g, ALU.mult)\
                      .then_inc(acc_free[bank], 1)
                    dve.wait_ge(acc_free[bank], f + 1)
                    nc.vector.tensor_tensor(x, x, prod_g[:, tt, :], ALU.add).then_inc(gres_tmp, 1)
                else:
                    if tt == 0:
                        dve.wait_ge(gate_in[s.nth % 2], 32 * (s.nth // 2 + 1))
                    x = MIX[:, tt, n * G:(n + 1) * G]
                    dst = x if e["m"] == 0 else prod_t[:, tt, :]
                    nc.vector.scalar_tensor_tensor(out=dst, in0=gate_t[:, s.nth % 2, tt, :], scalar=1.0,
                                                   in1=acc[:, bank, :], op0=ALU.add, op1=ALU.mult)\
                      .then_inc(acc_free[bank], 1)
                    dve.wait_ge(acc_free[bank], f + 1)
                    if e["m"] > 0:
                        nc.vector.tensor_tensor(x, x, prod_t[:, tt, :], ALU.add).then_inc(branch_tmp, 1)
                    else:
                        dve.sem_inc(branch_tmp, 1)
            if e["kind"] == "branch":
                dve.wait_ge(branch_tmp, 2 * (s.nth + 1))

        def stream(eng, st, split, evac, hidden):
            def body(it):
                steps = st.steps
                for i, s in enumerate(steps + [None]):
                    if s is not None:
                        split(eng, st, s, 0, it)
                    if i:
                        evac(eng, st, steps[i - 1], it)
                    if s is not None:
                        for c in range(1, len(s.chunks)):
                            split(eng, st, s, c, it)
                            if c == 2 and i and steps[i - 1].evac["kind"] == "relu2":
                                hidden(eng, st, steps[i - 1], it)
            passes(eng, st, body)

        def act_stream(act, st):
            stream(act, st, split_hi, act_evac, act_hidden)

        def dve_stream(dve, st):
            stream(dve, st, split_lo, dve_evac, dve_hidden)

        def pool_store(pool, st, s, it):
            e = s.evac
            for bank, tt in s.tiles:
                hold(pool, acc_free[bank], at(st, ("fill", bank), s.fill[bank] + 1, it))
                pool.dma_start(e["dst"](it, tt, s.width), stage_bufs[bank][0:e["rows"], 0:s.width])\
                    .then_inc(stored[bank], 16)
                if bank == 4:
                    hold(pool, stored[4], 16 * (at(st, ("put", 4), s.put[4], it)))
                    pool.sem_inc(mod_put, 1)
            if e.get("gates"):
                pool.wait_ge(nsa_ready, 2)
                pool.dma_start(AG.rearrange("(t p) n -> p t n", p=P), nsa_g[:, :, :]).then_inc(nsa_out, 16)

        def pool_stream(pool, st):
            def body(it):
                for s in st.steps:
                    e = s.evac
                    if e["kind"] == "relu2":
                        for bank, tt in s.tiles:
                            hold(pool, acc_free[bank], at(st, ("fill", bank), s.fill[bank] + 1, it))
                            last = nc.gpsimd.tensor_tensor(relu_t[:, tt, :], relu_t[:, tt, :], relu_t[:, tt, :],
                                                           ALU.mult)
                        last.then_inc(sq_done, 1)
                    elif e["kind"] == "store":
                        pool_store(pool, st, s, it)
            if st.name == "branch":
                for s in st.steps:
                    q, n, m = s.nth, s.evac["n"], s.evac["m"]
                    if q >= 2:
                        pool.wait_ge(branch_tmp, 2 * (q - 1))
                    for tt in range(2):
                        pool.dma_start(gate_t[:, q % 2, tt, :], GT[tt * P:(tt + 1) * P, m * DM + n * G:m * DM + (n + 1) * G])\
                            .then_inc(gate_in[q % 2], 16)
            else:
                passes(pool, st, body)

        def wait_stored(eng, upto):
            st = stages[upto]
            for b in range(5):
                k = st.base.get(("put", b), 0) + st.per.get(("put", b), 0) * st.times - (b == 4)
                if k:
                    eng.wait_ge(stored[b], 16 * k)

        def wait_freed(eng, upto):
            if upto is None:
                return
            st = stages[upto]
            for b in range(5):
                k = st.base.get(("fill", b), 0) + st.per.get(("fill", b), 0) * st.times
                if k:
                    eng.wait_ge(acc_free[b], k)

        prep_count = {"u": 0, "x": 0, "h": 0, "norm": 0}
        xn_ready = sem("xn_ready")
        tr_done = sem("tr_done")
        v_done = sem("v_done")
        ph_done, pl_done = sem("prep_hi_done"), sem("prep_lo_done")
        norm_ss, norm_rs = sem("norm_ss"), sem("norm_rs")

        class Prep:

            def __init__(self, name, tts, kts, T, after, off=0, vecs=None, scale=1.0, src=None):
                self.name, self.tts, self.kts, self.T, self.after = name, tts, kts, T, after
                self.off, self.vecs, self.scale = off, vecs, scale
                self.src = src or (lambda i: xn[:, i % 2, :])
                self.units = [(i, b) for i in range(len(tts)) for b in range(kts // 4)] if kts >= 4 else \
                             [(i, 0) for i in range(len(tts))]
                self.nb = min(kts, 4)
                self.u0, self.x0, self.h0 = prep_count["u"], prep_count["x"], prep_count["h"]
                prep_count["u"] += len(self.units)
                prep_count["x"] += len(tts)
                prep_count["h"] += len(self.units) if vecs else 0

            def bank(self, u):
                return 5 + u % 2

            def dst(self, t, tt, b):
                _, slot, k0 = tt
                o = self.off + (k0 + b * 4) * self.T
                return t[:, o:o + self.nb * self.T].rearrange("p (k t) -> p k t", k=self.nb)[
                    :, :, slot * P:(slot + 1) * P]

            def pe(self, pe):
                for u, (i, b) in enumerate(self.units):
                    pe.wait_ge(xn_ready, self.x0 + i + 1)
                    if u >= 2 or (self.u0 and u == 0):
                        u_ = u if u else 1
                        pe.wait_ge(pl_done if self.vecs is None else v_done, self.u0 + u_ - 1)
                    for j in range(self.nb):
                        last = nc.tensor.transpose(acc[:, self.bank(u), j * P:(j + 1) * P],
                                                   self.src(i)[:, (b * 4 + j) * P:(b * 4 + j + 1) * P], ident[:, :])
                    last.then_inc(tr_done, 1)

            def act(self, act, produce=None):
                wait_freed(act, self.after)
                per = len(self.units) // len(self.tts)
                if produce:
                    produce(act, 0)
                for u, (i, b) in enumerate(self.units):
                    tt = self.tts[i]
                    if produce and u % per == 0 and i + 1 < len(self.tts):
                        produce(act, i + 1)
                    act.wait_ge(tr_done, self.u0 + u + 1)
                    src = acc[:, self.bank(u), 0:self.nb * P].rearrange("p (k t) -> p k t", k=self.nb)
                    if self.vecs is None:
                        nc.scalar.activation(self.dst(a_hi, tt, b), src, ACT.Copy, scale=self.scale)\
                          .then_inc(v_done, 1)
                    else:
                        if u >= 2:
                            act.wait_ge(pl_done, self.u0 + u - 1)
                        g, s = self.vecs(tt[0])
                        for j in range(self.nb):
                            k = b * 4 + j
                            last = nc.scalar.activation(aff[:, u % 2, j, :], src[:, j, :], ACT.Identity,
                                                        bias=s[:, k:k + 1], scale=g[:, k:k + 1])
                        last.then_inc(v_done, 1)

            def dve(self, dve, produce=None):
                wait_freed(dve, self.after)
                per = len(self.units) // len(self.tts)
                if produce:
                    produce(dve, 0)
                for u, (i, b) in enumerate(self.units):
                    tt = self.tts[i]
                    if produce and u % per == 0 and i + 1 < len(self.tts):
                        produce(dve, i + 1)
                    dve.wait_ge(v_done, self.u0 + u + 1)
                    src = acc[:, self.bank(u), 0:self.nb * P].rearrange("p (k t) -> p k t", k=self.nb)
                    hi, lo = self.dst(a_hi, tt, b), self.dst(a_lo, tt, b)
                    if self.vecs is None and self.scale == 1.0:
                        nc.vector.tensor_tensor(lo, src, hi.bitcast(F32), ALU.subtract).then_inc(pl_done, 1)
                    elif self.vecs is None:
                        nc.vector.scalar_tensor_tensor(out=lo, in0=src, scalar=self.scale, in1=hi.bitcast(F32),
                                                       op0=ALU.mult, op1=ALU.subtract).then_inc(pl_done, 1)
                    else:
                        v = aff[:, u % 2, 0:self.nb, :]
                        nc.vector.tensor_copy(hi, v).then_inc(ph_done, 1)
                        dve.wait_ge(ph_done, self.h0 + u + 1)
                        nc.vector.tensor_tensor(lo, v, hi.bitcast(F32), ALU.subtract).then_inc(pl_done, 1)

            def finish(self, pe):
                pe.wait_ge(pl_done, self.u0 + len(self.units))

        pr = Arena([SCR])
        xn_at = SCR[0] + (-SCR[0]) % 32
        xn = pr("xn", [P, 2, DM])
        aff = pr("aff", [P, 2, 4, P])
        gt2 = pr("gt2", [P, DM])
        V_MIX, V_MLP, V_ZERO, V_NG, V_CTX, V_X = 0, 1, 2, 3, 4, 6

        def xtile(tt, T4_):
            if not T4_:
                return XR[:, tt, :]
            return CX[:, tt, :] if tt < 2 else XR[:, tt - 2, :]

        def pow_half(pool, dst, src, n, link, eps=EPS):
            link(nc.gpsimd.tensor_scalar(dst, src, 1.0 / n, eps, ALU.mult, ALU.add))
            w = int(np.prod(dst.shape[1:]))
            return nc.gpsimd.tensor_tensor(dst, dst, bass.AP(half[:, 0:1].tensor, half[:, 0:1].offset,
                                                             [list(half[:, 0:1].ap[0]), [0, w]]), ALU.pow)

        class Links:

            def __init__(self, name):
                self.name, self.sem, self.n, self.more, self.eng = name, sem(name), 0, 0, None

            @staticmethod
            def wait(eng, s, value):
                eng.wait_ge(s, value)

            def __call__(self, ins):
                self.n += 1
                ins.then_inc(self.sem, 1)
                (hold if self.name == "pool_link" else Links.wait)(self.eng, self.sem, self.n + self.more)

            def enter(self, it, per, times):
                self.start, self.per, self.times = self.n, per, times
                self.more = it * per if times > 1 else 0

            def leave(self):
                assert self.n - self.start == self.per, (self.n - self.start, self.per)
                self.n += self.per * (self.times - 1)
                self.more = 0

        links = {"dve": Links("dve_link"), "pool": Links("pool_link")}

        class Norm:

            def __init__(self, prep, four, col):
                self.p, self.four, self.col = prep, four, col
                self.n0 = prep_count["norm"]
                prep_count["norm"] += len(prep.tts)

            def x(self, i):
                return xtile(self.p.tts[i][0], self.four)

            def act(self, act, i):
                if i >= 2:
                    act.wait_ge(tr_done, self.p.u0 + (i - 1) * (len(self.p.units) // len(self.p.tts)))
                nc.scalar.activation(xn[:, i % 2, :], self.x(i), ACT.Square,
                                     accum_out=small[:, self.col + i:self.col + i + 1]).then_inc(norm_ss, 1)

            def pool(self, pool):
                link = links["pool"]
                for i in range(len(self.p.tts)):
                    pool.wait_ge(norm_ss, self.n0 + i + 1)
                    c = small[:, self.col + i:self.col + i + 1]
                    pow_half(pool, c, c, DM, link).then_inc(norm_rs, 1)

            def dve(self, dve, i):
                dve.wait_ge(norm_rs, self.n0 + i + 1)
                c = small[:, self.col + i:self.col + i + 1]
                nc.vector.tensor_scalar(xn[:, i % 2, :], self.x(i), c, None, ALU.mult)\
                  .then_inc(xn_ready, 1)

        at_count = {}
        s = lambda n: sem("at_" + n)
        at_loaded, at_shaped, j_done = s("loaded"), s("shaped"), s("j_done")
        j_copied = [s("j_copied_act"), s("j_copied_dve")]
        s_done, m_done, p_done, t_done, tc_done = s("s_done"), s("m_done"), s("p_done"), s("t_done"), s("tc_done")
        o_done, e_done, at_saved, at_ss, at_rs = s("o_done"), s("e_done"), s("saved"), s("ss"), s("rs")
        rows_in = s("rows_in")
        rows_open, pass_open, outs_free = s("rows_open"), s("pass_open"), s("outs_free")

        class Attn:

            def __init__(self, name, times, guard=False, fill=None):
                self.name, self.times, self.guard, self.fill = name, times, guard, fill
                self.jobs, self.units, self.rows, self.loads, self.saves = [], [], [], [], []
                self.shape_ops, self.late_ops, self.norms, self.shape_n, self.base = None, None, [], 0, {}
                self.slots, self.outs = {}, {}
                if fill is not None:
                    n = 0
                    for s_ in fill.steps:
                        for c in range(len(s_.chunks)):
                            self.slots.setdefault(3 + n * 3 // 2, []).append((s_, c))
                            n += 1
                        self.outs[3 + (n - 1) * 3 // 2 + 1] = s_

            def fill_chunks(self, slot, f, eng, it):
                for s_, c in self.slots.get(slot, []):
                    f(eng, self.fill, s_, c, it)

            def place_rows(self, ar):
                n = self.name
                self.pb, self.ptb = ar(n + "_p", [P, 3, G]), ar(n + "_pt", [P, 2, 4, P])
                self.st = ar(n + "_st", [P, 8, 4])

            def seal(self):
                self.U, self.J = len(self.units), len(self.jobs)
                J = self.J
                adds = dict(u=self.U, j=J, ja=(J + 1) // 2, jd=J // 2, passes=1, rows=len(self.rows), loads=len(self.loads),
                            saves=len(self.saves), ss=1 if self.norms else 0)
                for k, v in adds.items():
                    self.base[k] = at_count.get(k, 0)
                    at_count[k] = at_count.get(k, 0) + v * self.times
                at_count["open"] = at_count.get("open", 0)
                self.base["open"] = at_count["open"]
                at_count["open"] += self.times + 1
                self.sinks = [sum(1 for w in self.units[:u] if w.sink is not None) for u in range(self.U + 1)]
                self.el = [0]
                for w in self.units:
                    self.el.append(self.el[-1] + 1 + (w.sink is not None or self.guard) + (w.coeff is not None))

            def each(self, eng, body):
                if self.times > 1:
                    with eng.Fori(0, self.times) as it:
                        body(it)
                else:
                    body(0)

            def pool(self, pool):
                B = self.base

                pool.sem_inc(outs_free, 1)

                def body(it):
                    if self.norms:
                        hold(pool, at_ss, B['ss'] + it + 1)
                        link = links["pool"]
                        link.enter(it, len(self.norms), self.times)
                        for c, w in self.norms:
                            last = pow_half(pool, c, c, w, link)
                        last.then_inc(at_rs, 1)
                        link.leave()
                    if self.fill is not None:
                        for s_ in self.fill.steps:
                            pool_store(pool, self.fill, s_, it)
                    for q, (dst, src) in enumerate(self.saves):
                        if q == 0:
                            hold(pool, e_done, B['u'] + self.U * it + self.U)
                        pool.dma_start(dst(it), src).then_inc(at_saved, 16)
                    hold(pool, at_saved, 16 * (B['saves'] + len(self.saves) * (it + 1)))
                    pool.sem_inc(outs_free, 1)
                self.each(pool, body)

            def sp(self, sp):
                B = self.base
                if B['open']:
                    sp.wait_ge(outs_free, B['open'])

                def body(it):
                    hold(sp, rows_open, B['open'] + it + 1)
                    for dst, src in self.rows:
                        sp.dma_start(dst, src(it), allow_slow_non_contiguous=True).then_inc(rows_in, 16)
                    hold(sp, pass_open, B['open'] + it + 1)
                    for dst, src in self.loads:
                        sp.dma_start(dst, src(it), allow_slow_non_contiguous=True).then_inc(at_loaded, 16)
                    if self.fill is not None:
                        for s_ in self.fill.steps:
                            sp_chunks(sp, self.fill, s_, it)
                self.each(sp, body)

            def pe(self, pe):
                U, J, B = self.U, self.J, self.base

                def body(it):
                    if self.fill is not None:
                        hold(pe, acc_free[4], at(self.fill, ("fill", 4), 0, it))
                    for j, (srcs, _, _) in enumerate(self.jobs):
                        if j == 0:
                            hold(pe, at_shaped, B['passes'] + it + 1)
                        if j >= 2:
                            done = (j // 2)
                            tot = (J + 1) // 2 if j % 2 == 0 else J // 2
                            hold(pe, j_copied[j % 2], B['jd' if j % 2 else 'ja'] + tot * it + done)
                        for x, src in enumerate(srcs):
                            w = src.shape[-1]
                            last = nc.tensor.transpose(acc[0:w, j % 2, x * P:(x + 1) * P], src, ident[:, :])
                        last.then_inc(j_done, 1)
                    pe.wait_ge(j_copied[0], B['ja'] + ((J + 1) // 2) * (it + 1))
                    if J > 1:
                        pe.wait_ge(j_copied[1], B['jd'] + (J // 2) * (it + 1))
                    hold(pe, at_loaded, 16 * (B['loads'] + len(self.loads) * (it + 1)))
                    for u in range(U + 3):
                        if u < U:
                            w = self.units[u]
                            if u >= 2:
                                pe.wait_ge(p_done, B['u'] + U * it + u - 1)
                            bank = 4 + u % 2
                            n = len(w.q)
                            for x in range(n):
                                last = nc.tensor.matmul(acc[:, bank, 0:w.keys], w.q[x], w.k[x], start=x == 0,
                                                        stop=x == n - 1 and w.bias is None)
                            if w.bias is not None:
                                b, c0 = w.bias
                                last = nc.tensor.matmul(acc[:, bank, c0:w.keys], ident[:, :], b,
                                                        start=False, stop=True)
                            last.then_inc(s_done, 1)
                        self.fill_chunks(u, pe_chunk, pe, it)
                        if 0 <= u - 2 < U:
                            t = u - 2
                            w = self.units[t]
                            pe.wait_ge(p_done, B['u'] + U * it + t + 1)
                            if t >= 2:
                                pe.wait_ge(tc_done, B['u'] + U * it + t - 1)
                            for x, vt in enumerate(w.v):
                                kk = min(P, w.keys - x * P)
                                last = nc.tensor.transpose(acc[0:kk, (2, 6)[t % 2], x * P:(x + 1) * P],
                                                           self.pb[:, t % 3, x * P:x * P + kk], ident[:, :])
                            last.then_inc(t_done, 1)
                        if 0 <= u - 3 < U:
                            t = u - 3
                            w = self.units[t]
                            pe.wait_ge(tc_done, B['u'] + U * it + t + 1)
                            if t >= 2:
                                pe.wait_ge(e_done, B['u'] + U * it + t - 1)
                            for x, vt in enumerate(w.v):
                                kk = min(P, w.keys - x * P)
                                last = nc.tensor.matmul(acc[:, (3, 7)[t % 2], 0:P], self.ptb[0:kk, t % 2, x, :], vt,
                                                        start=x == 0, stop=x == len(w.v) - 1)
                            last.then_inc(o_done, 1)
                self.each(pe, body)
                if self.fill is not None:
                    n = self.fill.base[("fill", 4)] + self.fill.per[("fill", 4)] * self.times
                    pe.wait_ge(acc_free[4], n)

            def act(self, act):
                U, J, B = self.U, self.J, self.base

                def body(it):
                    for j in range(0, J, 2):
                        act.wait_ge(j_done, B['j'] + J * it + j + 1)
                        srcs, dst, scale = self.jobs[j]
                        w, n = srcs[0].shape[-1], len(srcs)
                        nc.scalar.activation(dst, acc[0:w, 0, 0:n * P], ACT.Copy, scale=scale)\
                          .then_inc(j_copied[0], 1)
                    for u in range(U + 2):
                        if u < U:
                            w = self.units[u]
                            act.wait_ge(m_done, B['u'] + U * it + u + 1)
                            if u >= 3:
                                act.wait_ge(t_done, B['u'] + U * it + u - 2)
                            st = self.st[:, u % 8, :]
                            if w.sink is not None:
                                nc.scalar.activation(st[:, 2:3], w.sink, ACT.Exp, bias=st[:, 0:1])
                            nc.scalar.activation(self.pb[:, u % 3, 0:w.keys], acc[:, 4 + u % 2, 0:w.keys], ACT.Exp,
                                                 bias=st[:, 0:1], accum_out=st[:, 1:2]).then_inc(p_done, 1)
                        self.fill_chunks(u + 2, split_hi, act, it)
                        if u in self.outs:
                            act_evac(act, self.fill, self.outs[u], it)
                        if 0 <= u - 2 < U:
                            t = u - 2
                            w = self.units[t]
                            act.wait_ge(t_done, B['u'] + U * it + t + 1)
                            if t >= 2:
                                act.wait_ge(o_done, B['u'] + U * it + t - 1)
                            kk, n = min(P, w.keys), len(w.v)
                            nc.scalar.activation(self.ptb[0:kk, t % 2, 0:n, :],
                                                 acc[0:kk, (2, 6)[t % 2], 0:n * P].rearrange("p (n t) -> p n t", n=n),
                                                 ACT.Copy).then_inc(tc_done, 1)
                self.each(act, body)

            def dve(self, dve):
                U, J, B = self.U, self.J, self.base

                dve.sem_inc(rows_open, 1)
                dve.sem_inc(pass_open, 1)

                def body(it):
                    dve.wait_ge(rows_in, 16 * (B['rows'] + len(self.rows) * (it + 1)))
                    link = links["dve"]
                    link.enter(it, self.shape_n + self.sinks[U] + self.el[U], self.times)
                    if self.shape_ops:
                        self.shape_ops(dve, link, it)
                    dve.sem_inc(at_shaped, 1)
                    for j in range(1, J, 2):
                        dve.wait_ge(j_done, B['j'] + J * it + j + 1)
                        srcs, dst, scale = self.jobs[j]
                        w, n = srcs[0].shape[-1], len(srcs)
                        nc.vector.tensor_scalar(dst, acc[0:w, 1, 0:n * P], scale, None, ALU.mult)\
                          .then_inc(j_copied[1], 1)
                    dve.wait_ge(j_done, B['j'] + J * (it + 1))
                    dve.sem_inc(rows_open, 1)
                    dve.wait_ge(at_loaded, 16 * (B['loads'] + len(self.loads) * (it + 1)))
                    dve.wait_ge(outs_free, B['open'] + it + 1)
                    if self.late_ops:
                        self.late_ops(dve, link, it)
                    for u in range(U + 4):
                        if u < U:
                            w = self.units[u]
                            dve.wait_ge(s_done, B['u'] + U * it + u + 1)
                            if u >= 8:
                                dve.wait_ge(e_done, B['u'] + U * it + u - 7)
                            m = self.st[:, u % 8, 0:1]
                            ins = nc.vector.tensor_reduce(m, acc[:, 4 + u % 2, 0:w.keys], AX.X, ALU.max, negate=True)
                            if w.sink is not None:
                                link(ins)
                                ins = nc.vector.scalar_tensor_tensor(out=m, in0=w.sink, scalar=-1.0, in1=m,
                                                                     op0=ALU.mult, op1=ALU.min)
                            ins.then_inc(m_done, 1)
                        self.fill_chunks(u + 1, split_lo, dve, it)
                        if 0 <= u - 4 < U:
                            t = u - 4
                            w = self.units[t]
                            st = self.st[:, t % 8, :]
                            dve.wait_ge(o_done, B['u'] + U * it + t + 1)
                            if w.add:
                                dve.wait_ge(e_done, B['u'] + U * it + t)
                            if w.sink is not None and self.guard:
                                link(nc.vector.tensor_scalar(st[:, 1:2], st[:, 1:2], st[:, 2:3], TINY,
                                                             ALU.add, ALU.max))
                            elif w.sink is not None:
                                link(nc.vector.tensor_tensor(st[:, 1:2], st[:, 1:2], st[:, 2:3], ALU.add))
                            elif self.guard:
                                link(nc.vector.tensor_scalar(st[:, 1:2], st[:, 1:2], TINY, None, ALU.max))
                            link(nc.vector.reciprocal(st[:, 3:4], st[:, 1:2]))
                            if w.coeff is not None:
                                link(nc.vector.tensor_tensor(st[:, 3:4], st[:, 3:4], w.coeff, ALU.mult))
                            o = acc[:, (3, 7)[t % 2], 0:P]
                            if w.add:
                                nc.vector.scalar_tensor_tensor(out=w.out, in0=o, scalar=st[:, 3:4], in1=w.out,
                                                               op0=ALU.mult, op1=ALU.add).then_inc(e_done, 1)
                            else:
                                nc.vector.tensor_scalar(w.out, o, st[:, 3:4], None, ALU.mult)\
                                  .then_inc(e_done, 1)
                    dve.wait_ge(e_done, B['u'] + U * it + U)
                    dve.sem_inc(pass_open, 1)
                    link.leave()
                self.each(dve, body)
        setup_in = sem("setup_in")
        brev_mm, brev_sb, brev_out = sem("brev_mm"), sem("brev_sb"), sem("brev_out")
        silu_t, lam_e = sem("silu_t"), sem("lam_e")
        su = Arena([(ALO[0] + 16384, ALO[1])])
        onehot_t, relb_t = su("onehot_t", [BUCKETS, G]), su("relb_t", [BUCKETS, 24])
        bmask_t, brev_t = su("bmask_t", [24, G]), su("brev_t", [24, G])
        cv, ct = su("cv", [P, KT, 2]), su("ct", [P, KT, 2])
        lamv, lamp = su("lamv", [P, 4, 64]), su("lamp", [P, 2, 64])
        lam = small[:, 40:44]
        SETUP_LOADS = 13

        def bcast(ap, n=P):
            return bass.AP(ap.tensor, ap.offset, [[0, n]] + [list(x) for x in ap.ap])

        def setup_act_loads(act):
            loads = [(onehot_t[:, :], C["onehot"]), (relb_t[:, :], A["rel_bias"]), (bmask_t[:, :], C["bmask"]),
                     (cv[:, :, 0], A["c_ctx_2"].rearrange("(k p) -> p k", p=P)),
                     (cv[:, :, 1], A["c_2"][0].rearrange("(k p) -> p k", p=P)),
                     (vec[:, V_MIX, :], A["norm_mix"][0].rearrange("(k p) -> p k", p=P)),
                     (vec[:, V_MLP, :], A["norm_mlp"][0].rearrange("(k p) -> p k", p=P)),
                     (vec[:, V_NG, :], A["norm_g_2"][0].rearrange("(k p) -> p k", p=P)),
                     (lamv[:, 0, :], bcast(A["a_lam_q1_2"][0])), (lamv[:, 1, :], bcast(A["a_lam_k1_2"][0])),
                     (lamv[:, 2, :], bcast(A["a_lam_q2_2"][0])), (lamv[:, 3, :], bcast(A["a_lam_k2_2"][0])),
                     (small[:, 44:45], C["valid"])]
            assert len(loads) == SETUP_LOADS
            for dst, src in loads:
                act.dma_start(dst, src, allow_slow_non_contiguous=True).then_inc(setup_in, 16)

        def setup_gpsimd(pool):
            for s, n in ((acc_free[4], 1), (mod_put, 1), (ht_done, 1), (sq_done, 1),
                         (hh_done, 1), (hl_done, 1)):
                pool.sem_inc(s, n)
            nc.gpsimd.memset(half[:, :], -0.5)
            nc.gpsimd.memset(ident[:, :], 0.0).then_inc(setup_gp, 1)
            pool.wait_ge(setup_gp, 1)
            nc.gpsimd.affine_select(out=ident[:, :], in_=ident[:, :], compare_op=ALU.not_equal, fill=1.0, base=0,
                                    pattern=[[-1, P]], channel_multiplier=1).then_inc(setup_gp, 1)
            pool.wait_ge(setup_gp, 2)

        def setup_pe(pe):
            pe.wait_ge(setup_in, 16 * SETUP_LOADS)
            pe.wait_ge(setup_gp, 2)
            nc.tensor.matmul(acc[0:24, 7, :], relb_t[:, :], onehot_t[:, :], start=True, stop=True)\
              .then_inc(brev_mm, 1)

        def setup_act(act):
            act.wait_ge(setup_in, 16 * SETUP_LOADS)
            nc.scalar.activation(ct[:, :, :], cv[:, :, :], ACT.Tanh, scale=0.5).then_inc(silu_t, 1)
            act.wait_ge(lam_e, 1)
            nc.scalar.activation(lam[:, 0:2], lam[:, 0:2], ACT.Exp).then_inc(lam_e, 1)

        def setup_vector(dve):
            link = links["dve"]
            dve.wait_ge(setup_in, 16 * SETUP_LOADS)
            nc.vector.memset(vec[:, V_ZERO, :], 0.0)
            link(nc.vector.memset(MV[:, :].bitcast(F32), 0.0))
            link(nc.vector.tensor_tensor(lamp[:, 0, :], lamv[:, 0, :], lamv[:, 1, :], ALU.mult))
            link(nc.vector.tensor_tensor(lamp[:, 1, :], lamv[:, 2, :], lamv[:, 3, :], ALU.mult))
            nc.vector.tensor_reduce(lam[:, 0:2], lamp[:, :, :], AX.X, ALU.add).then_inc(lam_e, 1)
            dve.wait_ge(lam_e, 2)
            link(nc.vector.tensor_tensor(lam[:, 2:3], lam[:, 1:2], lam[:, 0:1], ALU.subtract))
            link(nc.vector.tensor_scalar(lam[:, 2:3], lam[:, 2:3], -LAM_INIT, None, ALU.add))
            dve.wait_ge(silu_t, 1)
            link(nc.vector.scalar_tensor_tensor(out=ct[:, :, :], in0=ct[:, :, :], scalar=1.0, in1=cv[:, :, :],
                                                op0=ALU.add, op1=ALU.mult))
            link(nc.vector.tensor_scalar(ct[:, :, :], ct[:, :, :], 0.5, None, ALU.mult))
            mv = MV[:, 0:4 * KT].rearrange("p (k c) -> p k c", c=4)
            link(nc.vector.tensor_copy(mv[:, :, 0:2], ct[:, :, :]))
            link(nc.vector.tensor_tensor(mv[:, :, 2:4], ct[:, :, :], mv[:, :, 0:2].bitcast(F32), ALU.subtract))
            dve.wait_ge(brev_mm, 1)
            nc.vector.tensor_tensor(brev_t[:, :], acc[0:24, 7, :], bmask_t[:, :], ALU.add).then_inc(brev_sb, 1)
            dve.wait_ge(brev_sb, 1)

        def setup_brev(pool):
            pool.wait_ge(brev_sb, 1)
            pool.dma_start(BREV[:, :], brev_t[:, :]).then_inc(brev_out, 16)
            pool.wait_ge(brev_out, 16)

        bt_out = sem("bt_out")

        def setup_bias_tiles(act):
            act.wait_ge(brev_out, 16)
            src = BREV[0]
            act.dma_start(BROW[:, :, :], bass.AP(src.tensor, 0, [[G, 24], [0, P], [1, G]])).then_inc(bt_out, 16)

        X2 = [(0, 0, 0), (1, 1, 0)]
        X4 = [(t, t, 0) for t in range(4)]
        row = lambda i: vec[:, i, :]
        p1 = Prep("p1", X2, KT, 256, None, vecs=lambda tt: (row(V_MIX), row(V_ZERO)))
        n1 = Norm(p1, False, 0)
        p2 = Prep("p2", [(0, 0, 0), (0, 0, 12), (1, 1, 0), (1, 1, 12)], 12, 256, "cmp1")
        p3 = Prep("p3", X2, KT, 256, "branch", src=lambda i: MIX[:, i, :])
        p4 = Prep("p4", X2, KT, 256, "out1", vecs=lambda tt: (row(V_MLP), row(V_ZERO)))
        n4 = Norm(p4, False, 4)
        mod_vecs = lambda tt: (row(V_CTX), row(V_CTX + 1)) if tt < 2 else (row(V_X), row(V_X + 1))
        p5 = Prep("p5", X4, KT, 512, "mlp", vecs=mod_vecs)
        n5 = Norm(p5, True, 8)
        p6 = Prep("p6", X4, KT, 512, "in2_end")
        p7 = Prep("p7", X4, KT, 512, "out2", vecs=mod_vecs)
        n7 = Norm(p7, True, 12)
        p8q = Prep("p8q", [(2, 2, 0), (3, 3, 0)], 4, 512, "in3")
        p8k = Prep("p8k", X4, 2, 512, "in3", off=2048)
        p9 = Prep("p9", [(2, 2, 0), (3, 3, 0)], KT, 512, "kvb")

        cmp_in, cmp_tr = sem("cmp_in"), sem("cmp_tr")
        cmp_hi, cmp_th, cmp_tr2, cmp_gt, cmp_mm, cmp_o, cmp_out = (
            sem("cmp_hi"), sem("cmp_th"), sem("cmp_tr2"), sem("cmp_gt"), sem("cmp_mm"),
            sem("cmp_o"), sem("cmp_out"))
        cp = Arena([SCR])
        CW = 2176
        cmp_rows = cp("cmp_rows", [P, 2, 512])
        cmp_pos = cp("cmp_pos", [64, HD])
        kvT = cp("kvT", [P, 4, 256])
        posT = cp("posT", [P, 64])
        cmp_v = cp("cmp_v", [P, CW])
        gel = cp("gel", [32, 4, 512])
        cmp_w2t = cp("cmp_w2t", [P, 2, 2, HD])
        gT = place("gT", [P, 4, 32], AHI[0])
        cmp_ok = place("cmp_ok", [P, 32], AHI[0] + 1024)
        cmp_ov = place("cmp_ov", [32, HD], AHI[0] + 2048)

        def cmp_pool_loads(pool):
            wait_stored(pool, "qkv")
            pool.wait_ge(pl_done, p1.u0 + len(p1.units))
            for tt in range(2):
                pool.dma_start(cmp_rows[:, tt, :], U1[tt * P:(tt + 1) * P, 1024:1536]).then_inc(cmp_in, 16)
            pool.dma_start(cmp_pos[:, :], A["cmp_pos"][0].rearrange("w l d -> (w l) d")).then_inc(cmp_in, 16)
            pool.dma_start(cmp_w2t[:, :, :, :], A["cmp_w2"][0].rearrange("w (j p) d -> p w j d", p=P))\
                .then_inc(cmp_in, 16)

        def cmp_pe_prep(pe):
            pe.wait_ge(cmp_in, 64)
            for tt in range(2):
                for b in range(4):
                    nc.tensor.transpose(acc[:, 5 + b // 2, (b % 2) * 256 + tt * P:(b % 2) * 256 + (tt + 1) * P],
                                        cmp_rows[:, tt, b * P:(b + 1) * P], ident[:, :])
            nc.tensor.transpose(acc[:, 7, 0:64], cmp_pos[:, :], ident[0:64, 0:64]).then_inc(cmp_tr, 1)

        def cmp_dve_prep(dve):
            link = links["dve"]
            dve.wait_ge(cmp_tr, 1)
            for b in range(2):
                link(nc.vector.tensor_copy(kvT[:, 2 * b:2 * b + 2, :],
                                           acc[:, 5 + b, :].rearrange("p (a t) -> p a t", a=2)))
            link(nc.vector.tensor_copy(posT[:, :], acc[:, 7, 0:64]))
            link(nc.vector.memset(cmp_v[:, :], 0.0))
            for w in range(2):
                for kv in range(2):
                    o = cmp_v[:, w * 1024:w * 1024 + 960].rearrange("p (l v c) -> p l v c", l=32, v=2)[:, :, kv, :]
                    base = kvT[:, 2 * w + kv, 0:1]
                    src = bass.AP(base.tensor, base.offset, [list(base.ap[0]), [1, 32], [16, NCMP]])
                    pos = posT[:, w * 32:w * 32 + 1]
                    pb = bass.AP(pos.tensor, pos.offset, [list(pos.ap[0]), [1, 32], [0, NCMP]])
                    link(nc.vector.tensor_tensor(o, src, pb, ALU.add))
            wait_freed(dve, "gates")
            link(nc.vector.tensor_copy(a_hi[:, 4096:4096 + CW], cmp_v[:, :]))
            nc.vector.tensor_tensor(a_lo[:, 4096:4096 + CW], cmp_v[:, :], a_hi[:, 4096:4096 + CW].bitcast(F32),
                                    ALU.subtract).then_inc(cmp_hi, 1)

        def cmp_dve_gelu(dve):
            for w in range(2):
                wait_done(dve, stages["cmp1"], stages["cmp1"].steps[w], w, 0)
            g = lambda i: gel[0:30, i, :].rearrange("p (w n) -> p w n", w=2)
            link = links["dve"]
            link(nc.vector.tensor_copy(g(0), acc[0:30, 0:2, 0:256]))
            for w in range(2):
                dve.sem_inc(acc_free[w], 1)
            link(nc.vector.tensor_tensor(g(1), g(0), g(0), ALU.mult))
            link(nc.vector.tensor_scalar(g(1), g(1), 0.044715, 1.0, ALU.mult, ALU.add))
            nc.vector.tensor_tensor(g(1), g(1), g(0), ALU.mult).then_inc(cmp_th, 1)
            dve.wait_ge(cmp_th, 2)
            link(nc.vector.scalar_tensor_tensor(out=g(2), in0=g(2), scalar=1.0, in1=g(0), op0=ALU.add, op1=ALU.mult))
            nc.vector.tensor_scalar(g(3), g(2), 0.5, None, ALU.mult).then_inc(cmp_gt, 1)
            dve.wait_ge(cmp_tr2, 1)
            nc.vector.tensor_copy(gT[:, :, 0:30], acc[:, 5, 0:128].rearrange("p (a b) -> p a b", a=4)[:, :, 0:30])\
              .then_inc(cmp_gt, 1)
            dve.wait_ge(cmp_mm, 1)
            nc.vector.tensor_copy(cmp_ok[:, 0:30], acc[:, 6, 0:30]).then_inc(cmp_o, 1)
            nc.vector.tensor_copy(cmp_ov[0:30, :], acc[0:30, 7, 0:P]).then_inc(cmp_o, 1)

        def cmp_act(act):
            act.wait_ge(cmp_th, 1)
            nc.scalar.activation(gel[0:30, 2, :], gel[0:30, 1, :], ACT.Tanh, scale=GELU_C).then_inc(cmp_th, 1)

        def cmp_pe(pe):
            pe.wait_ge(cmp_gt, 1)
            for a in range(4):
                last = nc.tensor.transpose(acc[:, 5, a * 32:a * 32 + 30], gel[0:30, 3, a * P:(a + 1) * P],
                                           ident[0:30, 0:30])
            last.then_inc(cmp_tr2, 1)
            pe.wait_ge(cmp_gt, 2)
            for j in range(2):
                nc.tensor.matmul(acc[:, 6, 0:30], cmp_w2t[:, 0, j, :], gT[:, j, 0:30], start=j == 0, stop=j == 1)
            for j in range(2):
                last = nc.tensor.matmul(acc[0:30, 7, 0:P], gT[:, 2 + j, 0:30], cmp_w2t[:, 1, j, :],
                                        start=j == 0, stop=j == 1)
            last.then_inc(cmp_mm, 1)

        def cmp_pool_store(pool):
            pool.wait_ge(cmp_o, 2)
            pool.dma_start(CMPK[:, :], cmp_ok[:, 0:30]).then_inc(cmp_out, 16)
            pool.dma_start(CMPV[:, :], cmp_ov[0:30, :]).then_inc(cmp_out, 16)
            pool.wait_ge(cmp_out, 32)

        at1 = Attn("at1", 2, guard=True, fill=stages["mod1"])
        ar = Arena([SCR, AHI, ALO])
        at1.place_rows(ar)
        q1 = [ar(f"q1_{m}", [P, 2, 512]) for m in range(3)]
        k1 = [ar(f"k1_{n}", [P, 2, HD]) for n in "swbc"]
        v1 = [ar(f"v1_{n}", [P, 2, HD]) for n in "swbc"]
        q1T = [ar(f"q1T_{m}", [P, 2, 4, P]) for m in range(3)]
        k1T = [ar(f"k1T_{n}", [P, 256]) for n in "swbc"]
        bias1 = [ar(f"bias1_{m}", [P, 4, 256]) for m in range(3)]
        ckT, cvt, cbias = ar("ckT", [P, NCMP]), ar("cvt", [NCMP, HD]), ar("cbias", [P, 2, 4, NCMP])
        gA, gV, sink1 = ar("gA", [P, 2, 12]), ar("gV", [P, 2, 4]), ar("sink1", [P, 4])
        ob1 = ar("ob1", [P, 2, 3, 512])
        QC = [0, 2584, 4120]
        KC = [1536, 2048, 3608, 5144]
        VC = [1792, 2304, 3864, 5400]

        def tiles_of(U, c0, w, step):
            n = U.shape[0] // P
            return lambda it: U[:, bass.ds(c0 + it * step, w)].rearrange("(t p) n -> p t n", p=P)

        def skewed(h0, off, per_key, keys, heads=4):
            def f(it):
                head = BROW[bass.ds(it * 4 + h0, heads), 0, off:off + 1]
                return bass.AP(head.tensor, head.offset, [[G - 1, P]] + [[P * G, 4]] * (heads > 1) + [[per_key, keys]])
            return f

        for m in range(3):
            at1.rows.append((q1[m][:, :, :], tiles_of(U1, QC[m], 512, 512)))
            at1.loads.append((bias1[m][:, :, :], skewed(8 * m, 127, 1, 256)))
        for n in range(4):
            at1.rows.append((k1[n][:, :, :], tiles_of(U1, KC[n], HD, HD)))
            at1.loads.append((v1[n][:, :, :], tiles_of(U1, VC[n], HD, HD)))
        for qt in range(2):
            for g in range(4):
                at1.loads.append((cbias[:, qt, g, :], skewed(g, 286 - P * qt, 16, NCMP, 1)))
        at1.loads.append((ckT[:, :], lambda it: CMPK[:, bass.ds(it * NCMP, NCMP)]))
        at1.loads.append((cvt[:, :], lambda it: CMPV[bass.ds(it * NCMP, NCMP), :]))
        at1.loads.append((gA[:, :, :], tiles_of(AG, 0, 12, 12)))
        at1.loads.append((sink1[:, :], lambda it: bcast(A["swa_sinks"][0, bass.ds(it * 4, 4)])))

        def shape1(dve, link, it):
            link(nc.vector.tensor_scalar(gA[:, :, :], gA[:, :, :], 0.5, 0.5, ALU.mult, ALU.add))
            g0 = gA[:, :, :].rearrange("p t (g b) -> p t g b", b=3)[:, :, :, 0]
            link(nc.vector.tensor_scalar(gV[:, 0, :], g0[:, 0, :], small[:, 44:45], None, ALU.mult))
            link(nc.vector.tensor_copy(gV[:, 1, :], g0[:, 1, :]))
        at1.late_ops, at1.shape_n = shape1, 3
        for m in range(3):
            for tt in range(2):
                at1.jobs.append(([q1[m][:, tt, g * P:(g + 1) * P] for g in range(4)],
                                 q1T[m][:, tt, :, :].rearrange("p g t -> p (g t)"), SCALE))
        for n in range(4):
            at1.jobs.append(([k1[n][:, tt, :] for tt in range(2)], k1T[n][:, :], 1.0))
        for g in range(4):
            for qt in range(2):
                L = (qt + 1) * P
                bb = lambda m: (bias1[m][:, g, 256 - L:256], 0)
                o = lambda m: ob1[:, qt, m, g * P:(g + 1) * P]
                vt = lambda n: [v1[n][:, t, :] for t in range(qt + 1)]
                gate = lambda b: gA[:, qt, 3 * g + b:3 * g + b + 1]
                qa = [q1T[0][:, qt, g, :]]
                at1.units += [
                    Unit(qa, [ckT[:, :]], [cvt[:, :]], NCMP, o(0), (cbias[:, qt, g, :], 0), None, gV[:, qt, g:g + 1]),
                    Unit(qa, [k1T[0][:, 0:L]], vt(0), L, o(0), bb(0), None, gate(1), True),
                    Unit(qa, [k1T[1][:, 0:L]], vt(1), L, o(0), bb(0), None, gate(2), True),
                    Unit([q1T[1][:, qt, g, :]], [k1T[2][:, 0:L]], vt(2), L, o(1), bb(1), sink1[:, g:g + 1]),
                    Unit([q1T[2][:, qt, g, :]], [k1T[3][:, 0:L]], vt(3), L, o(2), bb(2))]
        for tt in range(2):
            at1.saves.append((lambda it, tt=tt: OB[tt * P:(tt + 1) * P, :].rearrange("p (m n) -> p m n", m=3)[
                :, :, bass.ds(it * 512, 512)], ob1[:, tt, :, :]))
        at1.seal()

        def rope(link, x, o, h, cs, tmp):
            t, m = x.shape[1], x.shape[2]
            c, s = [bass.AP(a.tensor, a.offset, [list(a.ap[0]), list(a.ap[1]), [0, m], [1, h]]) for a in cs]
            x1, x2 = x[:, :, :, o:o + h], x[:, :, :, o + h:o + 2 * h]
            y = [tmp[:, i * t * m * h:(i + 1) * t * m * h].rearrange("p (t m h) -> p t m h", t=t, m=m)
                 for i in range(4)]
            link(nc.vector.tensor_tensor(y[0], x1, c, ALU.mult))
            link(nc.vector.tensor_tensor(y[1], x2, s, ALU.mult))
            link(nc.vector.tensor_tensor(y[2], x1, s, ALU.mult))
            link(nc.vector.tensor_tensor(y[3], x2, c, ALU.mult))
            link(nc.vector.tensor_tensor(x1, y[0], y[1], ALU.subtract))
            link(nc.vector.tensor_tensor(x2, y[2], y[3], ALU.add))

        def rows3(ap, inner):
            return bass.AP(ap.tensor, ap.offset, [list(ap.ap[0]), [1, ap.shape[1]], [0, inner]])

        def cols3(ap, outer):
            return bass.AP(ap.tensor, ap.offset, [list(ap.ap[0]), [0, outer], [1, ap.shape[1]]])

        atA = Attn("atA", 4, fill=stages["modA"])
        ar = Arena([SCR, AHI, ALO])
        atA.place_rows(ar)
        qA, kA, vA = (ar(n, [P, 4, 2, HD]) for n in ("qA", "kA", "vA"))
        qAT, kAT = ar("qAT", [P, 2, 4, P]), ar("kAT", [P, 2, 4, P])
        oA2, tmpA = ar("oA2", [P, 4, 2, HD]), ar("tmpA", [P, 2048])
        csA = ar("csA", [P, 2, 2, 32])
        for dst, c0 in ((qA, 0), (kA, 1024), (vA, 2048)):
            (atA.loads if dst is vA else atA.rows).append(
                (dst[:, :, :, :].rearrange("p t h d -> p t (h d)"), tiles_of(U2, c0, 256, 256)))
        atA.rows.append((csA[:, :, :, :], lambda it: C["cs64"].rearrange("c (t p) h -> p c t h", p=P)))

        def shapeA(dve, link, it):
            for x in (qA, kA):
                v = x[:, 2:4, :, :].rearrange("p t h (m d) -> p t (h m) d", m=2)
                rope(link, v, 0, 32, (csA[:, 0, :, :], csA[:, 1, :, :]), tmpA[:, :])
        atA.shape_ops, atA.shape_n = shapeA, 12
        for src, dst, sc in ((qA, qAT, 0.125), (kA, kAT, 1.0)):
            for h in range(2):
                atA.jobs.append(([src[:, t, h, :] for t in range(4)],
                                 dst[:, h, :, :].rearrange("p t n -> p (t n)"), sc))
        for h in range(2):
            for qt in range(4):
                L = 256 if qt < 2 else 512
                for m in range(2):
                    r = slice(64 * m, 64 * m + 64)
                    atA.units.append(Unit([qAT[r, h, qt, :]], [kAT[r, h, 0:L // P, :].rearrange("p t n -> p (t n)")],
                                          [vA[:, t, h, :] for t in range(L // P)], L, oA2[:, qt, h, :],
                                          coeff=lam[:, 2:3] if m else None, add=m == 1))
        atA.saves.append((lambda it: O2[:, bass.ds(it * 256, 256)].rearrange("(t p) n -> p t n", p=P),
                          oA2[:, :, :, :].rearrange("p t h d -> p t (h d)")))
        atA.seal()

        atB = Attn("atB", 2, fill=stages["modB"])
        ar = Arena([SCR, AHI, ALO])
        atB.place_rows(ar)
        qB_, kB, vB = ar("qB_", [P, 4, 4, HD]), ar("kB", [P, 4, HD]), ar("vB", [P, 4, HD])
        qBT, kBT = ar("qBT", [P, 4, 4, P]), ar("kBT", [P, 512])
        oB, tmpB = ar("oB", [P, 4, 4, HD]), ar("tmpB", [P, 2048])
        csB, bandB, sinkB = ar("csB", [P, 2, 2, 64]), ar("bandB", [P, 2, 256]), ar("sinkB", [P, 4])
        for dst, c0, w in ((qB_[:, :, :, :].rearrange("p t h d -> p t (h d)"), 3072, 512), (kB[:, :, :], 4096, HD),
                           (vB[:, :, :], 4352, HD)):
            (atB.loads if c0 == 4352 else atB.rows).append((dst, tiles_of(U2, c0, w, w)))
        atB.rows.append((csB[:, :, :, :], lambda it: C["cs128"].rearrange("c (t p) h -> p c t h", p=P)))
        atB.loads.append((bandB[:, :, :], lambda it: C["band"].rearrange("(t p) n -> p t n", p=P)))
        atB.loads.append((sinkB[:, :], lambda it: bcast(A["b_sink_2"][0, bass.ds(it * 4, 4)])))

        def shapeB(dve, link, it):
            cs = (csB[:, 0, :, :], csB[:, 1, :, :])
            rope(link, qB_[:, 2:4, :, :], 0, 64, cs, tmpB[:, :])
            rope(link, kB[:, 2:4, :].rearrange("p t (m d) -> p t m d", m=1), 0, 64, cs, tmpB[:, :])
        atB.shape_ops, atB.shape_n = shapeB, 12
        for t in range(4):
            atB.jobs.append(([qB_[:, t, g, :] for g in range(4)], qBT[:, t, :, :].rearrange("p g n -> p (g n)"), SCALE))
        atB.jobs.append(([kB[:, t, :] for t in range(4)], kBT[:, :], 1.0))
        for g in range(4):
            for qt in range(4):
                L = 256 if qt < 2 else 512
                atB.units.append(Unit([qBT[:, qt, g, :]], [kBT[:, 0:L]], [vB[:, t, :] for t in range(L // P)], L,
                                      oB[:, qt, g, :], bias=None if qt < 2 else (bandB[:, qt - 2, :], 256),
                                      sink=sinkB[:, g:g + 1]))
        atB.saves.append((lambda it: O2[:, bass.ds(1024 + it * 512, 512)].rearrange("(t p) n -> p t n", p=P),
                          oB[:, :, :, :].rearrange("p t h d -> p t (h d)")))
        atB.seal()

        atC = Attn("atC", 2)
        ar = Arena([SCR, AHI, ALO])
        atC.place_rows(ar)
        qC, kC, vC = ar("qC", [P, 2, 4, HD]), ar("kC", [P, 4, HD]), ar("vC", [P, 4, HD])
        qCT, kCT = ar("qCT", [P, 2, 4, P]), ar("kCT", [P, 512])
        oC, tmpC = ar("oC", [P, 2, 4, HD]), ar("tmpC", [P, 2048])
        csC, gC, rC = ar("csC", [P, 2, 2, 64]), ar("gC", [P, 2, HD]), ar("rC", [P, 16])
        lat = lambda U, c0, w, step: (lambda it: U[CTX:CTX + SEQ, bass.ds(c0 + it * step, w)]
                                      .rearrange("(t p) n -> p t n", p=P))
        atC.loads += [(vC[:, :, :], tiles_of(U3, 1280, HD, HD))]
        atC.rows += [(qC[:, :, :, :].rearrange("p t h d -> p t (h d)"), lat(U3, 0, 512, 512)),
                      (kC[:, :, :], tiles_of(U3, 1024, HD, HD)),
                      (csC[:, :, :, :], lambda it: C["cs128"].rearrange("c (t p) h -> p c t h", p=P)),
                      (gC[:, 0, :], lambda it: bcast(A["c_q_g_2"][0])), (gC[:, 1, :], lambda it: bcast(A["c_k_g_2"][0]))]
        atC.norms = [(rC[:, 0:12], HD)]

        def shapeC(dve, link, it):
            q, k = qC[:, :, :, :].rearrange("p t h d -> p (t h) d"), kC[:, :, :]
            sq = tmpC[:, 0:1536].rearrange("p (m d) -> p m d", d=HD)
            link(nc.vector.tensor_tensor(sq[:, 0:8, :], q, q, ALU.mult))
            link(nc.vector.tensor_tensor(sq[:, 8:12, :], k, k, ALU.mult))
            nc.vector.tensor_reduce(rC[:, 0:12], sq, AX.X, ALU.add).then_inc(at_ss, 1)
            dve.wait_ge(at_rs, it + 1)
            for x, c, n, g in ((q, 0, 8, 0), (k, 8, 4, 1)):
                link(nc.vector.tensor_tensor(x, x, rows3(rC[:, c:c + n], HD), ALU.mult))
                link(nc.vector.tensor_tensor(x, x, cols3(gC[:, g, :], n), ALU.mult))
            cs = (csC[:, 0, :, :], csC[:, 1, :, :])
            rope(link, qC[:, :, :, :], 0, 64, cs, tmpC[:, :])
            rope(link, kC[:, 2:4, :].rearrange("p t (m d) -> p t m d", m=1), 0, 64, cs, tmpC[:, :])
        atC.shape_ops, atC.shape_n = shapeC, 18
        for t in range(2):
            atC.jobs.append(([qC[:, t, g, :] for g in range(4)], qCT[:, t, :, :].rearrange("p g n -> p (g n)"), SCALE))
        atC.jobs.append(([kC[:, t, :] for t in range(4)], kCT[:, :], 1.0))
        for g in range(4):
            for qt in range(2):
                atC.units.append(Unit([qCT[:, qt, g, :]], [kCT[:, :]], [vC[:, t, :] for t in range(4)], 512,
                                      oC[:, qt, g, :]))
        atC.saves.append((lambda it: O3[CTX:CTX + SEQ, bass.ds(it * 512, 512)].rearrange("(t p) n -> p t n", p=P),
                          oC[:, :, :, :].rearrange("p t h d -> p t (h d)")))
        atC.seal()

        atD = Attn("atD", 2)
        ar = Arena([SCR, AHI, ALO])
        atD.place_rows(ar)
        qD, kvD, peD = ar("qD", [P, 2, 4, 192]), ar("kvD", [P, 4, 4, 256]), ar("peD", [P, 4, 64])
        qDT, qPT = ar("qDT", [P, 2, 4, P]), ar("qPT", [64, 2, 4, P])
        kDT, kPT = ar("kDT", [P, 4, 512]), ar("kPT", [64, 512])
        oD, tmpD, csD = ar("oD", [P, 2, 4, HD]), ar("tmpD", [P, 1024]), ar("csD", [P, 2, 2, 32])
        DSC = 192 ** -0.5
        def kv_half(t, half):
            return (kvD[:, t, :, half * HD:(half + 1) * HD],
                    lambda it: KVB[t * P:(t + 1) * P, bass.ds(it * 1024, 1024)].rearrange("p (h d) -> p h d", h=4)[
                        :, :, half * HD:(half + 1) * HD])
        atD.loads += [kv_half(t, 1) for t in range(4)]
        atD.rows += [kv_half(t, 0) for t in range(4)] + \
                    [(qD[:, :, :, :].rearrange("p t h d -> p t (h d)"), lat(QB, 0, 768, 768)),
                      (peD[:, :, :], tiles_of(U3, 2304, 64, 0)),
                      (csD[:, :, :, :], lambda it: C["cs64"].rearrange("c (t p) h -> p c t h", p=P))]

        def shapeD(dve, link, it):
            cs = (csD[:, 0, :, :], csD[:, 1, :, :])
            rope(link, qD[:, :, :, :], HD, 32, cs, tmpD[:, :])
            rope(link, peD[:, 2:4, :].rearrange("p t (m d) -> p t m d", m=1), 0, 32, cs, tmpD[:, :])
        atD.shape_ops, atD.shape_n = shapeD, 12
        for t in range(2):
            atD.jobs.append(([qD[:, t, g, 0:HD] for g in range(4)], qDT[:, t, :, :].rearrange("p g n -> p (g n)"), DSC))
            atD.jobs.append(([qD[:, t, g, HD:192] for g in range(4)], qPT[:, t, :, :].rearrange("p g n -> p (g n)"), DSC))
        for g in range(4):
            atD.jobs.append(([kvD[:, t, g, 0:HD] for t in range(4)], kDT[:, g, :], 1.0))
        atD.jobs.append(([peD[:, t, :] for t in range(4)], kPT[:, :], 1.0))
        for g in range(4):
            for qt in range(2):
                atD.units.append(Unit([qDT[:, qt, g, :], qPT[:, qt, g, :]], [kDT[:, g, :], kPT[:, :]],
                                      [kvD[:, t, g, HD:256] for t in range(4)], 512, oD[:, qt, g, :]))
        atD.saves.append((lambda it: O3[CTX:CTX + SEQ, bass.ds(1024 + it * 512, 512)].rearrange("(t p) n -> p t n", p=P),
                          oD[:, :, :, :].rearrange("p t h d -> p t (h d)")))
        atD.seal()

        p2_in = [sem("p2_in0"), sem("p2_in1")]

        def p2_pool(pool):
            pool.wait_ge(at_saved, 64)
            for i, (tt, _, k0) in enumerate(p2.tts):
                if i >= 2:
                    pool.wait_ge(tr_done, p2.u0 + 3 * (i - 1))
                pool.dma_start(xn[:, i % 2, 0:1536], OB[tt * P:(tt + 1) * P, k0 * P:k0 * P + 1536])\
                    .then_inc(p2_in[i % 2], 16)

        def p2_dve(dve, i):
            dve.wait_ge(p2_in[i % 2], 16 * (i // 2 + 1))
            dve.sem_inc(xn_ready, 1)

        def gated(p, O, U, g0, norm, tag):
            gi, gx = sem(tag + "_gin"), [sem(tag + "_xin0"), sem(tag + "_xin1")]
            gs, gss, grs, gu = (sem(tag + n) for n in ("_silu", "_ss", "_rs", "_used"))
            sub = small[:, 48:56]

            def pool(pool):
                link = links["pool"]
                for i, (tt, _, _) in enumerate(p.tts):
                    if i >= 2:
                        pool.wait_ge(tr_done, p.u0 + 4 * (i - 1))
                    if i >= 1:
                        pool.wait_ge(gu, i)
                    pool.dma_start(xn[:, i % 2, :], tok(O, tt)).then_inc(gx[i % 2], 16)
                    pool.dma_start(gt2[:, :], U[tt * P:(tt + 1) * P, g0:g0 + DM]).then_inc(gi, 16)
                    if norm:
                        pool.wait_ge(gss, i + 1)
                        pow_half(pool, sub, sub, HD, link).then_inc(grs, 1)

            def act(act, i):
                act.wait_ge(gi, 16 * (i + 1))
                nc.scalar.activation(gt2[:, :], gt2[:, :], ACT.Silu).then_inc(gs, 1)

            def dve(dve, i, link):
                x = xn[:, i % 2, :]
                dve.wait_ge(gx[i % 2], 16 * (i // 2 + 1))
                if norm:
                    xa = x[:, 0:1024].rearrange("p (h d) -> p h d", h=8)
                    sq = aff[:, :, :, :].rearrange("p a b c -> p (a b) c")
                    link(nc.vector.tensor_tensor(sq, xa, xa, ALU.mult))
                    nc.vector.tensor_reduce(sub, sq, AX.X, ALU.add).then_inc(gss, 1)
                    dve.wait_ge(grs, i + 1)
                    link(nc.vector.tensor_tensor(xa, xa, rows3(sub, HD), ALU.mult))
                    link(nc.vector.tensor_tensor(xa, xa, cols3(subg[:, :], 8), ALU.mult))
                dve.wait_ge(gs, i + 1)
                ins = nc.vector.tensor_tensor(x, x, gt2[:, :], ALU.mult)
                ins.then_inc(xn_ready, 1)
                dve.wait_ge(xn_ready, p.x0 + i + 1)
                dve.sem_inc(gu, 1)
            return pool, act, dve

        g6_pool, g6_act, g6_dve = gated(p6, O2, U2, 4608, True, "g6")
        g9_pool, g9_act, g9_dve = gated(p9, O3, U3, 2368, False, "g9")

        p8_in, p8_ss, p8_rs = (sem(n) for n in ("p8_in", "p8_ss", "p8_rs"))
        lr = place("lr", [P, 4, 768], xn_at)
        gq, gk = place("gq", [P, 512], xn_at + 12288), place("gk", [P, 256], xn_at + 14336)
        lq = place("lq", [P, 4, 768], xn_at + 16384)
        p8q.src = lambda i: lr[:, 2 + i, 0:512]
        p8k.src = lambda i: lr[:, i, 512:768]

        def p8_pool(pool):
            wait_stored(pool, "in3")
            pool.wait_ge(pl_done, p7.u0 + len(p7.units))
            pool.dma_start(lr[:, 2:4, 0:512], U3[CTX:CTX + SEQ, 1536:2048].rearrange("(t p) n -> p t n", p=P))\
                .then_inc(p8_in, 16)
            pool.dma_start(lr[:, :, 512:768], U3[:, 2048:2304].rearrange("(t p) n -> p t n", p=P)).then_inc(p8_in, 16)
            pool.dma_start(gq[:, :], bcast(A["d_q_a_g_2"][0])).then_inc(p8_in, 16)
            pool.dma_start(gk[:, :], bcast(A["d_kv_a_g_2"][0])).then_inc(p8_in, 16)
            pool.wait_ge(p8_ss, 1)
            link = links["pool"]
            pow_half(pool, small[:, 56:58], small[:, 56:58], 512, link)
            pow_half(pool, small[:, 58:62], small[:, 58:62], 256, link).then_inc(p8_rs, 1)

        def p8_dve(dve):
            link = links["dve"]
            dve.wait_ge(p8_in, 64)
            q, k = lr[:, 2:4, 0:512], lr[:, :, 512:768]
            link(nc.vector.tensor_tensor(lq[:, 2:4, 0:512], q, q, ALU.mult))
            link(nc.vector.tensor_tensor(lq[:, :, 512:768], k, k, ALU.mult))
            link(nc.vector.tensor_reduce(small[:, 56:58], lq[:, 2:4, 0:512], AX.X, ALU.add))
            nc.vector.tensor_reduce(small[:, 58:62], lq[:, :, 512:768], AX.X, ALU.add).then_inc(p8_ss, 1)
            dve.wait_ge(p8_rs, 1)
            link(nc.vector.tensor_tensor(q, q, rows3(small[:, 56:58], 512), ALU.mult))
            link(nc.vector.tensor_tensor(k, k, rows3(small[:, 58:62], 256), ALU.mult))
            link(nc.vector.tensor_tensor(q, q, cols3(gq[:, :], 2), ALU.mult))
            link(nc.vector.tensor_tensor(k, k, cols3(gk[:, :], 4), ALU.mult))
            dve.sem_inc(xn_ready, 6)

        mf_in, mf_sum, mf_out = sem("mf_in"), sem("mf_sum"), sem("mf_out")
        mid_gain = place("mid_gain", [P, DM], xn_at + 16384)
        mid_in, mid_ss, mid_rs, mid_done = (sem(n) for n in ("mid_in", "mid_ss", "mid_rs", "mid_done"))
        vec_in, vec_link = sem("vec_in"), sem("vec_link")

        def mod_pool(pool, layer, upto):
            wait_stored(pool, upto)
            cols = slice(layer * 3 * DM, (layer + 1) * 3 * DM)
            pool.dma_start(mfr[:, :, :], MODP[:, cols].rearrange("r (p n) -> p r n", p=P)).then_inc(mf_in, 16)
            pool.dma_start(mfb[:, :], A["b_mod_2"][layer].rearrange("(p n) -> p n", p=P)).then_inc(mf_in, 16)
            pool.wait_ge(mf_sum, layer + 1)
            pool.dma_start(MODF[:, cols].rearrange("r (p n) -> p r n", p=P), mfo[:, :, :]).then_inc(mf_out, 16)
            pool.wait_ge(mf_out, 16 * (layer + 1))

        def mod_dve(dve, layer):
            dve.wait_ge(mf_in, 32 * (layer + 1))
            links["dve"](nc.vector.tensor_tensor(mfo[:, :, :], mfr[:, 0:2, :], mfr[:, 2:4, :], ALU.add))
            nc.vector.tensor_tensor(mfo[:, :, :], mfo[:, :, :], cols3(mfb[:, :], 2), ALU.add).then_inc(mf_sum, 1)

        def modfin_pool(pool):
            pool.wait_ge(pl_done, p4.u0 + len(p4.units))
            pool.wait_ge(sq_done, 17)
            pool.wait_ge(ht_done, 17)
            pool.dma_start(mid_gain[:, :], bcast(A["norm_final"])).then_inc(mid_in, 16)
            pool.dma_start(subg[:, :], bcast(A["a_sub_g_2"][0])).then_inc(mid_in, 16)
            vec_pool(pool, 0)
            pool.wait_ge(mid_ss, 2)
            link = links["pool"]
            pow_half(pool, small[:, 62:64], small[:, 62:64], DM, link).then_inc(mid_rs, 1)

        def vec_pool(pool, layer):
            o = layer * 3 * DM
            for r, (src, c) in enumerate(((0, DM), (0, 0), (1, DM), (1, 0))):
                pool.dma_start(vec[:, V_CTX + r, :], MODF[src, o + c:o + c + DM].rearrange("(k p) -> p k", p=P),
                               allow_slow_non_contiguous=True)\
                    .then_inc(vec_in, 16)
            pool.dma_start(vec[:, V_NG, :], A["norm_g_2"][layer].rearrange("(k p) -> p k", p=P),
                           allow_slow_non_contiguous=True).then_inc(vec_in, 16)

        def vec_dve(dve, layer):
            dve.wait_ge(vec_in, 80 * (layer + 1))
            for i, r in enumerate((V_CTX, V_X)):
                nc.vector.scalar_tensor_tensor(out=vec[:, r, :], in0=vec[:, r, :], scalar=1.0, in1=vec[:, V_NG, :],
                                               op0=ALU.add, op1=ALU.mult).then_inc(vec_link, 1)
            dve.wait_ge(vec_link, 2 * (layer + 1))

        def mid_act(act):
            wait_freed(act, "mlp")
            for tt in range(2):
                nc.scalar.activation(mid_junk[:, tt, :], XR[:, tt, :], ACT.Square,
                                     accum_out=small[:, 62 + tt:63 + tt]).then_inc(mid_ss, 1)
        mid_junk = place("mid_junk", [P, 2, DM], AHI[0])

        def mid_dve(dve):
            link = links["dve"]
            dve.wait_ge(mid_in, 32)
            link(nc.vector.tensor_scalar(subg[:, :], subg[:, :], 1.0 - LAM_INIT, None, ALU.mult))
            dve.wait_ge(mid_rs, 1)
            for tt in range(2):
                nc.vector.scalar_tensor_tensor(out=XR[:, tt, :], in0=XR[:, tt, :], scalar=small[:, 62 + tt:63 + tt],
                                               in1=mid_gain[:, :], op0=ALU.mult, op1=ALU.mult).then_inc(mid_done, 1)
            dve.wait_ge(mid_done, 2)

        gbc_in = sem("gbc_in")

        def gbc_pool(pool, layer, p):
            pool.wait_ge(pl_done, p.u0 + len(p.units))
            o = layer * 3 * DM + 2 * DM
            pool.dma_start(gbc_c[:, :], bcast(MODF[0, o:o + DM])).then_inc(gbc_in, 16)
            pool.dma_start(gbc_x[:, :], bcast(MODF[1, o:o + DM])).then_inc(gbc_in, 16)

        fin_in, fin_ss, fin_rs, fin_y, fin_out = (sem(n) for n in ("fin_in", "fin_ss", "fin_rs", "fin_y",
                                                                   "fin_out"))
        fin_gain = place("fin_gain", [P, DM], ALO[0])
        fin_junk = place("fin_junk", [P, 2, DM], AHI[0])

        x_in, cx_in = sem("x_in"), sem("cx_in")
        block = ctx.enter_context(nc.Block())

        @block.sync
        def _(sp):
            for tt in range(2):
                sp.dma_start(XR[:, tt, :], A["x"][0, tt * P:(tt + 1) * P, :]).then_inc(x_in, 16)
            for name in ("qkv0", "qkv", "gates", "cmp1"):
                sp_stream(sp, stages[name])
            wait_stored(sp, "qkv")
            wait_freed(sp, "gates")
            sp.wait_ge(nsa_out, 16)
            sp.wait_ge(cmp_out, 32)
            sp.wait_ge(bt_out, 16)
            at1.sp(sp)
            for name in ("branch", "out1", "mlp", "in2", "in2_end"):
                sp_stream(sp, stages[name])
            wait_stored(sp, "in2_end")
            wait_freed(sp, "in2_end")
            atA.sp(sp)
            atB.sp(sp)
            for name in ("out2", "in3", "qb", "kvb"):
                sp_stream(sp, stages[name])
            wait_stored(sp, "kvb")
            wait_freed(sp, "kvb")
            atC.sp(sp)
            atD.sp(sp)
            sp_stream(sp, stages["out3"])

        @block.gpsimd
        def _(pool):
            links["pool"].eng = pool
            setup_gpsimd(pool)
            n1.pool(pool)
            setup_brev(pool)
            for name in ("qkv0", "qkv"):
                pool_stream(pool, stages[name])
            cmp_pool_loads(pool)
            pool_stream(pool, stages["gates"])
            cmp_pool_store(pool)
            at1.pool(pool)
            p2_pool(pool)
            wait_stored(pool, "gates")
            pool.wait_ge(pl_done, p2.u0 + len(p2.units))
            pool_stream(pool, stages["branch"])
            mod_pool(pool, 0, "mod1")
            n4.pool(pool)
            pool.wait_ge(pl_done, p3.u0 + len(p3.units))
            for tt in range(2):
                pool.dma_start(CX[:, tt, :], A["ctx_2"][0, tt * P:(tt + 1) * P, :]).then_inc(cx_in, 16)
            pool_stream(pool, stages["mlp"])
            modfin_pool(pool)
            n5.pool(pool)
            pool_stream(pool, stages["in2"])
            pool_stream(pool, stages["in2_end"])
            atA.pool(pool)
            atB.pool(pool)
            g6_pool(pool)
            gbc_pool(pool, 0, p6)
            mod_pool(pool, 1, "modB")
            wait_freed(pool, "out2")
            pool.wait_ge(gres_tmp, 16)
            vec_pool(pool, 1)
            n7.pool(pool)
            pool_stream(pool, stages["in3"])
            p8_pool(pool)
            pool_stream(pool, stages["qb"])
            pool_stream(pool, stages["kvb"])
            atC.pool(pool)
            atD.pool(pool)
            g9_pool(pool)
            gbc_pool(pool, 1, p9)
            wait_freed(pool, "out3")
            pool.dma_start(fin_gain[:, :], bcast(A["final_g_2"])).then_inc(fin_in, 16)
            pool.wait_ge(fin_ss, 2)
            link = links["pool"]
            pow_half(pool, small[:, 46:48], small[:, 46:48], DM, link).then_inc(fin_rs, 1)
            for tt in range(2):
                pool.wait_ge(fin_y, tt + 1)
                pool.dma_start(out[0, tt * P:(tt + 1) * P, :], XR[:, tt, :]).then_inc(fin_out, 16)
            pool.wait_ge(fin_out, 32)

        @block.tensor
        def _(pe):
            setup_pe(pe)
            p1.pe(pe)
            p1.finish(pe)
            for name in ("qkv0", "qkv", "gates"):
                pe_stream(pe, stages[name])
            cmp_pe_prep(pe)
            pe.wait_ge(cmp_hi, 1)
            pe_stream(pe, stages["cmp1"])
            cmp_pe(pe)
            at1.pe(pe)
            p2.pe(pe)
            p2.finish(pe)
            pe_stream(pe, stages["branch"])
            p3.pe(pe)
            p3.finish(pe)
            pe_stream(pe, stages["out1"])
            p4.pe(pe)
            p4.finish(pe)
            pe_stream(pe, stages["mlp"])
            p5.pe(pe)
            p5.finish(pe)
            pe_stream(pe, stages["in2"])
            pe_stream(pe, stages["in2_end"])
            atA.pe(pe)
            atB.pe(pe)
            p6.pe(pe)
            p6.finish(pe)
            pe_stream(pe, stages["out2"])
            p7.pe(pe)
            p7.finish(pe)
            pe_stream(pe, stages["in3"])
            p8q.pe(pe)
            p8k.pe(pe)
            p8q.finish(pe)
            p8k.finish(pe)
            pe_stream(pe, stages["qb"])
            pe_stream(pe, stages["kvb"])
            atC.pe(pe)
            atD.pe(pe)
            p9.pe(pe)
            p9.finish(pe)
            pe_stream(pe, stages["out3"])

        @block.scalar
        def _(act):
            setup_act_loads(act)
            act.wait_ge(x_in, 32)
            setup_act(act)
            p1.act(act, n1.act)
            setup_bias_tiles(act)
            for name in ("qkv0", "qkv", "gates", "cmp1"):
                act_stream(act, stages[name])
            cmp_act(act)
            at1.act(act)
            p2.act(act)
            act_stream(act, stages["branch"])
            p3.act(act)
            act_stream(act, stages["out1"])
            p4.act(act, n4.act)
            act_stream(act, stages["mlp"])
            mid_act(act)
            act.wait_ge(mid_done, 2)
            act.wait_ge(cx_in, 32)
            act.wait_ge(vec_link, 2)
            p5.act(act, n5.act)
            act_stream(act, stages["in2"])
            act_stream(act, stages["in2_end"])
            atA.act(act)
            atB.act(act)
            p6.act(act, g6_act)
            act_stream(act, stages["out2"])
            act.wait_ge(gres_tmp, 16)
            act.wait_ge(vec_link, 4)
            p7.act(act, n7.act)
            act_stream(act, stages["in3"])
            p8q.act(act)
            p8k.act(act)
            act_stream(act, stages["qb"])
            act_stream(act, stages["kvb"])
            atC.act(act)
            atD.act(act)
            p9.act(act, g9_act)
            act_stream(act, stages["out3"])
            act.wait_ge(gres_tmp, 24)
            for tt in range(2):
                nc.scalar.activation(fin_junk[:, tt, :], XR[:, tt, :], ACT.Square,
                                     accum_out=small[:, 46 + tt:47 + tt]).then_inc(fin_ss, 1)

        @block.vector
        def _(dve):
            links["dve"].eng = dve
            setup_vector(dve)
            p1.dve(dve, n1.dve)
            for name in ("qkv0", "qkv", "gates"):
                dve_stream(dve, stages[name])
            cmp_dve_prep(dve)
            dve_stream(dve, stages["cmp1"])
            cmp_dve_gelu(dve)
            at1.dve(dve)
            p2.dve(dve, p2_dve)
            dve_stream(dve, stages["branch"])
            dve.sem_inc(xn_ready, 2)
            p3.dve(dve)
            mod_dve(dve, 0)
            dve_stream(dve, stages["out1"])
            p4.dve(dve, n4.dve)
            dve_stream(dve, stages["mlp"])
            mid_dve(dve)
            vec_dve(dve, 0)
            p5.dve(dve, n5.dve)
            dve_stream(dve, stages["in2"])
            dve_stream(dve, stages["in2_end"])
            atA.dve(dve)
            atB.dve(dve)
            link6 = links["dve"]
            p6.dve(dve, lambda e, i: g6_dve(e, i, link6))
            dve.wait_ge(gbc_in, 32)
            mod_dve(dve, 1)
            dve_stream(dve, stages["out2"])
            vec_dve(dve, 1)
            p7.dve(dve, n7.dve)
            dve_stream(dve, stages["in3"])
            p8_dve(dve)
            p8q.dve(dve)
            p8k.dve(dve)
            dve_stream(dve, stages["qb"])
            dve_stream(dve, stages["kvb"])
            atC.dve(dve)
            atD.dve(dve)
            link9 = links["dve"]
            p9.dve(dve, lambda e, i: g9_dve(e, i, link9))
            dve.wait_ge(gbc_in, 64)
            dve_stream(dve, stages["out3"])
            dve.wait_ge(fin_in, 16)
            dve.wait_ge(fin_rs, 1)
            for tt in range(2):
                nc.vector.scalar_tensor_tensor(out=XR[:, tt, :], in0=XR[:, tt, :], scalar=small[:, 46 + tt:47 + tt],
                                               in1=fin_gain[:, :], op0=ALU.mult, op1=ALU.mult).then_inc(fin_y, 1)


def constants():
    dist = 255 - np.arange(G)
    n = np.maximum(dist, 0)
    large = np.minimum(16 + (np.log(np.maximum(n, 1) / 16.0) / np.log(8.0) * 16).astype(np.int64), BUCKETS - 1)
    bucket = np.where(n < 16, n, large)
    onehot = (np.arange(BUCKETS)[:, None] == bucket[None]).astype(np.float32)
    bmask = np.zeros((24, G), np.float32)
    bmask[:, dist < 0] = NEG
    bmask[8:16, dist >= 128] = NEG
    valid = (np.arange(P) >= 31).astype(np.float32)[:, None]
    q, k = np.arange(SEQ)[:, None], np.arange(SEQ)[None]
    band = np.where(np.abs(k - q) <= 128, 0.0, NEG).astype(np.float32)

    def angles(dim):
        pos = np.arange(SEQ)
        r, c = (pos // 64).astype(np.float32), (pos % 64).astype(np.float32)
        f = dim // 4
        inv = (np.float32(10000.0) ** (-np.arange(f, dtype=np.float32) / np.float32(f))).astype(np.float32)
        a = np.concatenate([r[:, None] * inv[None], c[:, None] * inv[None]], -1)
        return np.stack([np.cos(a), np.sin(a)]).astype(np.float32)
    return dict(onehot=onehot, bmask=bmask, valid=valid, band=band, cs128=angles(128), cs64=angles(64))


_INS = ["x", "w_in", "cmp_pos", "cmp_w1", "cmp_w2", "swa_sinks", "w_branch", "w_out", "w_mlp_in", "w_mlp_out",
        "norm_mix", "norm_mlp", "norm_final", "rel_bias", "c_2", "ctx_2", "c_ctx_2", "w_mod_2", "b_mod_2",
        "norm_g_2", "w_o_2", "final_g_2", "e_w_in_2", "a_lam_q1_2", "a_lam_k1_2", "a_lam_q2_2", "a_lam_k2_2",
        "a_sub_g_2", "b_sink_2", "o_w_in_2", "c_q_g_2", "c_k_g_2", "d_q_a_g_2", "d_kv_a_g_2", "d_w_q_b_2",
        "d_w_kv_b_2"]


def kernel(**inputs):
    import concourse.bacc as _bacc
    from concourse.bass_utils import run_bass_kernel_spmd as _run

    nc = _bacc.Bacc("TRN2", target_bir_lowering=False, num_devices=1)
    arrays, given, consts = {}, {}, {}
    for group_, names, values in (("in", _INS, inputs), ("const", None, constants())):
        for name in names or values:
            a = np.ascontiguousarray(values[name])
            arrays[f"{group_}_{name}"] = a
            ap = nc.dram_tensor(f"{group_}_{name}", a.shape, mybir.dt.from_np(a.dtype), kind="ExternalInput").ap()
            (given if group_ == "in" else consts)[name] = ap
    out = nc.dram_tensor("out", (1, SEQ, DM), F32, kind="ExternalOutput").ap()
    two_blocks(nc, given, consts, out)
    r = _run(nc, [arrays], core_ids=[0])
    return r.results[0]["out"]
```

```python
from contextlib import ExitStack

import numpy as np

import concourse.bass as bass
from concourse import mybir

F32 = mybir.dt.float32
F32R = mybir.dt.float32r
ACT = mybir.ActivationFunctionType
ALU = mybir.AluOpType
AX = mybir.AxisListType

P = 128
DM = 2048
KT = DM // P
SEQ = 256
CTX = 256
HD = 128
G = 512
CH = 1024
QKV1 = 5656
GATE0 = 2560
NCMP = (SEQ - 32) // 16 + 1
NM = 3 * DM // P
RAWS, SPLITS = 8, 4
NEG = -1e30
EPS = 1e-6
TINY = 1e-30
GELU_C = float(np.sqrt(2.0 / np.pi))
SCALE = HD ** -0.5
BUCKETS = 32
LAM_INIT = 0.2


class Step:

    def __init__(self, chunks, tiles, lhs, evac, width=G, wtiles=2):
        self.chunks, self.tiles, self.lhs, self.evac = chunks, tiles, lhs, evac
        self.width, self.wtiles, self.pair = width, wtiles, None

    def beside(self, other):
        self.pair = other
        return self

    def groups(self):
        return [self] + ([self.pair] if self.pair else [])

    def order(self):
        return [(g, c) for c in range(len(self.chunks)) for g in self.groups()]


class Stage:

    def __init__(self, steps, times=1):
        self.steps, self.times = steps, times


def count_stages(stages):
    total = {("fill", 4): 1, ("put", 4): 1, "relu2": 1}
    for st in stages:
        st.base = dict(total)
        local = {}
        for s in st.steps:
            for g in s.groups():
                g.no = {}
            for g, c in s.order():
                g.no[c] = local.get("chunk", 0)
                local["chunk"] = g.no[c] + 1
        for s in [g for s in st.steps for g in s.groups()]:
            s.fill, s.put = {}, {}
            s.done = {}
            for bank, _ in s.tiles[:-1]:
                s.done[bank] = local.get(("done", bank), 0)
                local[("done", bank)] = s.done[bank] + 1
            for bank, _ in s.tiles:
                s.fill[bank] = local.get(("fill", bank), 0)
                local[("fill", bank)] = s.fill[bank] + 1
                if s.evac["kind"] == "store":
                    s.put[bank] = local.get(("put", bank), 0)
                    local[("put", bank)] = s.put[bank] + 1
            for kind in ("relu2", "branch"):
                if s.evac["kind"] == kind:
                    s.nth = local.get(kind, 0)
                    local[kind] = s.nth + 1
        st.per = local
        assert st.times == 1 or local["chunk"] % RAWS == 0
        for k, v in local.items():
            total[k] = total.get(k, 0) + v * st.times
    return total


def at(st, kind, local, it):
    return st.base.get(kind, 0) + local + (st.per.get(kind, 0) * it if st.times > 1 else 0)


class Unit:

    def __init__(self, q, k, v, keys, out, bias=None, sink=None, coeff=None, add=False):
        self.q, self.k, self.v, self.keys, self.out = q, k, v, keys, out
        self.bias, self.sink, self.coeff, self.add = bias, sink, coeff, add


def two_blocks(nc, A, C, out):
    ctx = ExitStack()
    with ctx:
        here = [nc.sbuf_base + (-nc.sbuf_base) % 64]
        fence = ctx.enter_context(nc.sbuf_tensor("fence", [P, (nc.sbuf_bytes_remaining - 256) // 4], F32))

        def place(name, shape, offset, dt=F32):
            return nc.alloc_sbuf_tensor_at(name, shape, dt, offset=offset)

        def take(n):
            o = here[0]
            here[0] += n + (-n) % 32
            assert here[0] <= nc.sbuf_usable_end, here
            return o

        def sb(name, shape, dt=F32):
            return place(name, shape, take(4 * int(np.prod(shape[1:]))), dt)

        def sem(name):
            return ctx.enter_context(nc.semaphore(name))

        def dram(name, shape):
            return nc.dram_tensor(name, shape, F32, kind="Internal").ap()

        raw = sb("raw", [P, RAWS, CH])
        w_hi = sb("w_hi", [P, SPLITS, CH], F32R)
        w_lo = sb("w_lo", [P, SPLITS, CH], F32R)
        act_hi_at, act_lo_at = take(32768), take(32768)
        a_hi = place("a_hi", [P, 8192], act_hi_at, F32R)
        a_lo = place("a_lo", [P, 8192], act_lo_at, F32R)
        XR = sb("XR", [P, 2, DM])
        CX = sb("CX", [P, 2, DM])
        MIX = CX
        stage = sb("stage", [P, 4, G])
        ident = sb("ident", [P, P])
        small = sb("small", [P, 64])
        half = sb("half", [P, 2])

        class Arena:

            def __init__(self, regions):
                self.regions = [list(r) for r in regions]

            def __call__(self, name, shape, dt=F32):
                n = 4 * int(np.prod(shape[1:]))
                n += (-n) % 32
                for r in self.regions:
                    if r[0] + n <= r[1]:
                        r[0] += n
                        return place(name, shape, r[0] - n, dt)
                raise AssertionError((name, n, self.regions))

        AHI, ALO = (act_hi_at, act_hi_at + 32768), (act_lo_at, act_lo_at + 32768)

        acc = ctx.enter_context(nc.psum_tensor("acc", [P, 8, G], F32))

        U1 = dram("U1", (SEQ, QKV1))
        AG = dram("AG", (SEQ, 24))
        GT = dram("GT", (SEQ, 3 * DM))
        OB = dram("OB", (SEQ, 3 * 1024))
        MODP = dram("MODP", (4, 2 * 3 * DM))
        BREV = dram("BREV", (24, G))
        BROW = dram("BROW", (24, P, G))
        CMPK = dram("CMPK", (HD, 2 * NCMP))
        CMPV = dram("CMPV", (2 * NCMP, HD))
        MODF = dram("MODF", (2, 2 * 3 * DM))
        U2 = dram("U2", (CTX + SEQ, 6656))
        O2 = dram("O2", (CTX + SEQ, DM))
        U3 = dram("U3", (CTX + SEQ, 4416))
        QB = dram("QB", (CTX + SEQ, 1536))
        KVB = dram("KVB", (CTX + SEQ, DM))
        O3 = dram("O3", (CTX + SEQ, DM))

        def tok(ap, tt):
            return ap[tt * P:(tt + 1) * P, :]

        def lhs_act(T, off=0):
            def f(part, kt, tt):
                o = off + kt * T + tt * P
                return (a_hi, a_lo)[part][:, o:o + P]
            return f

        MV = sb("MV", [P, KT * 4 + P], F32R)

        def lhs_mod(part, kt, tt):
            return MV[:, kt * 4:kt * 4 + P]

        def wcols(W, k0, n0, width=G, nk=2):
            def f(it):
                c = n0(it) if callable(n0) else n0
                kk = k0(it) if callable(k0) else k0
                return W.rearrange("(k p) n -> p k n", p=P)[:, bass.ds(kk, nk), bass.ds(c, width)]
            return f

        def group(W, n0, tiles, lhs, evac, kts=KT, k0=0, width=G):
            ch = [wcols(W, (lambda it, j=j: (k0(it) if callable(k0) else k0) + j), n0, width)
                  for j in range(0, kts, 2)]
            return Step(ch, tiles, lhs, evac, width)

        def store(dst, func=ACT.Copy, scale=1.0, rows=P):
            return dict(kind="store", dst=dst, func=func, scale=scale, rows=rows)

        T2 = [(0, 0), (1, 1)]
        T4 = [(0, 0), (1, 1), (2, 2), (3, 3)]
        TX = [(2, 2), (3, 3)]

        def to(D, n0, t0=0):
            return lambda it, tt, w: D[tt * P:(tt + 1) * P, bass.ds(n0(it) if callable(n0) else n0, w)]

        x256, x512 = lhs_act(256), lhs_act(512)
        win = A["w_in"][0]
        stages = {}
        GQ = -(-QKV1 // (12 * 8)) * 8
        gg = GATE0 // GQ
        assert gg == 5 and GATE0 + 24 <= (gg + 1) * GQ and QKV1 > 11 * GQ
        stages["qkv0"] = Stage([group(win, gg * GQ, T2, x256, dict(store(to(U1, gg * GQ)), gates=GATE0 - gg * GQ),
                                      width=GQ)])
        stages["qkv_end"] = Stage([group(win, 11 * GQ, T2, x256, store(to(U1, 11 * GQ)), width=QKV1 - 11 * GQ)])
        stages["qkv"] = Stage([group(win, lambda it, j=j: (it * 6 + j) * GQ, T2, x256,
                                     store(to(U1, lambda it, j=j: (it * 6 + j) * GQ)), width=GQ)
                               for j in range(5)], 2)
        stages["gates"] = Stage([group(win, lambda it, j=j: QKV1 + (it * 4 + j) * G, T2, x256,
                                       store(to(GT, lambda it, j=j: (it * 4 + j) * G), ACT.Tanh, 0.5))
                                 for j in range(4)], 3)
        def lhs_cmp(which):
            def f(part, kt, tt):
                o = which * 1024 + kt * 30
                return (a_hi, a_lo)[part][:, 4096 + o:4096 + o + P]
            return f

        def w1chunk(which, c):
            return lambda it: A["cmp_w1"][0, which].rearrange("(k p) n -> p k n", p=P)[:, c * 4:c * 4 + 4, :]

        stages["cmp1"] = Stage([Step([w1chunk(w, c) for c in range(8)], [(w, 0)], lhs_cmp(w),
                                     dict(kind="hold"), 256, 4) for w in range(2)])

        def branch_steps():
            steps = []
            for n in range(4):
                for m in range(3):
                    steps.append(group(A["w_branch"][0, m], n * G, T2, (lambda part, kt, tt, m=m:
                                 x256(part, m * 8 + kt, tt)), dict(kind="branch", n=n, m=m), kts=8))
            return steps
        stages["branch"] = Stage(branch_steps())
        stages["out1"] = Stage([group(A["w_out"][0], n * G, T2, x256,
                                      dict(kind="resid", n=n, scale=0.5)) for n in range(4)])

        h256 = lhs_act(256, 4096)

        def mod_steps(layer, n, first=0):
            def col(r):
                return lambda it: (first + it * n + r) * G
            return [group(A["w_mod_2"][layer], col(r), [(4, 0)], lhs_mod,
                          store(lambda it, tt, w, r=r: MODP[:, bass.ds(layer * 3 * DM + col(r)(it), w)], rows=4))
                    for r in range(n)]
        stages["modA"] = Stage(mod_steps(1, 2), 4)
        stages["modB"] = Stage(mod_steps(1, 2, 8), 2)

        def mlp_steps():
            ins = [group(A["w_mlp_in"][0], lambda it, j=j: it * DM + j * G, T2, x256,
                         dict(kind="relu2", j=j)) for j in range(4)]
            outs = [group(A["w_mlp_out"][0], n * G, T2, h256, dict(kind="resid", n=n, scale=1.0),
                          k0=lambda it: it * KT) for n in range(4)]
            for s_, m in zip(ins[1:], mod_steps(0, 3)):
                s_.beside(m)
            return ins + outs
        stages["mlp"] = Stage(mlp_steps(), 4)
        ew = A["e_w_in_2"][0]
        stages["in2"] = Stage([group(ew, lambda it, j=j: (it * 3 + j) * G, T4, x512,
                                     store(to(U2, lambda it, j=j: (it * 3 + j) * G))) for j in range(3)], 3)
        stages["in2_end"] = Stage([group(ew, n * G, T4, x512, store(to(U2, n * G), ACT.Silu)) for n in range(9, 13)])
        stages["out2"] = Stage([group(A["w_o_2"][0], n * G, T4, x512, dict(kind="gresid", n=n))
                                for n in range(4)])
        ow = A["o_w_in_2"][0]
        cols3 = [(0, TX, G), (G, TX, G), (2 * G, T4, G), (3 * G, TX, G), (4 * G, T4, 320)] + \
                [(2368 + j * G, TX, G) for j in range(4)]
        in3 = [group(ow, c, tl, x512, store(to(U3, c), ACT.Silu if c >= 2368 else ACT.Copy), width=w)
               for c, tl, w in cols3]
        stages["in3_low"], stages["in3"], stages["in3_gates"] = Stage(in3[3:5]), Stage(in3[0:3]), Stage(in3[5:])
        q4 = lhs_act(512)
        kv2 = lhs_act(512, 2048)
        stages["qb"] = Stage([group(A["d_w_q_b_2"][0], n * G, TX, q4, store(to(QB, n * G)), kts=4)
                              for n in range(3)])
        stages["kvb"] = Stage([Step([wcols(A["d_w_kv_b_2"][0], 0, n * G, G, 2)], T4, kv2,
                                    store(to(KVB, n * G)), G, 2) for n in range(4)])
        stages["out3"] = Stage([group(A["w_o_2"][1], n * G, TX, x512, dict(kind="gresid", n=n))
                                for n in range(4)])
        order = ["qkv0", "qkv", "qkv_end", "gates", "cmp1", "branch", "out1", "mlp", "in2", "in2_end", "modA", "modB",
                 "out2", "in3_low", "in3", "in3_gates", "qb", "kvb", "out3"]
        for name in order:
            stages[name].name = name
            stages[name].next = stages[name].split = None
        for run in (("qkv0", "qkv", "qkv_end", "gates", "cmp1"), ("branch", "out1", "mlp", "in2", "in2_end"),
                    ("out2", "in3_low", "in3", "in3_gates", "qb", "kvb")):
            for a, b in zip(run, run[1:]):
                stages[a].next, stages[b].split = stages[b], True
        totals = count_stages([stages[n] for n in order])

        held = sem("held")
        setup_gp = sem("setup_gp")
        landed = [sem(f"landed{i}") for i in range(RAWS)]
        hi_ready, lo_ready = sem("hi_ready"), sem("lo_ready")
        w_used = sem("w_used")
        acc_done = [sem(f"acc_done{b}") for b in range(3)]
        acc_free = [sem(f"acc_free{b}") for b in range(5)]
        stored = [sem(f"stored{b}") for b in range(5)]
        mod_put = sem("mod_put")
        stage_bufs = [stage[:, b, :] for b in range(4)] + [sb("stage_mod", [4, G])[:, :]]
        nsa_g = sb("nsa_g", [P, 2, 24])
        nsa_ready, nsa_out = sem("nsa_ready"), sem("nsa_out")
        mfr, mfb, mfo = sb("mfr", [P, 4, NM]), sb("mfb", [P, NM]), sb("mfo", [P, 2, NM])
        vec = sb("vec", [P, 8, KT])
        subg = sb("subg", [P, 1])
        scr_at = here[0]
        SCR = (scr_at, nc.sbuf_usable_end - 64)
        relu_done, sq_done, ht_done, hh_done, hl_done = (sem("relu_done"), sem("sq_done"), sem("ht_done"),
                                                         sem("hh_done"), sem("hl_done"))
        gate_in = [sem(f"gate_in{i}") for i in range(2)]
        branch_tmp, gres_tmp = sem("branch_tmp"), sem("gres_tmp")

        ar = Arena([SCR])
        relu_t = ar("relu_t", [P, 2, G])
        gate_t = ar("gate_t", [P, 2, 2, G])
        prod_t = ar("prod_t", [P, 2, G])
        gbc_x, gbc_c = place("gbc_x", [P, DM], SCR[0] + 16384), place("gbc_c", [P, DM], SCR[0] + 24576)
        prod_g = place("prod_g", [P, 4, G], SCR[0])

        def wait_done(eng, st, s, bank, it):
            if bank in s.done:
                eng.wait_ge(acc_done[bank], at(st, ("done", bank), s.done[bank] + 1, it))
            else:
                eng.wait_ge(w_used, at(st, "chunk", s.no[len(s.chunks) - 1] + 1, it))

        def hold(eng, s, value):
            eng.wait_ge(s, value)
            if not isinstance(value, int):
                eng.sem_inc(held, 1)

        def passes(eng, st, body):
            if st.times > 1:
                with eng.Fori(0, st.times) as it:
                    body(it)
            else:
                body(0)

        def chunk_no(st, s, c, it):
            n = at(st, "chunk", s.no[c], 0)
            return n, (st.per["chunk"] * it if st.times > 1 else 0)

        def sp_chunks(sp, st, s, it):
            for g, c in s.order():
                n, more = chunk_no(st, g, c, it)
                if n >= RAWS:
                    sp.wait_ge(lo_ready, n - RAWS + 1 + more)
                dst = raw[:, n % RAWS, 0:g.wtiles * g.width].rearrange("p (k n) -> p k n", k=g.wtiles)
                sp.dma_start(dst, g.chunks[c](it)).then_inc(landed[n % RAWS], 16)

        def sp_stream(sp, st):
            passes(sp, st, lambda it: [sp_chunks(sp, st, s, it) for s in st.steps])

        def split_hi(act, st, s, c, it):
            n, more = chunk_no(st, s, c, it)
            size = s.wtiles * s.width
            act.wait_ge(landed[n % RAWS], 16 * (n // RAWS + 1) + (16 * (st.per["chunk"] // RAWS) * it
                                                                  if st.times > 1 else 0))
            if n >= SPLITS:
                act.wait_ge(w_used, n - SPLITS + 1 + more)
            nc.scalar.activation(w_hi[:, n % SPLITS, 0:size], raw[:, n % RAWS, 0:size], ACT.Copy)\
              .then_inc(hi_ready, 1)

        def split_lo(dve, st, s, c, it):
            n, more = chunk_no(st, s, c, it)
            size = s.wtiles * s.width
            dve.wait_ge(hi_ready, n + 1 + more)
            nc.vector.tensor_tensor(w_lo[:, n % SPLITS, 0:size], raw[:, n % RAWS, 0:size],
                                    w_hi[:, n % SPLITS, 0:size].bitcast(F32), ALU.subtract)\
              .then_inc(lo_ready, 1)

        def psum_bank(st, bank):
            return 0 if st.name in ("modA", "modB") else bank

        def pe_chunk(pe, st, s, c, it):
            n, more = chunk_no(st, s, c, it)
            pe.wait_ge(lo_ready, n + 1 + more)
            for bank, tt in s.tiles:
                if c == 0:
                    f = at(st, ("fill", bank), s.fill[bank], it)
                    if not (isinstance(f, int) and f == 0):
                        pe.wait_ge(acc_free[bank], f)
                o = acc[:, psum_bank(st, bank), 0:s.width]
                for k in range(s.wtiles):
                    kt = c * s.wtiles + k
                    wh = w_hi[:, n % SPLITS, k * s.width:(k + 1) * s.width]
                    wl = w_lo[:, n % SPLITS, k * s.width:(k + 1) * s.width]
                    first = kt == 0
                    end = kt == len(s.chunks) * s.wtiles - 1
                    nc.tensor.matmul(o, s.lhs(0, kt, tt), wh, start=first, stop=False)
                    if s.lhs is lhs_mod:
                        last = nc.tensor.matmul(o, s.lhs(0, kt, tt), wl, start=False, stop=end)
                    else:
                        nc.tensor.matmul(o, s.lhs(0, kt, tt), wl, start=False, stop=False)
                        last = nc.tensor.matmul(o, s.lhs(1, kt, tt), wh, start=False, stop=end)
                if end and bank in s.done:
                    last.then_inc(acc_done[bank], 1)
            last.then_inc(w_used, 1)

        def pe_stream(pe, st):
            def body(it):
                prev = None
                for s in st.steps:
                    for g, c in s.order():
                        if st.name == "mlp" and g.evac["kind"] == "resid" and g.evac["n"] == 0 and c in (0, 6):
                            pe.wait_ge(hl_done, at(st, "relu2", 3 if c == 0 else 4, it))
                        pe_chunk(pe, st, g, c, it)
                        if c == 3 and g is s and prev is not None and prev.evac["kind"] == "relu2":
                            pe_hidden(pe, st, prev, it)
                    prev = s
            passes(pe, st, body)

        def pe_hidden(pe, st, s, it):
            r = at(st, "relu2", s.nth, it)
            pe.wait_ge(sq_done, r + 1)
            if not (isinstance(r, int) and r == 0):
                pe.wait_ge(hl_done, r)
            for tt in range(2):
                for j in range(4):
                    last = nc.tensor.transpose(acc[:, 6 + tt, j * P:(j + 1) * P],
                                               relu_t[:, tt, j * P:(j + 1) * P], ident[:, :])
            last.then_inc(ht_done, 1)

        def hid(t, s, tt):
            o = 4096 + s.evac["j"] * 4 * 256
            return t[:, o:o + 1024].rearrange("p (j t) -> p j t", j=4)[:, :, tt * P:(tt + 1) * P]

        def act_evac(act, st, s, it):
            e = s.evac
            for bank, tt in s.tiles:
                f = at(st, ("fill", bank), s.fill[bank], it)
                if e["kind"] == "store":
                    wait_done(act, st, s, bank, it)
                    p = at(st, ("put", bank), s.put[bank], it)
                    if bank == 4:
                        act.wait_ge(mod_put, p)
                    elif not (isinstance(p, int) and p == 0):
                        act.wait_ge(stored[bank], 16 * p)
                    r = e["rows"]
                    if e.get("gates"):
                        c0 = e["gates"]
                        nc.scalar.activation(nsa_g[:, tt, :], acc[:, bank, c0:c0 + 24], ACT.Tanh, scale=0.5)\
                          .then_inc(nsa_ready, 1)
                    nc.scalar.activation(stage_bufs[bank][0:r, 0:s.width], acc[0:r, psum_bank(st, bank), 0:s.width],
                                         e["func"], scale=e["scale"]).then_inc(acc_free[bank], 1)
                elif e["kind"] == "relu2":
                    wait_done(act, st, s, bank, it)
                    if tt == 0:
                        r = at(st, "relu2", s.nth, it)
                        if not (isinstance(r, int) and r == 0):
                            act.wait_ge(ht_done, r)
                    nc.scalar.activation(relu_t[:, tt, :], acc[:, bank, :], ACT.Relu)\
                      .then_inc(acc_free[bank], 1)

        def act_hidden(act, st, s, it):
            act.wait_ge(ht_done, at(st, "relu2", s.nth, it) + 1)
            for tt in range(2):
                last = nc.scalar.activation(hid(a_hi, s, tt), acc[:, 6 + tt, :].rearrange("p (j t) -> p j t", j=4),
                                            ACT.Copy)
            last.then_inc(hh_done, 1)

        def dve_hidden(dve, st, s, it):
            dve.wait_ge(hh_done, at(st, "relu2", s.nth, it) + 1)
            for tt in range(2):
                last = nc.vector.tensor_tensor(hid(a_lo, s, tt), acc[:, 6 + tt, :].rearrange("p (j t) -> p j t", j=4),
                                               hid(a_hi, s, tt).bitcast(F32), ALU.subtract)
            last.then_inc(hl_done, 1)

        def dve_evac(dve, st, s, it):
            e = s.evac
            if e["kind"] not in ("resid", "gresid", "branch"):
                return
            for bank, tt in s.tiles:
                f = at(st, ("fill", bank), s.fill[bank], it)
                wait_done(dve, st, s, bank, it)
                n = e.get("n", 0)
                if e["kind"] == "resid":
                    x = XR[:, tt, n * G:(n + 1) * G]
                    nc.vector.scalar_tensor_tensor(out=x, in0=acc[:, bank, :], scalar=e["scale"], in1=x,
                                                   op0=ALU.mult, op1=ALU.add).then_inc(acc_free[bank], 1)
                elif e["kind"] == "gresid":
                    x = (CX[:, tt, n * G:(n + 1) * G] if tt < 2 else XR[:, tt - 2, n * G:(n + 1) * G])
                    g = (gbc_c if tt < 2 else gbc_x)[:, n * G:(n + 1) * G]
                    nc.vector.tensor_tensor(prod_g[:, tt, :], acc[:, bank, :], g, ALU.mult)\
                      .then_inc(acc_free[bank], 1)
                    dve.wait_ge(acc_free[bank], f + 1)
                    nc.vector.tensor_tensor(x, x, prod_g[:, tt, :], ALU.add).then_inc(gres_tmp, 1)
                else:
                    if tt == 0:
                        dve.wait_ge(gate_in[s.nth % 2], 32 * (s.nth // 2 + 1))
                    x = MIX[:, tt, n * G:(n + 1) * G]
                    dst = x if e["m"] == 0 else prod_t[:, tt, :]
                    nc.vector.scalar_tensor_tensor(out=dst, in0=gate_t[:, s.nth % 2, tt, :], scalar=1.0,
                                                   in1=acc[:, bank, :], op0=ALU.add, op1=ALU.mult)\
                      .then_inc(acc_free[bank], 1)
                    dve.wait_ge(acc_free[bank], f + 1)
                    if e["m"] > 0:
                        nc.vector.tensor_tensor(x, x, prod_t[:, tt, :], ALU.add).then_inc(branch_tmp, 1)
                    else:
                        dve.sem_inc(branch_tmp, 1)
            if e["kind"] == "branch":
                dve.wait_ge(branch_tmp, 2 * (s.nth + 1))

        def stream(eng, st, split, evac, hidden):
            def body(it):
                steps = st.steps
                for i, s in enumerate(steps + [None]):
                    if s is not None and i:
                        split(eng, st, s, 0, it)
                    elif i and st.times > 1:
                        assert st.next.steps[0].width * st.next.steps[0].wtiles <= steps[0].width * steps[0].wtiles
                        split(eng, st, steps[0], 0, it + 1)
                    elif i and st.next is not None:
                        split(eng, st.next, st.next.steps[0], 0, 0)
                    if i:
                        for g in steps[i - 1].groups():
                            evac(eng, st, g, it)
                    if s is not None:
                        for g, c in s.order()[1:]:
                            split(eng, st, g, c, it)
                            if c == 5 and g is s and i and steps[i - 1].evac["kind"] == "relu2":
                                hidden(eng, st, steps[i - 1], it)
            if not st.split:
                split(eng, st, st.steps[0], 0, 0)
            passes(eng, st, body)

        def act_stream(act, st):
            stream(act, st, split_hi, act_evac, act_hidden)

        def dve_stream(dve, st):
            stream(dve, st, split_lo, dve_evac, dve_hidden)

        def pool_store(pool, st, s, it):
            e = s.evac
            for bank, tt in s.tiles:
                hold(pool, acc_free[bank], at(st, ("fill", bank), s.fill[bank] + 1, it))
                pool.dma_start(e["dst"](it, tt, s.width), stage_bufs[bank][0:e["rows"], 0:s.width])\
                    .then_inc(stored[bank], 16)
                if bank == 4:
                    hold(pool, stored[4], 16 * (at(st, ("put", 4), s.put[4], it)))
                    pool.sem_inc(mod_put, 1)
            if e.get("gates"):
                pool.wait_ge(nsa_ready, 2)
                pool.dma_start(AG.rearrange("(t p) n -> p t n", p=P), nsa_g[:, :, :]).then_inc(nsa_out, 16)

        def pool_stream(pool, st):
            def body(it):
                for s in [g for s in st.steps for g in s.groups()]:
                    e = s.evac
                    if e["kind"] == "relu2":
                        for bank, tt in s.tiles:
                            hold(pool, acc_free[bank], at(st, ("fill", bank), s.fill[bank] + 1, it))
                            last = nc.gpsimd.tensor_tensor(relu_t[:, tt, :], relu_t[:, tt, :], relu_t[:, tt, :],
                                                           ALU.mult)
                        last.then_inc(sq_done, 1)
                    elif e["kind"] == "store":
                        pool_store(pool, st, s, it)
            if st.name == "branch":
                for s in st.steps:
                    q, n, m = s.nth, s.evac["n"], s.evac["m"]
                    if q >= 2:
                        pool.wait_ge(branch_tmp, 2 * (q - 1))
                    for tt in range(2):
                        pool.dma_start(gate_t[:, q % 2, tt, :], GT[tt * P:(tt + 1) * P, m * DM + n * G:m * DM + (n + 1) * G])\
                            .then_inc(gate_in[q % 2], 16)
            else:
                passes(pool, st, body)

        def wait_stored(eng, upto):
            st = stages[upto]
            for b in range(5):
                k = st.base.get(("put", b), 0) + st.per.get(("put", b), 0) * st.times - (b == 4)
                if k:
                    eng.wait_ge(stored[b], 16 * k)

        def wait_freed(eng, upto):
            if upto is None:
                return
            st = stages[upto]
            for b in range(5):
                k = st.base.get(("fill", b), 0) + st.per.get(("fill", b), 0) * st.times
                if k:
                    eng.wait_ge(acc_free[b], k)

        prep_count = {"u": 0, "x": 0, "h": 0, "norm": 0}
        xn_ready = sem("xn_ready")
        tr_done = sem("tr_done")
        v_done = sem("v_done")
        ph_done, pl_done = sem("prep_hi_done"), sem("prep_lo_done")
        norm_ss, norm_rs = sem("norm_ss"), sem("norm_rs")

        class Prep:

            def __init__(self, name, tts, kts, T, after, off=0, vecs=None, gain=None, src=None, late=False):
                self.name, self.tts, self.kts, self.T, self.after = name, tts, kts, T, after
                self.off, self.vecs, self.gain, self.late = off, vecs, gain, late
                self.src = src or (lambda i: xn[:, i % 2, :])
                self.units = [(i, b) for i in range(len(tts)) for b in range(kts // 4)] if kts >= 4 else \
                             [(i, 0) for i in range(len(tts))]
                self.nb = min(kts, 4)
                self.u0, self.x0, self.h0 = prep_count["u"], prep_count["x"], prep_count["h"]
                prep_count["u"] += len(self.units)
                prep_count["x"] += len(tts)
                prep_count["h"] += len(self.units) if vecs else 0

            def bank(self, u):
                return 5 + u % 2

            def dst(self, t, tt, b):
                _, slot, k0 = tt
                o = self.off + (k0 + b * 4) * self.T
                return t[:, o:o + self.nb * self.T].rearrange("p (k t) -> p k t", k=self.nb)[
                    :, :, slot * P:(slot + 1) * P]

            def pe(self, pe):
                for u, (i, b) in enumerate(self.units):
                    pe.wait_ge(xn_ready, self.x0 + i + 1)
                    if u >= 2 or (self.u0 and u == 0):
                        u_ = u if u else 1
                        pe.wait_ge(pl_done if self.vecs is None else v_done, self.u0 + u_ - 1)
                    for j in range(self.nb):
                        last = nc.tensor.transpose(acc[:, self.bank(u), j * P:(j + 1) * P],
                                                   self.src(i)[:, (b * 4 + j) * P:(b * 4 + j + 1) * P], ident[:, :])
                    last.then_inc(tr_done, 1)

            def produces(self, u, late):
                per = len(self.units) // len(self.tts)
                return self.late == late and u % per == (per - 1 if late else 0) and u + per < len(self.units)

            def act(self, act, produce=None, load=None):
                wait_freed(act, self.after)
                if load:
                    load(act, 0)
                if produce:
                    produce(act, 0)
                for u, (i, b) in enumerate(self.units):
                    tt = self.tts[i]
                    if load and b == 0 and i + 1 < len(self.tts):
                        load(act, i + 1)
                    if produce and self.produces(u, False):
                        produce(act, i + 1)
                    act.wait_ge(tr_done, self.u0 + u + 1)
                    src = acc[:, self.bank(u), 0:self.nb * P].rearrange("p (k t) -> p k t", k=self.nb)
                    if self.vecs is None and self.gain and b < self.gain[1]:
                        nc.scalar.activation(self.dst(a_hi, tt, b), src, ACT.Copy, scale=self.gain[0])\
                          .then_inc(v_done, 1)
                    elif self.vecs is None:
                        nc.scalar.activation(self.dst(a_hi, tt, b), src, ACT.Copy).then_inc(v_done, 1)
                    else:
                        if u >= 2:
                            act.wait_ge(pl_done, self.u0 + u - 1)
                        g, s = self.vecs(tt[0])
                        for j in range(self.nb):
                            k = b * 4 + j
                            last = nc.scalar.activation(aff[:, u % 2, j, :], src[:, j, :], ACT.Identity,
                                                        bias=s[:, k:k + 1], scale=g[:, k:k + 1])
                        last.then_inc(v_done, 1)
                    if produce and self.produces(u, True):
                        produce(act, i + 1)

            def dve(self, dve, produce=None):
                wait_freed(dve, self.after)
                if produce:
                    produce(dve, 0)
                for u, (i, b) in enumerate(self.units):
                    tt = self.tts[i]
                    if produce and self.produces(u, False):
                        produce(dve, i + 1)
                    dve.wait_ge(v_done, self.u0 + u + 1)
                    src = acc[:, self.bank(u), 0:self.nb * P].rearrange("p (k t) -> p k t", k=self.nb)
                    hi, lo = self.dst(a_hi, tt, b), self.dst(a_lo, tt, b)
                    if self.vecs is None and not (self.gain and b < self.gain[1]):
                        nc.vector.tensor_tensor(lo, src, hi.bitcast(F32), ALU.subtract).then_inc(pl_done, 1)
                    elif self.vecs is None:
                        nc.vector.scalar_tensor_tensor(out=lo, in0=src, scalar=self.gain[0], in1=hi.bitcast(F32),
                                                       op0=ALU.mult, op1=ALU.subtract).then_inc(pl_done, 1)
                    else:
                        v = aff[:, u % 2, 0:self.nb, :]
                        nc.vector.tensor_copy(hi, v).then_inc(ph_done, 1)
                        dve.wait_ge(ph_done, self.h0 + u + 1)
                        nc.vector.tensor_tensor(lo, v, hi.bitcast(F32), ALU.subtract).then_inc(pl_done, 1)
                    if produce and self.produces(u, True):
                        produce(dve, i + 1)

            def finish(self, pe):
                pe.wait_ge(pl_done, self.u0 + len(self.units))

        pr = Arena([SCR])
        xn_at = SCR[0] + (-SCR[0]) % 32
        xn = pr("xn", [P, 2, DM])
        aff = pr("aff", [P, 2, 4, P])
        gt2 = place("gt2", [P, 2, DM], xn_at + 16384)
        V_MIX, V_MLP, V_ZERO, V_NG, V_CTX, V_X = 0, 1, 2, 3, 4, 6

        def xtile(tt, T4_):
            if not T4_:
                return XR[:, tt, :]
            return CX[:, tt, :] if tt < 2 else XR[:, tt - 2, :]

        def pow_half(pool, dst, src, n, link, eps=EPS):
            link(nc.gpsimd.tensor_scalar(dst, src, 1.0 / n, eps, ALU.mult, ALU.add))
            w = int(np.prod(dst.shape[1:]))
            return nc.gpsimd.tensor_tensor(dst, dst, bass.AP(half[:, 0:1].tensor, half[:, 0:1].offset,
                                                             [list(half[:, 0:1].ap[0]), [0, w]]), ALU.pow)

        class Links:

            def __init__(self, name):
                self.name, self.sem, self.n, self.more, self.eng = name, sem(name), 0, 0, None

            @staticmethod
            def wait(eng, s, value):
                eng.wait_ge(s, value)

            def __call__(self, ins):
                self.n += 1
                ins.then_inc(self.sem, 1)
                (hold if self.name == "pool_link" else Links.wait)(self.eng, self.sem, self.n + self.more)

            def enter(self, it, per, times):
                self.start, self.per, self.times = self.n, per, times
                self.more = it * per if times > 1 else 0

            def leave(self):
                assert self.n - self.start == self.per, (self.n - self.start, self.per)
                self.n += self.per * (self.times - 1)
                self.more = 0

        links = {"dve": Links("dve_link"), "pool": Links("pool_link")}

        class Norm:

            def __init__(self, prep, four, col):
                self.p, self.four, self.col = prep, four, col
                self.n0 = prep_count["norm"]
                prep_count["norm"] += len(prep.tts)

            def x(self, i):
                return xtile(self.p.tts[i][0], self.four)

            def act(self, act, i):
                if i >= 2:
                    act.wait_ge(tr_done, self.p.u0 + (i - 1) * (len(self.p.units) // len(self.p.tts)))
                nc.scalar.activation(xn[:, i % 2, :], self.x(i), ACT.Square,
                                     accum_out=small[:, self.col + i:self.col + i + 1]).then_inc(norm_ss, 1)

            def pool(self, pool):
                link = links["pool"]
                for i in range(len(self.p.tts)):
                    pool.wait_ge(norm_ss, self.n0 + i + 1)
                    c = small[:, self.col + i:self.col + i + 1]
                    pow_half(pool, c, c, DM, link).then_inc(norm_rs, 1)

            def dve(self, dve, i):
                dve.wait_ge(norm_rs, self.n0 + i + 1)
                c = small[:, self.col + i:self.col + i + 1]
                nc.vector.tensor_scalar(xn[:, i % 2, :], self.x(i), c, None, ALU.mult)\
                  .then_inc(xn_ready, 1)

        at_count = {}
        s = lambda n: sem("at_" + n)
        at_loaded, at_shaped, j_done = s("loaded"), s("shaped"), s("j_done")
        j_copied = [s("j_copied_act"), s("j_copied_dve")]
        s_done, m_done, p_done, t_done, tc_done = s("s_done"), s("m_done"), s("p_done"), s("t_done"), s("tc_done")
        o_done, e_done, at_saved, at_ss, at_rs = s("o_done"), s("e_done"), s("saved"), s("ss"), s("rs")
        rows_in = s("rows_in")
        rows_open, pass_open, outs_free = s("rows_open"), s("pass_open"), s("outs_free")

        class Attn:

            def __init__(self, name, times, guard=False, fill=None, follows=False):
                self.follows = follows
                self.name, self.times, self.guard, self.fill, self.opened = name, times, guard, fill, False
                self.jobs, self.units, self.rows, self.loads, self.saves = [], [], [], [], []
                self.shape_ops, self.late_ops, self.norms, self.shape_n, self.base = None, None, [], 0, {}
                self.slots, self.outs = {}, {}
                if fill is not None:
                    n = 0
                    for s_ in fill.steps:
                        for c in range(len(s_.chunks)):
                            self.slots.setdefault(3 + n * 3 // 4, []).append((s_, c))
                            n += 1
                        self.outs[3 + (n - 1) * 3 // 4 + 1] = s_

            def fill_chunks(self, slot, f, eng, it):
                for s_, c in self.slots.get(slot, []):
                    f(eng, self.fill, s_, c, it)

            def place_rows(self, ar):
                n = self.name
                self.pb, self.ptb = ar(n + "_p", [P, 3, G]), ar(n + "_pt", [P, 2, 4, P])
                self.st = ar(n + "_st", [P, 8, 4])

            def seal(self):
                self.U, self.J = len(self.units), len(self.jobs)
                J = self.J
                adds = dict(u=self.U, j=J, ja=(J + 1) // 2, jd=J // 2, passes=1, rows=len(self.rows), loads=len(self.loads),
                            saves=len(self.saves), ss=1 if self.norms else 0)
                for k, v in adds.items():
                    self.base[k] = at_count.get(k, 0)
                    at_count[k] = at_count.get(k, 0) + v * self.times
                at_count["open"] = at_count.get("open", 0)
                self.base["open"] = at_count["open"]
                at_count["open"] += self.times + 1
                self.base["rows_open"] = at_count.get("rows_open", 0) - self.follows
                at_count["rows_open"] = self.base["rows_open"] + self.times + 1
                self.sinks = [sum(1 for w in self.units[:u] if w.sink is not None) for u in range(self.U + 1)]
                self.el = [0]
                for w in self.units:
                    self.el.append(self.el[-1] + 1 + (w.sink is not None or self.guard) + (w.coeff is not None))

            def each(self, eng, body):
                if self.times > 1:
                    with eng.Fori(0, self.times) as it:
                        body(it)
                else:
                    body(0)

            def pool(self, pool):
                B = self.base

                pool.sem_inc(outs_free, 1)

                def body(it):
                    if self.norms:
                        hold(pool, at_ss, B['ss'] + it + 1)
                        link = links["pool"]
                        link.enter(it, len(self.norms), self.times)
                        for c, w in self.norms:
                            last = pow_half(pool, c, c, w, link)
                        last.then_inc(at_rs, 1)
                        link.leave()
                    if self.fill is not None:
                        for s_ in self.fill.steps:
                            pool_store(pool, self.fill, s_, it)
                    for q, (dst, src) in enumerate(self.saves):
                        if q == 0:
                            hold(pool, e_done, B['u'] + self.U * it + self.U)
                        pool.dma_start(dst(it), src).then_inc(at_saved, 16)
                    hold(pool, at_saved, 16 * (B['saves'] + len(self.saves) * (it + 1)))
                    pool.sem_inc(outs_free, 1)
                self.each(pool, body)

            def sp_rows(self, sp, it=0):
                if self.base['open'] and isinstance(it, int) and it == 0 and not self.follows:
                    sp.wait_ge(outs_free, self.base['open'])
                hold(sp, rows_open, self.base['rows_open'] + it + 1)
                for dst, src in self.rows:
                    sp.dma_start(dst, src(it), allow_slow_non_contiguous=True).then_inc(rows_in, 16)

            def sp(self, sp):
                B = self.base

                def body(it, last=False):
                    hold(sp, pass_open, B['open'] + it + 1)
                    for dst, src in self.loads:
                        sp.dma_start(dst, src(it), allow_slow_non_contiguous=True).then_inc(at_loaded, 16)
                    if self.fill is not None:
                        for s_ in self.fill.steps:
                            sp_chunks(sp, self.fill, s_, it)
                    if not last:
                        self.sp_rows(sp, it + 1)
                if B['open']:
                    sp.wait_ge(outs_free, B['open'])
                if self.times > 2:
                    with sp.Fori(0, self.times - 1) as it:
                        body(it)
                else:
                    body(0)
                body(self.times - 1, True)

            def pe(self, pe):
                U, J, B = self.U, self.J, self.base

                def body(it):
                    if self.fill is not None:
                        hold(pe, acc_free[4], at(self.fill, ("fill", 4), 0, it))
                    for j, (srcs, _, _) in enumerate(self.jobs):
                        if j == 0:
                            hold(pe, at_shaped, B['passes'] + it + 1)
                        if j >= 2:
                            done = (j // 2)
                            tot = (J + 1) // 2 if j % 2 == 0 else J // 2
                            hold(pe, j_copied[j % 2], B['jd' if j % 2 else 'ja'] + tot * it + done)
                        for x, src in enumerate(srcs):
                            w = src.shape[-1]
                            last = nc.tensor.transpose(acc[0:w, j % 2, x * P:(x + 1) * P], src, ident[:, :])
                        last.then_inc(j_done, 1)
                    pe.wait_ge(j_copied[0], B['ja'] + ((J + 1) // 2) * (it + 1))
                    if J > 1:
                        pe.wait_ge(j_copied[1], B['jd'] + (J // 2) * (it + 1))
                    hold(pe, at_loaded, 16 * (B['loads'] + len(self.loads) * (it + 1)))
                    for u in range(U + 3):
                        if u < U:
                            w = self.units[u]
                            if u >= 2:
                                pe.wait_ge(p_done, B['u'] + U * it + u - 1)
                            bank = 4 + u % 2
                            n = len(w.q)
                            for x in range(n):
                                last = nc.tensor.matmul(acc[:, bank, 0:w.keys], w.q[x], w.k[x], start=x == 0,
                                                        stop=x == n - 1 and w.bias is None)
                            if w.bias is not None:
                                b, c0 = w.bias
                                last = nc.tensor.matmul(acc[:, bank, c0:w.keys], ident[:, :], b,
                                                        start=False, stop=True)
                            last.then_inc(s_done, 1)
                        self.fill_chunks(u, pe_chunk, pe, it)
                        if 0 <= u - 2 < U:
                            t = u - 2
                            w = self.units[t]
                            pe.wait_ge(p_done, B['u'] + U * it + t + 1)
                            if t >= 2:
                                pe.wait_ge(tc_done, B['u'] + U * it + t - 1)
                            for x, vt in enumerate(w.v):
                                kk = min(P, w.keys - x * P)
                                last = nc.tensor.transpose(acc[0:kk, (2, 6)[t % 2], x * P:(x + 1) * P],
                                                           self.pb[:, t % 3, x * P:x * P + kk], ident[:, :])
                            last.then_inc(t_done, 1)
                        if 0 <= u - 3 < U:
                            t = u - 3
                            w = self.units[t]
                            pe.wait_ge(tc_done, B['u'] + U * it + t + 1)
                            if t >= 2:
                                pe.wait_ge(e_done, B['u'] + U * it + t - 1)
                            for x, vt in enumerate(w.v):
                                kk = min(P, w.keys - x * P)
                                last = nc.tensor.matmul(acc[:, (3, 7)[t % 2], 0:P], self.ptb[0:kk, t % 2, x, :], vt,
                                                        start=x == 0, stop=x == len(w.v) - 1)
                            last.then_inc(o_done, 1)
                self.each(pe, body)
                if self.fill is not None:
                    n = self.fill.base[("fill", 4)] + self.fill.per[("fill", 4)] * self.times
                    pe.wait_ge(acc_free[4], n)

            def act(self, act):
                U, J, B = self.U, self.J, self.base

                def body(it):
                    for j in range(0, J, 2):
                        act.wait_ge(j_done, B['j'] + J * it + j + 1)
                        srcs, dst, scale = self.jobs[j]
                        w, n = srcs[0].shape[-1], len(srcs)
                        nc.scalar.activation(dst, acc[0:w, 0, 0:n * P], ACT.Copy, scale=scale)\
                          .then_inc(j_copied[0], 1)
                    for u in range(U + 2):
                        if u < U:
                            w = self.units[u]
                            act.wait_ge(m_done, B['u'] + U * it + u + 1)
                            if u >= 3:
                                act.wait_ge(t_done, B['u'] + U * it + u - 2)
                            st = self.st[:, u % 8, :]
                            if w.sink is not None:
                                nc.scalar.activation(st[:, 2:3], w.sink, ACT.Exp, bias=st[:, 0:1])
                            nc.scalar.activation(self.pb[:, u % 3, 0:w.keys], acc[:, 4 + u % 2, 0:w.keys], ACT.Exp,
                                                 bias=st[:, 0:1], accum_out=st[:, 1:2]).then_inc(p_done, 1)
                        self.fill_chunks(u + 2, split_hi, act, it)
                        if u in self.outs:
                            act_evac(act, self.fill, self.outs[u], it)
                        if 0 <= u - 2 < U:
                            t = u - 2
                            w = self.units[t]
                            act.wait_ge(t_done, B['u'] + U * it + t + 1)
                            if t >= 2:
                                act.wait_ge(o_done, B['u'] + U * it + t - 1)
                            kk, n = min(P, w.keys), len(w.v)
                            nc.scalar.activation(self.ptb[0:kk, t % 2, 0:n, :],
                                                 acc[0:kk, (2, 6)[t % 2], 0:n * P].rearrange("p (n t) -> p n t", n=n),
                                                 ACT.Copy).then_inc(tc_done, 1)
                self.each(act, body)

            def open_rows(self, dve):
                dve.sem_inc(rows_open, 1)
                self.opened = True

            def dve(self, dve):
                U, J, B = self.U, self.J, self.base

                if not self.opened and not self.follows:
                    self.open_rows(dve)
                dve.sem_inc(pass_open, 1)

                def body(it):
                    dve.wait_ge(rows_in, 16 * (B['rows'] + len(self.rows) * (it + 1)))
                    link = links["dve"]
                    link.enter(it, self.shape_n + self.sinks[U] + self.el[U], self.times)
                    if self.shape_ops:
                        self.shape_ops(dve, link, it)
                    if self.follows:
                        dve.wait_ge(outs_free, B['open'])
                    dve.sem_inc(at_shaped, 1)
                    for j in range(1, J, 2):
                        dve.wait_ge(j_done, B['j'] + J * it + j + 1)
                        srcs, dst, scale = self.jobs[j]
                        w, n = srcs[0].shape[-1], len(srcs)
                        nc.vector.tensor_scalar(dst, acc[0:w, 1, 0:n * P], scale, None, ALU.mult)\
                          .then_inc(j_copied[1], 1)
                    dve.wait_ge(j_done, B['j'] + J * (it + 1))
                    dve.sem_inc(rows_open, 1)
                    dve.wait_ge(at_loaded, 16 * (B['loads'] + len(self.loads) * (it + 1)))
                    dve.wait_ge(outs_free, B['open'] + it + 1)
                    if self.late_ops:
                        self.late_ops(dve, link, it)
                    for u in range(U + 4):
                        if u < U:
                            w = self.units[u]
                            dve.wait_ge(s_done, B['u'] + U * it + u + 1)
                            if u >= 8:
                                dve.wait_ge(e_done, B['u'] + U * it + u - 7)
                            m = self.st[:, u % 8, 0:1]
                            ins = nc.vector.tensor_reduce(m, acc[:, 4 + u % 2, 0:w.keys], AX.X, ALU.max, negate=True)
                            if w.sink is not None:
                                link(ins)
                                ins = nc.vector.scalar_tensor_tensor(out=m, in0=w.sink, scalar=-1.0, in1=m,
                                                                     op0=ALU.mult, op1=ALU.min)
                            ins.then_inc(m_done, 1)
                        self.fill_chunks(u + 1, split_lo, dve, it)
                        if 0 <= u - 4 < U:
                            t = u - 4
                            w = self.units[t]
                            st = self.st[:, t % 8, :]
                            dve.wait_ge(o_done, B['u'] + U * it + t + 1)
                            if w.add:
                                dve.wait_ge(e_done, B['u'] + U * it + t)
                            if w.sink is not None and self.guard:
                                link(nc.vector.tensor_scalar(st[:, 1:2], st[:, 1:2], st[:, 2:3], TINY,
                                                             ALU.add, ALU.max))
                            elif w.sink is not None:
                                link(nc.vector.tensor_tensor(st[:, 1:2], st[:, 1:2], st[:, 2:3], ALU.add))
                            elif self.guard:
                                link(nc.vector.tensor_scalar(st[:, 1:2], st[:, 1:2], TINY, None, ALU.max))
                            link(nc.vector.reciprocal(st[:, 3:4], st[:, 1:2]))
                            if w.coeff is not None:
                                link(nc.vector.tensor_tensor(st[:, 3:4], st[:, 3:4], w.coeff, ALU.mult))
                            o = acc[:, (3, 7)[t % 2], 0:P]
                            if w.add:
                                nc.vector.scalar_tensor_tensor(out=w.out, in0=o, scalar=st[:, 3:4], in1=w.out,
                                                               op0=ALU.mult, op1=ALU.add).then_inc(e_done, 1)
                            else:
                                nc.vector.tensor_scalar(w.out, o, st[:, 3:4], None, ALU.mult)\
                                  .then_inc(e_done, 1)
                    dve.wait_ge(e_done, B['u'] + U * it + U)
                    dve.sem_inc(pass_open, 1)
                    link.leave()
                self.each(dve, body)
        setup_in = sem("setup_in")
        brev_mm, brev_sb, brev_out = sem("brev_mm"), sem("brev_sb"), sem("brev_out")
        silu_t, lam_e = sem("silu_t"), sem("lam_e")
        su = Arena([(ALO[0] + 16384, ALO[1])])
        onehot_t, relb_t = su("onehot_t", [BUCKETS, G]), su("relb_t", [BUCKETS, 24])
        bmask_t, brev_t = su("bmask_t", [24, G]), su("brev_t", [24, G])
        cv, ct = su("cv", [P, KT, 2]), su("ct", [P, KT, 2])
        lamv, lamp = su("lamv", [P, 4, 64]), su("lamp", [P, 2, 64])
        lam = small[:, 40:44]
        SETUP_LOADS = 13

        def bcast(ap, n=P):
            return bass.AP(ap.tensor, ap.offset, [[0, n]] + [list(x) for x in ap.ap])

        def setup_act_loads(act):
            loads = [(onehot_t[:, :], C["onehot"]), (relb_t[:, :], A["rel_bias"]), (bmask_t[:, :], C["bmask"]),
                     (cv[:, :, 0], A["c_ctx_2"].rearrange("(k p) -> p k", p=P)),
                     (cv[:, :, 1], A["c_2"][0].rearrange("(k p) -> p k", p=P)),
                     (vec[:, V_MIX, :], A["norm_mix"][0].rearrange("(k p) -> p k", p=P)),
                     (vec[:, V_MLP, :], A["norm_mlp"][0].rearrange("(k p) -> p k", p=P)),
                     (vec[:, V_NG, :], A["norm_g_2"][0].rearrange("(k p) -> p k", p=P)),
                     (lamv[:, 0, :], bcast(A["a_lam_q1_2"][0])), (lamv[:, 1, :], bcast(A["a_lam_k1_2"][0])),
                     (lamv[:, 2, :], bcast(A["a_lam_q2_2"][0])), (lamv[:, 3, :], bcast(A["a_lam_k2_2"][0])),
                     (small[:, 44:45], C["valid"])]
            assert len(loads) == SETUP_LOADS
            for dst, src in loads:
                act.dma_start(dst, src, allow_slow_non_contiguous=True).then_inc(setup_in, 16)

        def setup_gpsimd(pool):
            for s, n in ((acc_free[4], 1), (mod_put, 1), (ht_done, 1), (sq_done, 1),
                         (hh_done, 1), (hl_done, 1)):
                pool.sem_inc(s, n)
            nc.gpsimd.memset(half[:, :], -0.5)
            nc.gpsimd.memset(ident[:, :], 0.0).then_inc(setup_gp, 1)
            pool.wait_ge(setup_gp, 1)
            nc.gpsimd.affine_select(out=ident[:, :], in_=ident[:, :], compare_op=ALU.not_equal, fill=1.0, base=0,
                                    pattern=[[-1, P]], channel_multiplier=1).then_inc(setup_gp, 1)
            pool.wait_ge(setup_gp, 2)

        def setup_pe(pe):
            pe.wait_ge(setup_in, 16 * SETUP_LOADS)
            pe.wait_ge(setup_gp, 2)
            nc.tensor.matmul(acc[0:24, 7, :], relb_t[:, :], onehot_t[:, :], start=True, stop=True)\
              .then_inc(brev_mm, 1)

        def setup_act(act):
            act.wait_ge(setup_in, 16 * SETUP_LOADS)
            nc.scalar.activation(ct[:, :, :], cv[:, :, :], ACT.Tanh, scale=0.5).then_inc(silu_t, 1)
            act.wait_ge(lam_e, 1)
            nc.scalar.activation(lam[:, 0:2], lam[:, 0:2], ACT.Exp).then_inc(lam_e, 1)

        def setup_vector(dve):
            link = links["dve"]
            dve.wait_ge(setup_in, 16 * SETUP_LOADS)
            nc.vector.memset(vec[:, V_ZERO, :], 0.0)
            link(nc.vector.memset(MV[:, :].bitcast(F32), 0.0))
            link(nc.vector.tensor_tensor(lamp[:, 0, :], lamv[:, 0, :], lamv[:, 1, :], ALU.mult))
            link(nc.vector.tensor_tensor(lamp[:, 1, :], lamv[:, 2, :], lamv[:, 3, :], ALU.mult))
            nc.vector.tensor_reduce(lam[:, 0:2], lamp[:, :, :], AX.X, ALU.add).then_inc(lam_e, 1)
            dve.wait_ge(lam_e, 2)
            link(nc.vector.tensor_tensor(lam[:, 2:3], lam[:, 1:2], lam[:, 0:1], ALU.subtract))
            link(nc.vector.tensor_scalar(lam[:, 2:3], lam[:, 2:3], -LAM_INIT, None, ALU.add))
            dve.wait_ge(silu_t, 1)
            link(nc.vector.scalar_tensor_tensor(out=ct[:, :, :], in0=ct[:, :, :], scalar=1.0, in1=cv[:, :, :],
                                                op0=ALU.add, op1=ALU.mult))
            link(nc.vector.tensor_scalar(ct[:, :, :], ct[:, :, :], 0.5, None, ALU.mult))
            mv = MV[:, 0:4 * KT].rearrange("p (k c) -> p k c", c=4)
            link(nc.vector.tensor_copy(mv[:, :, 0:2], ct[:, :, :]))
            link(nc.vector.tensor_tensor(mv[:, :, 2:4], ct[:, :, :], mv[:, :, 0:2].bitcast(F32), ALU.subtract))
            dve.wait_ge(brev_mm, 1)
            nc.vector.tensor_tensor(brev_t[:, :], acc[0:24, 7, :], bmask_t[:, :], ALU.add).then_inc(brev_sb, 1)
            dve.wait_ge(brev_sb, 1)

        def setup_brev(pool):
            pool.wait_ge(brev_sb, 1)
            pool.dma_start(BREV[:, :], brev_t[:, :]).then_inc(brev_out, 16)
            pool.wait_ge(brev_out, 16)

        bt_out = sem("bt_out")

        def setup_bias_tiles(act):
            act.wait_ge(brev_out, 16)
            src = BREV[0]
            act.dma_start(BROW[:, :, :], bass.AP(src.tensor, 0, [[G, 24], [0, P], [1, G]])).then_inc(bt_out, 16)

        X2 = [(0, 0, 0), (1, 1, 0)]
        X4 = [(t, t, 0) for t in range(4)]
        row = lambda i: vec[:, i, :]
        p1 = Prep("p1", X2, KT, 256, None, vecs=lambda tt: (row(V_MIX), row(V_ZERO)))
        n1 = Norm(p1, False, 0)
        p2 = Prep("p2", [(0, 0, 0), (0, 0, 12), (1, 1, 0), (1, 1, 12)], 12, 256, "cmp1")
        p3 = Prep("p3", X2, KT, 256, "branch", src=lambda i: MIX[:, i, :])
        p4 = Prep("p4", X2, KT, 256, "out1", vecs=lambda tt: (row(V_MLP), row(V_ZERO)))
        n4 = Norm(p4, False, 4)
        mod_vecs = lambda tt: (row(V_CTX), row(V_CTX + 1)) if tt < 2 else (row(V_X), row(V_X + 1))
        p5 = Prep("p5", X4, KT, 512, "mlp", vecs=mod_vecs)
        n5 = Norm(p5, True, 8)
        p6 = Prep("p6", X4, KT, 512, "in2_end", gain=(subg[:, 0:1], 2), late=True)
        p7 = Prep("p7", X4, KT, 512, "out2", vecs=mod_vecs)
        n7 = Norm(p7, True, 12)
        p8q = Prep("p8q", [(2, 2, 0), (3, 3, 0)], 4, 512, "in3_gates")
        p8k = Prep("p8k", X4, 2, 512, "in3_gates", off=2048)
        p9 = Prep("p9", [(2, 2, 0), (3, 3, 0)], KT, 512, "kvb")

        cmp_in, cmp_tr = sem("cmp_in"), sem("cmp_tr")
        cmp_hi, cmp_th, cmp_tr2, cmp_gt, cmp_mm, cmp_o, cmp_out = (
            sem("cmp_hi"), sem("cmp_th"), sem("cmp_tr2"), sem("cmp_gt"), sem("cmp_mm"),
            sem("cmp_o"), sem("cmp_out"))
        cp = Arena([SCR])
        CW = 2176
        cmp_rows = cp("cmp_rows", [P, 2, 512])
        cmp_pos = cp("cmp_pos", [64, HD])
        kvT = cp("kvT", [P, 4, 256])
        posT = cp("posT", [P, 64])
        cmp_v = cp("cmp_v", [P, CW])
        gel = cp("gel", [32, 4, 512])
        cmp_w2t = cp("cmp_w2t", [P, 2, 2, HD])
        gT = place("gT", [P, 4, 32], AHI[0])
        cmp_ok = place("cmp_ok", [P, 32], AHI[0] + 1024)
        cmp_ov = place("cmp_ov", [32, HD], AHI[0] + 2048)

        def cmp_pool_loads(pool):
            wait_stored(pool, "qkv_end")
            pool.wait_ge(pl_done, p1.u0 + len(p1.units))
            for tt in range(2):
                pool.dma_start(cmp_rows[:, tt, :], U1[tt * P:(tt + 1) * P, 1024:1536]).then_inc(cmp_in, 16)
            pool.dma_start(cmp_pos[:, :], A["cmp_pos"][0].rearrange("w l d -> (w l) d")).then_inc(cmp_in, 16)
            pool.dma_start(cmp_w2t[:, :, :, :], A["cmp_w2"][0].rearrange("w (j p) d -> p w j d", p=P))\
                .then_inc(cmp_in, 16)

        def cmp_pe_prep(pe):
            pe.wait_ge(cmp_in, 64)
            for tt in range(2):
                for b in range(4):
                    nc.tensor.transpose(acc[:, 5 + b // 2, (b % 2) * 256 + tt * P:(b % 2) * 256 + (tt + 1) * P],
                                        cmp_rows[:, tt, b * P:(b + 1) * P], ident[:, :])
            nc.tensor.transpose(acc[:, 7, 0:64], cmp_pos[:, :], ident[0:64, 0:64]).then_inc(cmp_tr, 1)

        def cmp_dve_prep(dve):
            link = links["dve"]
            dve.wait_ge(cmp_tr, 1)
            for b in range(2):
                link(nc.vector.tensor_copy(kvT[:, 2 * b:2 * b + 2, :],
                                           acc[:, 5 + b, :].rearrange("p (a t) -> p a t", a=2)))
            link(nc.vector.tensor_copy(posT[:, :], acc[:, 7, 0:64]))
            link(nc.vector.memset(cmp_v[:, :], 0.0))
            for w in range(2):
                for kv in range(2):
                    o = cmp_v[:, w * 1024:w * 1024 + 960].rearrange("p (l v c) -> p l v c", l=32, v=2)[:, :, kv, :]
                    base = kvT[:, 2 * w + kv, 0:1]
                    src = bass.AP(base.tensor, base.offset, [list(base.ap[0]), [1, 32], [16, NCMP]])
                    pos = posT[:, w * 32:w * 32 + 1]
                    pb = bass.AP(pos.tensor, pos.offset, [list(pos.ap[0]), [1, 32], [0, NCMP]])
                    link(nc.vector.tensor_tensor(o, src, pb, ALU.add))
            wait_freed(dve, "gates")
            link(nc.vector.tensor_copy(a_hi[:, 4096:4096 + CW], cmp_v[:, :]))
            nc.vector.tensor_tensor(a_lo[:, 4096:4096 + CW], cmp_v[:, :], a_hi[:, 4096:4096 + CW].bitcast(F32),
                                    ALU.subtract).then_inc(cmp_hi, 1)

        def cmp_dve_gelu(dve):
            for w in range(2):
                wait_done(dve, stages["cmp1"], stages["cmp1"].steps[w], w, 0)
            g = lambda i: gel[0:30, i, :].rearrange("p (w n) -> p w n", w=2)
            link = links["dve"]
            link(nc.vector.tensor_copy(g(0), acc[0:30, 0:2, 0:256]))
            for w in range(2):
                dve.sem_inc(acc_free[w], 1)
            link(nc.vector.tensor_tensor(g(1), g(0), g(0), ALU.mult))
            link(nc.vector.tensor_scalar(g(1), g(1), 0.044715, 1.0, ALU.mult, ALU.add))
            nc.vector.tensor_tensor(g(1), g(1), g(0), ALU.mult).then_inc(cmp_th, 1)
            dve.wait_ge(cmp_th, 2)
            link(nc.vector.scalar_tensor_tensor(out=g(2), in0=g(2), scalar=1.0, in1=g(0), op0=ALU.add, op1=ALU.mult))
            nc.vector.tensor_scalar(g(3), g(2), 0.5, None, ALU.mult).then_inc(cmp_gt, 1)
            dve.wait_ge(cmp_tr2, 1)
            nc.vector.tensor_copy(gT[:, :, 0:30], acc[:, 5, 0:128].rearrange("p (a b) -> p a b", a=4)[:, :, 0:30])\
              .then_inc(cmp_gt, 1)
            dve.wait_ge(cmp_mm, 1)
            nc.vector.tensor_copy(cmp_ok[:, 0:30], acc[:, 6, 0:30]).then_inc(cmp_o, 1)
            nc.vector.tensor_copy(cmp_ov[0:30, :], acc[0:30, 7, 0:P]).then_inc(cmp_o, 1)

        def cmp_act(act):
            act.wait_ge(cmp_th, 1)
            nc.scalar.activation(gel[0:30, 2, :], gel[0:30, 1, :], ACT.Tanh, scale=GELU_C).then_inc(cmp_th, 1)

        def cmp_pe(pe):
            pe.wait_ge(cmp_gt, 1)
            for a in range(4):
                last = nc.tensor.transpose(acc[:, 5, a * 32:a * 32 + 30], gel[0:30, 3, a * P:(a + 1) * P],
                                           ident[0:30, 0:30])
            last.then_inc(cmp_tr2, 1)
            pe.wait_ge(cmp_gt, 2)
            for j in range(2):
                nc.tensor.matmul(acc[:, 6, 0:30], cmp_w2t[:, 0, j, :], gT[:, j, 0:30], start=j == 0, stop=j == 1)
            for j in range(2):
                last = nc.tensor.matmul(acc[0:30, 7, 0:P], gT[:, 2 + j, 0:30], cmp_w2t[:, 1, j, :],
                                        start=j == 0, stop=j == 1)
            last.then_inc(cmp_mm, 1)

        def cmp_pool_store(pool):
            pool.wait_ge(cmp_o, 2)
            pool.dma_start(CMPK[:, :], cmp_ok[:, 0:30]).then_inc(cmp_out, 16)
            pool.dma_start(CMPV[:, :], cmp_ov[0:30, :]).then_inc(cmp_out, 16)
            pool.wait_ge(cmp_out, 32)

        at1 = Attn("at1", 2, guard=True)
        cmp_end = 4 * (4096 + CW)
        ends = Arena([(AHI[0] + cmp_end, AHI[1]), (ALO[0] + cmp_end, ALO[1]), (cp.regions[0][0], SCR[1])])
        q1 = [ends(f"q1_{m}", [P, 2, 512]) for m in range(3)]
        k1 = [ends(f"k1_{n}", [P, 2, HD]) for n in "swbc"]
        ar = Arena([(SCR[0], cp.regions[0][0]), (AHI[0], AHI[0] + cmp_end), (ALO[0], ALO[0] + cmp_end)] + ends.regions)
        at1.place_rows(ar)
        v1 = [ar(f"v1_{n}", [P, 2, HD]) for n in "swbc"]
        q1T = [ar(f"q1T_{m}", [P, 2, 4, P]) for m in range(3)]
        k1T = [ar(f"k1T_{n}", [P, 256]) for n in "swbc"]
        bias1 = [ar(f"bias1_{m}", [P, 4, 256]) for m in range(3)]
        ckT, cvt, cbias = ar("ckT", [P, NCMP]), ar("cvt", [NCMP, HD]), ar("cbias", [P, 2, 4, NCMP])
        gA, gV, sink1 = ar("gA", [P, 2, 12]), ar("gV", [P, 2, 4]), ar("sink1", [P, 4])
        ob1 = ar("ob1", [P, 2, 3, 512])
        QC = [0, 2584, 4120]
        KC = [1536, 2048, 3608, 5144]
        VC = [1792, 2304, 3864, 5400]

        def tiles_of(U, c0, w, step):
            n = U.shape[0] // P
            return lambda it: U[:, bass.ds(c0 + it * step, w)].rearrange("(t p) n -> p t n", p=P)

        def skewed(h0, off, per_key, keys, heads=4):
            def f(it):
                head = BROW[bass.ds(it * 4 + h0, heads), 0, off:off + 1]
                return bass.AP(head.tensor, head.offset, [[G - 1, P]] + [[P * G, 4]] * (heads > 1) + [[per_key, keys]])
            return f

        for m in range(3):
            at1.rows.append((q1[m][:, :, :], tiles_of(U1, QC[m], 512, 512)))
            at1.loads.append((bias1[m][:, :, :], skewed(8 * m, 127, 1, 256)))
        for n in range(4):
            at1.rows.append((k1[n][:, :, :], tiles_of(U1, KC[n], HD, HD)))
            at1.loads.append((v1[n][:, :, :], tiles_of(U1, VC[n], HD, HD)))
        for qt in range(2):
            for g in range(4):
                at1.loads.append((cbias[:, qt, g, :], skewed(g, 286 - P * qt, 16, NCMP, 1)))
        at1.loads.append((ckT[:, :], lambda it: CMPK[:, bass.ds(it * NCMP, NCMP)]))
        at1.loads.append((cvt[:, :], lambda it: CMPV[bass.ds(it * NCMP, NCMP), :]))
        at1.loads.append((gA[:, :, :], tiles_of(AG, 0, 12, 12)))
        at1.loads.append((sink1[:, :], lambda it: bcast(A["swa_sinks"][0, bass.ds(it * 4, 4)])))

        def shape1(dve, link, it):
            link(nc.vector.tensor_scalar(gA[:, :, :], gA[:, :, :], 0.5, 0.5, ALU.mult, ALU.add))
            g0 = gA[:, :, :].rearrange("p t (g b) -> p t g b", b=3)[:, :, :, 0]
            link(nc.vector.tensor_scalar(gV[:, 0, :], g0[:, 0, :], small[:, 44:45], None, ALU.mult))
            link(nc.vector.tensor_copy(gV[:, 1, :], g0[:, 1, :]))
        at1.late_ops, at1.shape_n = shape1, 3
        for m in range(3):
            for tt in range(2):
                at1.jobs.append(([q1[m][:, tt, g * P:(g + 1) * P] for g in range(4)],
                                 q1T[m][:, tt, :, :].rearrange("p g t -> p (g t)"), SCALE))
        for n in range(4):
            at1.jobs.append(([k1[n][:, tt, :] for tt in range(2)], k1T[n][:, :], 1.0))
        for g in range(4):
            for qt in range(2):
                L = (qt + 1) * P
                bb = lambda m: (bias1[m][:, g, 256 - L:256], 0)
                o = lambda m: ob1[:, qt, m, g * P:(g + 1) * P]
                vt = lambda n: [v1[n][:, t, :] for t in range(qt + 1)]
                gate = lambda b: gA[:, qt, 3 * g + b:3 * g + b + 1]
                qa = [q1T[0][:, qt, g, :]]
                at1.units += [
                    Unit(qa, [ckT[:, :]], [cvt[:, :]], NCMP, o(0), (cbias[:, qt, g, :], 0), None, gV[:, qt, g:g + 1]),
                    Unit(qa, [k1T[0][:, 0:L]], vt(0), L, o(0), bb(0), None, gate(1), True),
                    Unit(qa, [k1T[1][:, 0:L]], vt(1), L, o(0), bb(0), None, gate(2), True),
                    Unit([q1T[1][:, qt, g, :]], [k1T[2][:, 0:L]], vt(2), L, o(1), bb(1), sink1[:, g:g + 1]),
                    Unit([q1T[2][:, qt, g, :]], [k1T[3][:, 0:L]], vt(3), L, o(2), bb(2))]
        for tt in range(2):
            at1.saves.append((lambda it, tt=tt: OB[tt * P:(tt + 1) * P, :].rearrange("p (m n) -> p m n", m=3)[
                :, :, bass.ds(it * 512, 512)], ob1[:, tt, :, :]))
        at1.seal()

        def rope(link, x, o, h, cs, tmp):
            t, m = x.shape[1], x.shape[2]
            c, s = [bass.AP(a.tensor, a.offset, [list(a.ap[0]), list(a.ap[1]), [0, m], [1, h]]) for a in cs]
            x1, x2 = x[:, :, :, o:o + h], x[:, :, :, o + h:o + 2 * h]
            y = [tmp[:, i * t * m * h:(i + 1) * t * m * h].rearrange("p (t m h) -> p t m h", t=t, m=m)
                 for i in range(4)]
            link(nc.vector.tensor_tensor(y[0], x1, c, ALU.mult))
            link(nc.vector.tensor_tensor(y[1], x2, s, ALU.mult))
            link(nc.vector.tensor_tensor(y[2], x1, s, ALU.mult))
            link(nc.vector.tensor_tensor(y[3], x2, c, ALU.mult))
            link(nc.vector.tensor_tensor(x1, y[0], y[1], ALU.subtract))
            link(nc.vector.tensor_tensor(x2, y[2], y[3], ALU.add))

        def rows3(ap, inner):
            return bass.AP(ap.tensor, ap.offset, [list(ap.ap[0]), [1, ap.shape[1]], [0, inner]])

        def cols3(ap, outer):
            return bass.AP(ap.tensor, ap.offset, [list(ap.ap[0]), [0, outer], [1, ap.shape[1]]])

        atA = Attn("atA", 4, fill=stages["modA"])
        ar = Arena([SCR, AHI, ALO])
        qA, kA = (ar(n, [P, 4, 2, HD]) for n in ("qA", "kA"))
        tmpA = ar("tmpA", [P, 2048])
        csA = ar("csA", [P, 2, 2, 32])
        rows_end = SCR[0] + 4 * (2 * 2048 + 512 + 2 * 128) + 64
        assert ar.regions[0][0] <= rows_end
        ar = Arena([(rows_end, SCR[1]), AHI, ALO])
        atA.place_rows(ar)
        vA, qAT, kAT = ar("vA", [P, 4, 2, HD]), ar("qAT", [P, 2, 4, P]), ar("kAT", [P, 2, 4, P])
        oA2 = ar("oA2", [P, 4, 2, HD])
        for dst, c0 in ((qA, 0), (kA, 1024), (vA, 2048)):
            (atA.loads if dst is vA else atA.rows).append(
                (dst[:, :, :, :].rearrange("p t h d -> p t (h d)"), tiles_of(U2, c0, 256, 256)))
        atA.rows.append((csA[:, :, :, :], lambda it: C["cs64"].rearrange("c (t p) h -> p c t h", p=P)))

        def shapeA(dve, link, it):
            for x in (qA, kA):
                v = x[:, 2:4, :, :].rearrange("p t h (m d) -> p t (h m) d", m=2)
                rope(link, v, 0, 32, (csA[:, 0, :, :], csA[:, 1, :, :]), tmpA[:, :])
        atA.shape_ops, atA.shape_n = shapeA, 12
        for src, dst, sc in ((qA, qAT, 0.125), (kA, kAT, 1.0)):
            for h in range(2):
                atA.jobs.append(([src[:, t, h, :] for t in range(4)],
                                 dst[:, h, :, :].rearrange("p t n -> p (t n)"), sc))
        for h in range(2):
            for qt in range(4):
                L = 256 if qt < 2 else 512
                for m in range(2):
                    r = slice(64 * m, 64 * m + 64)
                    atA.units.append(Unit([qAT[r, h, qt, :]], [kAT[r, h, 0:L // P, :].rearrange("p t n -> p (t n)")],
                                          [vA[:, t, h, :] for t in range(L // P)], L, oA2[:, qt, h, :],
                                          coeff=lam[:, 2:3] if m else None, add=m == 1))
        atA.saves.append((lambda it: O2[:, bass.ds(it * 256, 256)].rearrange("(t p) n -> p t n", p=P),
                          oA2[:, :, :, :].rearrange("p t h d -> p t (h d)")))
        atA.seal()

        atB = Attn("atB", 2, fill=stages["modB"], follows=True)
        ar = Arena([(SCR[0], rows_end)])
        qB_, kB, tmpB = ar("qB_", [P, 4, 4, HD]), ar("kB", [P, 4, HD]), ar("tmpB", [P, 2048])
        csB = ar("csB", [P, 2, 2, 64])
        ar = Arena([(rows_end, SCR[1]), AHI, ALO])
        atB.place_rows(ar)
        vB = ar("vB", [P, 4, HD])
        qBT, kBT = ar("qBT", [P, 4, 4, P]), ar("kBT", [P, 512])
        oB = ar("oB", [P, 4, 4, HD])
        bandB, sinkB = ar("bandB", [P, 2, 256]), ar("sinkB", [P, 4])
        for dst, c0, w in ((qB_[:, :, :, :].rearrange("p t h d -> p t (h d)"), 3072, 512), (kB[:, :, :], 4096, HD),
                           (vB[:, :, :], 4352, HD)):
            (atB.loads if c0 == 4352 else atB.rows).append((dst, tiles_of(U2, c0, w, w)))
        atB.rows.append((csB[:, :, :, :], lambda it: C["cs128"].rearrange("c (t p) h -> p c t h", p=P)))
        atB.loads.append((bandB[:, :, :], lambda it: C["band"].rearrange("(t p) n -> p t n", p=P)))
        atB.loads.append((sinkB[:, :], lambda it: bcast(A["b_sink_2"][0, bass.ds(it * 4, 4)])))

        def shapeB(dve, link, it):
            cs = (csB[:, 0, :, :], csB[:, 1, :, :])
            rope(link, qB_[:, 2:4, :, :], 0, 64, cs, tmpB[:, :])
            rope(link, kB[:, 2:4, :].rearrange("p t (m d) -> p t m d", m=1), 0, 64, cs, tmpB[:, :])
        atB.shape_ops, atB.shape_n = shapeB, 12
        for t in range(4):
            atB.jobs.append(([qB_[:, t, g, :] for g in range(4)], qBT[:, t, :, :].rearrange("p g n -> p (g n)"), SCALE))
        atB.jobs.append(([kB[:, t, :] for t in range(4)], kBT[:, :], 1.0))
        for g in range(4):
            for qt in range(4):
                L = 256 if qt < 2 else 512
                atB.units.append(Unit([qBT[:, qt, g, :]], [kBT[:, 0:L]], [vB[:, t, :] for t in range(L // P)], L,
                                      oB[:, qt, g, :], bias=None if qt < 2 else (bandB[:, qt - 2, :], 256),
                                      sink=sinkB[:, g:g + 1]))
        atB.saves.append((lambda it: O2[:, bass.ds(1024 + it * 512, 512)].rearrange("(t p) n -> p t n", p=P),
                          oB[:, :, :, :].rearrange("p t h d -> p t (h d)")))
        atB.seal()

        atC = Attn("atC", 2)
        low_rank = 4 * 6 * 512
        ar = Arena([SCR, (AHI[0] + low_rank, AHI[1])])
        atC.place_rows(ar)
        qC, kC, vC = ar("qC", [P, 2, 4, HD]), ar("kC", [P, 4, HD]), ar("vC", [P, 4, HD])
        qCT, kCT = ar("qCT", [P, 2, 4, P]), ar("kCT", [P, 512])
        oC, tmpC = ar("oC", [P, 2, 4, HD]), ar("tmpC", [P, 2048])
        csC, gC, rC = ar("csC", [P, 2, 2, 64]), ar("gC", [P, 2, HD]), ar("rC", [P, 16])
        lat = lambda U, c0, w, step: (lambda it: U[CTX:CTX + SEQ, bass.ds(c0 + it * step, w)]
                                      .rearrange("(t p) n -> p t n", p=P))
        atC.loads += [(vC[:, :, :], tiles_of(U3, 1280, HD, HD))]
        atC.rows += [(qC[:, :, :, :].rearrange("p t h d -> p t (h d)"), lat(U3, 0, 512, 512)),
                      (kC[:, :, :], tiles_of(U3, 1024, HD, HD)),
                      (csC[:, :, :, :], lambda it: C["cs128"].rearrange("c (t p) h -> p c t h", p=P)),
                      (gC[:, 0, :], lambda it: bcast(A["c_q_g_2"][0])), (gC[:, 1, :], lambda it: bcast(A["c_k_g_2"][0]))]
        atC.norms = [(rC[:, 0:12], HD)]

        def shapeC(dve, link, it):
            q, k = qC[:, :, :, :].rearrange("p t h d -> p (t h) d"), kC[:, :, :]
            sq = tmpC[:, 0:1536].rearrange("p (m d) -> p m d", d=HD)
            link(nc.vector.tensor_tensor(sq[:, 0:8, :], q, q, ALU.mult))
            link(nc.vector.tensor_tensor(sq[:, 8:12, :], k, k, ALU.mult))
            nc.vector.tensor_reduce(rC[:, 0:12], sq, AX.X, ALU.add).then_inc(at_ss, 1)
            dve.wait_ge(at_rs, it + 1)
            for x, c, n, g in ((q, 0, 8, 0), (k, 8, 4, 1)):
                link(nc.vector.tensor_tensor(x, x, rows3(rC[:, c:c + n], HD), ALU.mult))
                link(nc.vector.tensor_tensor(x, x, cols3(gC[:, g, :], n), ALU.mult))
            cs = (csC[:, 0, :, :], csC[:, 1, :, :])
            rope(link, qC[:, :, :, :], 0, 64, cs, tmpC[:, :])
            rope(link, kC[:, 2:4, :].rearrange("p t (m d) -> p t m d", m=1), 0, 64, cs, tmpC[:, :])
        atC.shape_ops, atC.shape_n = shapeC, 18
        for t in range(2):
            atC.jobs.append(([qC[:, t, g, :] for g in range(4)], qCT[:, t, :, :].rearrange("p g n -> p (g n)"), SCALE))
        atC.jobs.append(([kC[:, t, :] for t in range(4)], kCT[:, :], 1.0))
        for g in range(4):
            for qt in range(2):
                atC.units.append(Unit([qCT[:, qt, g, :]], [kCT[:, :]], [vC[:, t, :] for t in range(4)], 512,
                                      oC[:, qt, g, :]))
        atC.saves.append((lambda it: O3[CTX:CTX + SEQ, bass.ds(it * 512, 512)].rearrange("(t p) n -> p t n", p=P),
                          oC[:, :, :, :].rearrange("p t h d -> p t (h d)")))
        atC.seal()

        atD = Attn("atD", 2, follows=True)
        ar = Arena([ALO])
        qD, kvD, peD = ar("qD", [P, 2, 4, 192]), ar("kvD", [P, 4, 4, 256]), ar("peD", [P, 4, 64])
        tmpD, csD = ar("tmpD", [P, 1024]), ar("csD", [P, 2, 2, 32])
        ar = Arena([SCR, AHI] + ar.regions)
        atD.place_rows(ar)
        qDT, qPT = ar("qDT", [P, 2, 4, P]), ar("qPT", [64, 2, 4, P])
        kDT, kPT = ar("kDT", [P, 4, 512]), ar("kPT", [64, 512])
        oD = ar("oD", [P, 2, 4, HD])
        DSC = 192 ** -0.5
        def kv_half(t, half):
            return (kvD[:, t, :, half * HD:(half + 1) * HD],
                    lambda it: KVB[t * P:(t + 1) * P, bass.ds(it * 1024, 1024)].rearrange("p (h d) -> p h d", h=4)[
                        :, :, half * HD:(half + 1) * HD])
        atD.loads += [kv_half(t, 1) for t in range(4)]
        atD.rows += [kv_half(t, 0) for t in range(4)] + \
                    [(qD[:, :, :, :].rearrange("p t h d -> p t (h d)"), lat(QB, 0, 768, 768)),
                      (peD[:, :, :], tiles_of(U3, 2304, 64, 0)),
                      (csD[:, :, :, :], lambda it: C["cs64"].rearrange("c (t p) h -> p c t h", p=P))]

        def shapeD(dve, link, it):
            cs = (csD[:, 0, :, :], csD[:, 1, :, :])
            rope(link, qD[:, :, :, :], HD, 32, cs, tmpD[:, :])
            rope(link, peD[:, 2:4, :].rearrange("p t (m d) -> p t m d", m=1), 0, 32, cs, tmpD[:, :])
        atD.shape_ops, atD.shape_n = shapeD, 12
        for t in range(2):
            atD.jobs.append(([qD[:, t, g, 0:HD] for g in range(4)], qDT[:, t, :, :].rearrange("p g n -> p (g n)"), DSC))
            atD.jobs.append(([qD[:, t, g, HD:192] for g in range(4)], qPT[:, t, :, :].rearrange("p g n -> p (g n)"), DSC))
        for g in range(4):
            atD.jobs.append(([kvD[:, t, g, 0:HD] for t in range(4)], kDT[:, g, :], 1.0))
        atD.jobs.append(([peD[:, t, :] for t in range(4)], kPT[:, :], 1.0))
        for g in range(4):
            for qt in range(2):
                atD.units.append(Unit([qDT[:, qt, g, :], qPT[:, qt, g, :]], [kDT[:, g, :], kPT[:, :]],
                                      [kvD[:, t, g, HD:256] for t in range(4)], 512, oD[:, qt, g, :]))
        atD.saves.append((lambda it: O3[CTX:CTX + SEQ, bass.ds(1024 + it * 512, 512)].rearrange("(t p) n -> p t n", p=P),
                          oD[:, :, :, :].rearrange("p t h d -> p t (h d)")))
        atD.seal()

        p2_in = [sem("p2_in0"), sem("p2_in1")]

        def p2_pool(pool):
            pool.wait_ge(at_saved, 64)
            for i, (tt, _, k0) in enumerate(p2.tts):
                if i >= 2:
                    pool.wait_ge(tr_done, p2.u0 + 3 * (i - 1))
                pool.dma_start(xn[:, i % 2, 0:1536], OB[tt * P:(tt + 1) * P, k0 * P:k0 * P + 1536])\
                    .then_inc(p2_in[i % 2], 16)

        def p2_dve(dve, i):
            dve.wait_ge(p2_in[i % 2], 16 * (i // 2 + 1))
            dve.sem_inc(xn_ready, 1)

        def gated(p, O, U, g0, norm, tag, saved):
            gi = [sem(f"{tag}_in0"), sem(f"{tag}_in1")]
            gsq, gss, grs, gmul = (sem(tag + n) for n in ("_sq", "_ss", "_rs", "_mul"))
            sub = small[:, 48:56]
            sq = stage[:, 0:2, :].rearrange("p a (b c) -> p (a b) c", c=HD)

            def pool(pool):
                for i in range(len(p.tts)):
                    pool.wait_ge(gi[i % 2], 32 * (i // 2 + 1))
                    nc.gpsimd.tensor_tensor(xn[:, i % 2, 1024:DM], xn[:, i % 2, 1024:DM], gt2[:, i % 2, 1024:DM],
                                            ALU.mult).then_inc(gmul, 1)
                    if norm:
                        pool.wait_ge(gss, i + 1)
                        pow_half(pool, sub, sub, HD, links["pool"]).then_inc(grs, 1)

            def load(act, i):
                for t in ((0, 1) if i == 0 else (i,)) if i != 1 else ():
                    tt = p.tts[t][0]
                    if t == 0:
                        act.wait_ge(at_saved, saved)
                    elif t >= 2:
                        act.wait_ge(tr_done, p.u0 + 4 * (t - 1))
                    act.dma_start(xn[:, t % 2, :], tok(O, tt)).then_inc(gi[t % 2], 16)
                    act.dma_start(gt2[:, t % 2, :], U[tt * P:(tt + 1) * P, g0:g0 + DM]).then_inc(gi[t % 2], 16)

            def act(act, i):
                if norm:
                    act.wait_ge(gi[i % 2], 32 * (i // 2 + 1))
                    if i:
                        act.wait_ge(gss, i)
                    else:
                        wait_stored(act, "in2_end")
                    nc.scalar.activation(sq, xn[:, i % 2, 0:1024].rearrange("p (h d) -> p h d", h=8), ACT.Square)\
                      .then_inc(gsq, 1)

            def dve(dve, i, link):
                x = xn[:, i % 2, :]
                dve.wait_ge(gi[i % 2], 32 * (i // 2 + 1))
                if norm:
                    xa = x[:, 0:1024].rearrange("p (h d) -> p h d", h=8)
                    dve.wait_ge(gsq, i + 1)
                    dve.wait_ge(xn_ready, p.x0 + i)
                    nc.vector.tensor_reduce(sub, sq, AX.X, ALU.add).then_inc(gss, 1)
                    link(nc.vector.tensor_tensor(x[:, 0:1024], x[:, 0:1024], gt2[:, i % 2, 0:1024], ALU.mult))
                    dve.wait_ge(grs, i + 1)
                    dve.wait_ge(gmul, i + 1)
                    ins = nc.vector.tensor_tensor(xa, xa, rows3(sub, HD), ALU.mult)
                else:
                    dve.wait_ge(gmul, i + 1)
                    ins = nc.vector.tensor_tensor(x[:, 0:1024], x[:, 0:1024], gt2[:, i % 2, 0:1024], ALU.mult)
                ins.then_inc(xn_ready, 1)
            return pool, load, act, dve

        g6_pool, g6_load, g6_act, g6_dve = gated(p6, O2, U2, 4608, True, "g6", 16 * (atB.base["saves"] + 2))
        g9_pool, g9_load, g9_act, g9_dve = gated(p9, O3, U3, 2368, False, "g9", 16 * (atD.base["saves"] + 2))

        p8_in, p8_ss, p8_rs = (sem(n) for n in ("p8_in", "p8_ss", "p8_rs"))
        lr = place("lr", [P, 4, 768], xn_at)
        gq, gk = place("gq", [P, 512], xn_at + 12288), place("gk", [P, 256], xn_at + 14336)
        lq = place("lq", [P, 4, 768], xn_at + 16384)
        p8q.src = lambda i: lr[:, 2 + i, 0:512]
        p8k.src = lambda i: lr[:, i, 512:768]

        def p8_pool(pool):
            wait_stored(pool, "in3_low")
            pool.wait_ge(pl_done, p7.u0 + len(p7.units))
            pool.dma_start(lr[:, 2:4, 0:512], U3[CTX:CTX + SEQ, 1536:2048].rearrange("(t p) n -> p t n", p=P))\
                .then_inc(p8_in, 16)
            pool.dma_start(lr[:, :, 512:768], U3[:, 2048:2304].rearrange("(t p) n -> p t n", p=P)).then_inc(p8_in, 16)
            pool.dma_start(gq[:, :], bcast(A["d_q_a_g_2"][0])).then_inc(p8_in, 16)
            pool.dma_start(gk[:, :], bcast(A["d_kv_a_g_2"][0])).then_inc(p8_in, 16)

        def p8_pool_norm(pool):
            pool.wait_ge(p8_ss, 1)
            link = links["pool"]
            pow_half(pool, small[:, 56:58], small[:, 56:58], 512, link)
            pow_half(pool, small[:, 58:62], small[:, 58:62], 256, link).then_inc(p8_rs, 1)

        def p8_dve(dve):
            link = links["dve"]
            dve.wait_ge(p8_in, 64)
            q, k = lr[:, 2:4, 0:512], lr[:, :, 512:768]
            link(nc.vector.tensor_tensor(lq[:, 2:4, 0:512], q, q, ALU.mult))
            link(nc.vector.tensor_tensor(lq[:, :, 512:768], k, k, ALU.mult))
            link(nc.vector.tensor_reduce(small[:, 56:58], lq[:, 2:4, 0:512], AX.X, ALU.add))
            nc.vector.tensor_reduce(small[:, 58:62], lq[:, :, 512:768], AX.X, ALU.add).then_inc(p8_ss, 1)
            dve.wait_ge(p8_rs, 1)
            link(nc.vector.tensor_tensor(q, q, rows3(small[:, 56:58], 512), ALU.mult))
            link(nc.vector.tensor_tensor(k, k, rows3(small[:, 58:62], 256), ALU.mult))
            link(nc.vector.tensor_tensor(q, q, cols3(gq[:, :], 2), ALU.mult))
            link(nc.vector.tensor_tensor(k, k, cols3(gk[:, :], 4), ALU.mult))
            dve.sem_inc(xn_ready, 6)

        mf_in, mf_out = sem("mf_in"), sem("mf_out")
        mid_gain = place("mid_gain", [P, DM], xn_at + 16384)
        mid_in, mid_ss, mid_rs, mid_done = (sem(n) for n in ("mid_in", "mid_ss", "mid_rs", "mid_done"))
        vec_in, vec_link = sem("vec_in"), sem("vec_link")

        def mod_pool(pool, layer, upto):
            wait_stored(pool, upto)
            cols = slice(layer * 3 * DM, (layer + 1) * 3 * DM)
            pool.dma_start(mfr[:, :, :], MODP[:, cols].rearrange("r (p n) -> p r n", p=P)).then_inc(mf_in, 16)
            pool.dma_start(mfb[:, :], A["b_mod_2"][layer].rearrange("(p n) -> p n", p=P)).then_inc(mf_in, 16)
            pool.wait_ge(mf_in, 32 * (layer + 1))
            link = links["pool"]
            link(nc.gpsimd.tensor_tensor(mfo[:, :, :], mfr[:, 0:2, :], mfr[:, 2:4, :], ALU.add))
            link(nc.gpsimd.tensor_tensor(mfo[:, :, :], mfo[:, :, :], cols3(mfb[:, :], 2), ALU.add))
            pool.dma_start(MODF[:, cols].rearrange("r (p n) -> p r n", p=P), mfo[:, :, :]).then_inc(mf_out, 16)
            pool.wait_ge(mf_out, 16 * (layer + 1))

        def mid_loads(pool):
            pool.wait_ge(pl_done, p4.u0 + len(p4.units))
            pool.dma_start(mid_gain[:, :], bcast(A["norm_final"])).then_inc(mid_in, 16)
            pool.dma_start(subg[:, :], A["a_sub_g_2"].rearrange("o d -> d o"), allow_slow_non_contiguous=True)\
                .then_inc(mid_in, 16)

        def mid_pool(pool):
            pool.wait_ge(mid_ss, 2)
            link = links["pool"]
            pow_half(pool, small[:, 62:64], small[:, 62:64], DM, link).then_inc(mid_rs, 1)

        def vec_pool(pool, layer):
            o = layer * 3 * DM
            for r, (src, c) in enumerate(((0, DM), (0, 0), (1, DM), (1, 0))):
                pool.dma_start(vec[:, V_CTX + r, :], MODF[src, o + c:o + c + DM].rearrange("(k p) -> p k", p=P),
                               allow_slow_non_contiguous=True)\
                    .then_inc(vec_in, 16)
            pool.dma_start(vec[:, V_NG, :], A["norm_g_2"][layer].rearrange("(k p) -> p k", p=P),
                           allow_slow_non_contiguous=True).then_inc(vec_in, 16)

        def vec_dve(dve, layer):
            dve.wait_ge(vec_in, 80 * (layer + 1))
            for i, r in enumerate((V_CTX, V_X)):
                nc.vector.scalar_tensor_tensor(out=vec[:, r, :], in0=vec[:, r, :], scalar=1.0, in1=vec[:, V_NG, :],
                                               op0=ALU.add, op1=ALU.mult).then_inc(vec_link, 1)
            dve.wait_ge(vec_link, 2 * (layer + 1))

        def mid_act(act):
            wait_freed(act, "mlp")
            for tt in range(2):
                nc.scalar.activation(mid_junk[:, tt, :], XR[:, tt, :], ACT.Square,
                                     accum_out=small[:, 62 + tt:63 + tt]).then_inc(mid_ss, 1)
        mid_junk = place("mid_junk", [P, 2, DM], AHI[0])

        def mid_dve(dve):
            link = links["dve"]
            dve.wait_ge(mid_in, 32)
            link(nc.vector.tensor_scalar(subg[:, :], subg[:, :], 1.0 - LAM_INIT, None, ALU.mult))
            dve.wait_ge(mid_rs, 1)
            for tt in range(2):
                nc.vector.scalar_tensor_tensor(out=XR[:, tt, :], in0=XR[:, tt, :], scalar=small[:, 62 + tt:63 + tt],
                                               in1=mid_gain[:, :], op0=ALU.mult, op1=ALU.mult).then_inc(mid_done, 1)
            dve.wait_ge(mid_done, 2)

        gbc_in = sem("gbc_in")

        def gbc_pool(pool, layer, p):
            pool.wait_ge(pl_done, p.u0 + len(p.units))
            o = layer * 3 * DM + 2 * DM
            pool.dma_start(gbc_c[:, :], bcast(MODF[0, o:o + DM])).then_inc(gbc_in, 16)
            pool.dma_start(gbc_x[:, :], bcast(MODF[1, o:o + DM])).then_inc(gbc_in, 16)

        fin_in, fin_ss, fin_rs, fin_y, fin_out = (sem(n) for n in ("fin_in", "fin_ss", "fin_rs", "fin_y",
                                                                   "fin_out"))
        fin_gain = place("fin_gain", [P, DM], ALO[0])
        fin_junk = place("fin_junk", [P, 2, DM], AHI[0])

        x_in, cx_in = sem("x_in"), sem("cx_in")
        block = ctx.enter_context(nc.Block())

        @block.sync
        def _(sp):
            for tt in range(2):
                sp.dma_start(XR[:, tt, :], A["x"][0, tt * P:(tt + 1) * P, :]).then_inc(x_in, 16)
            for name in ("qkv0", "qkv", "qkv_end", "gates", "cmp1"):
                sp_stream(sp, stages[name])
            wait_stored(sp, "qkv_end")
            sp.wait_ge(brev_out, 16)
            at1.sp_rows(sp)
            wait_freed(sp, "gates")
            sp.wait_ge(nsa_out, 16)
            sp.wait_ge(cmp_out, 32)
            sp.wait_ge(bt_out, 16)
            at1.sp(sp)
            for name in ("branch", "out1", "mlp", "in2", "in2_end"):
                sp_stream(sp, stages[name])
            wait_stored(sp, "in2")
            atA.sp_rows(sp)
            wait_freed(sp, "in2_end")
            atA.sp(sp)
            atB.sp_rows(sp)
            atB.sp(sp)
            for name in ("out2", "in3_low", "in3", "in3_gates", "qb"):
                sp_stream(sp, stages[name])
            wait_stored(sp, "in3")
            atC.sp_rows(sp)
            sp_stream(sp, stages["kvb"])
            wait_stored(sp, "kvb")
            wait_freed(sp, "kvb")
            atC.sp(sp)
            atD.sp_rows(sp)
            atD.sp(sp)
            sp_stream(sp, stages["out3"])

        @block.gpsimd
        def _(pool):
            links["pool"].eng = pool
            setup_gpsimd(pool)
            n1.pool(pool)
            setup_brev(pool)
            for name in ("qkv0", "qkv", "qkv_end"):
                pool_stream(pool, stages[name])
            cmp_pool_loads(pool)
            pool_stream(pool, stages["gates"])
            cmp_pool_store(pool)
            at1.pool(pool)
            p2_pool(pool)
            wait_stored(pool, "gates")
            pool.wait_ge(pl_done, p2.u0 + len(p2.units))
            pool_stream(pool, stages["branch"])
            n4.pool(pool)
            pool.wait_ge(pl_done, p3.u0 + len(p3.units))
            for tt in range(2):
                pool.dma_start(CX[:, tt, :], A["ctx_2"][0, tt * P:(tt + 1) * P, :]).then_inc(cx_in, 16)
            mid_loads(pool)
            pool_stream(pool, stages["mlp"])
            mod_pool(pool, 0, "mlp")
            vec_pool(pool, 0)
            mid_pool(pool)
            n5.pool(pool)
            pool_stream(pool, stages["in2"])
            pool_stream(pool, stages["in2_end"])
            atA.pool(pool)
            atB.pool(pool)
            g6_pool(pool)
            gbc_pool(pool, 0, p6)
            mod_pool(pool, 1, "modB")
            wait_freed(pool, "out2")
            pool.wait_ge(gres_tmp, 16)
            vec_pool(pool, 1)
            n7.pool(pool)
            pool_stream(pool, stages["in3_low"])
            p8_pool(pool)
            pool_stream(pool, stages["in3"])
            p8_pool_norm(pool)
            pool_stream(pool, stages["in3_gates"])
            pool_stream(pool, stages["qb"])
            pool_stream(pool, stages["kvb"])
            atC.pool(pool)
            atD.pool(pool)
            g9_pool(pool)
            gbc_pool(pool, 1, p9)
            wait_freed(pool, "out3")
            pool.dma_start(fin_gain[:, :], bcast(A["final_g_2"])).then_inc(fin_in, 16)
            pool.wait_ge(fin_ss, 2)
            link = links["pool"]
            pow_half(pool, small[:, 46:48], small[:, 46:48], DM, link).then_inc(fin_rs, 1)
            for tt in range(2):
                pool.wait_ge(fin_y, tt + 1)
                pool.dma_start(out[0, tt * P:(tt + 1) * P, :], XR[:, tt, :]).then_inc(fin_out, 16)
            pool.wait_ge(fin_out, 32)

        @block.tensor
        def _(pe):
            setup_pe(pe)
            p1.pe(pe)
            p1.finish(pe)
            for name in ("qkv0", "qkv", "qkv_end", "gates"):
                pe_stream(pe, stages[name])
            cmp_pe_prep(pe)
            pe.wait_ge(cmp_hi, 1)
            pe_stream(pe, stages["cmp1"])
            cmp_pe(pe)
            at1.pe(pe)
            p2.pe(pe)
            p2.finish(pe)
            pe_stream(pe, stages["branch"])
            p3.pe(pe)
            p3.finish(pe)
            pe_stream(pe, stages["out1"])
            p4.pe(pe)
            p4.finish(pe)
            pe_stream(pe, stages["mlp"])
            p5.pe(pe)
            p5.finish(pe)
            pe_stream(pe, stages["in2"])
            pe_stream(pe, stages["in2_end"])
            wait_freed(pe, "in2_end")
            atA.pe(pe)
            atB.pe(pe)
            p6.pe(pe)
            p6.finish(pe)
            pe_stream(pe, stages["out2"])
            p7.pe(pe)
            p7.finish(pe)
            for name in ("in3_low", "in3", "in3_gates"):
                pe_stream(pe, stages[name])
            p8q.pe(pe)
            p8k.pe(pe)
            p8q.finish(pe)
            p8k.finish(pe)
            pe_stream(pe, stages["qb"])
            pe_stream(pe, stages["kvb"])
            wait_freed(pe, "kvb")
            atC.pe(pe)
            atD.pe(pe)
            p9.pe(pe)
            p9.finish(pe)
            pe_stream(pe, stages["out3"])

        @block.scalar
        def _(act):
            setup_act_loads(act)
            act.wait_ge(x_in, 32)

            def p1_produce(eng, i):
                n1.act(eng, i)
                if i == 1:
                    setup_act(eng)
            p1.act(act, p1_produce)
            setup_bias_tiles(act)
            for name in ("qkv0", "qkv", "qkv_end", "gates", "cmp1"):
                act_stream(act, stages[name])
            cmp_act(act)
            at1.act(act)
            p2.act(act)
            act_stream(act, stages["branch"])
            p3.act(act)
            act_stream(act, stages["out1"])
            p4.act(act, n4.act)
            act_stream(act, stages["mlp"])
            mid_act(act)
            act.wait_ge(mid_done, 2)
            act.wait_ge(cx_in, 32)
            act.wait_ge(vec_link, 2)
            p5.act(act, n5.act)
            act_stream(act, stages["in2"])
            act_stream(act, stages["in2_end"])
            atA.act(act)
            atB.act(act)
            p6.act(act, g6_act, g6_load)
            act_stream(act, stages["out2"])
            act.wait_ge(gres_tmp, 16)
            act.wait_ge(vec_link, 4)
            p7.act(act, n7.act)
            for name in ("in3_low", "in3", "in3_gates"):
                act_stream(act, stages[name])
            p8q.act(act)
            p8k.act(act)
            act_stream(act, stages["qb"])
            act_stream(act, stages["kvb"])
            atC.act(act)
            atD.act(act)
            p9.act(act, g9_act, g9_load)
            act_stream(act, stages["out3"])
            act.wait_ge(gres_tmp, 24)
            for tt in range(2):
                nc.scalar.activation(fin_junk[:, tt, :], XR[:, tt, :], ACT.Square,
                                     accum_out=small[:, 46 + tt:47 + tt]).then_inc(fin_ss, 1)

        @block.vector
        def _(dve):
            links["dve"].eng = dve
            setup_vector(dve)
            p1.dve(dve, n1.dve)
            for name in ("qkv0", "qkv", "qkv_end", "gates"):
                dve_stream(dve, stages[name])
            at1.open_rows(dve)
            cmp_dve_prep(dve)
            dve_stream(dve, stages["cmp1"])
            cmp_dve_gelu(dve)
            dve.wait_ge(cmp_out, 32)
            at1.dve(dve)
            p2.dve(dve, p2_dve)
            dve_stream(dve, stages["branch"])
            dve.sem_inc(xn_ready, 2)
            p3.dve(dve)
            dve_stream(dve, stages["out1"])
            p4.dve(dve, n4.dve)
            dve_stream(dve, stages["mlp"])
            mid_dve(dve)
            vec_dve(dve, 0)
            p5.dve(dve, n5.dve)
            dve_stream(dve, stages["in2"])
            atA.open_rows(dve)
            dve_stream(dve, stages["in2_end"])
            atA.dve(dve)
            atB.dve(dve)
            link6 = links["dve"]
            p6.dve(dve, lambda e, i: g6_dve(e, i, link6))
            dve.wait_ge(gbc_in, 32)
            dve_stream(dve, stages["out2"])
            vec_dve(dve, 1)
            p7.dve(dve, n7.dve)
            dve_stream(dve, stages["in3_low"])
            dve_stream(dve, stages["in3"])
            p8_dve(dve)
            dve_stream(dve, stages["in3_gates"])
            p8q.dve(dve)
            p8k.dve(dve)
            atC.open_rows(dve)
            dve_stream(dve, stages["qb"])
            dve_stream(dve, stages["kvb"])
            atC.dve(dve)
            atD.dve(dve)
            link9 = links["dve"]
            p9.dve(dve, lambda e, i: g9_dve(e, i, link9))
            dve.wait_ge(gbc_in, 64)
            dve_stream(dve, stages["out3"])
            dve.wait_ge(fin_in, 16)
            dve.wait_ge(fin_rs, 1)
            for tt in range(2):
                nc.vector.scalar_tensor_tensor(out=XR[:, tt, :], in0=XR[:, tt, :], scalar=small[:, 46 + tt:47 + tt],
                                               in1=fin_gain[:, :], op0=ALU.mult, op1=ALU.mult).then_inc(fin_y, 1)


def constants():
    dist = 255 - np.arange(G)
    n = np.maximum(dist, 0)
    large = np.minimum(16 + (np.log(np.maximum(n, 1) / 16.0) / np.log(8.0) * 16).astype(np.int64), BUCKETS - 1)
    bucket = np.where(n < 16, n, large)
    onehot = (np.arange(BUCKETS)[:, None] == bucket[None]).astype(np.float32)
    bmask = np.zeros((24, G), np.float32)
    bmask[:, dist < 0] = NEG
    bmask[8:16, dist >= 128] = NEG
    valid = (np.arange(P) >= 31).astype(np.float32)[:, None]
    q, k = np.arange(SEQ)[:, None], np.arange(SEQ)[None]
    band = np.where(np.abs(k - q) <= 128, 0.0, NEG).astype(np.float32)

    def angles(dim):
        pos = np.arange(SEQ)
        r, c = (pos // 64).astype(np.float32), (pos % 64).astype(np.float32)
        f = dim // 4
        inv = (np.float32(10000.0) ** (-np.arange(f, dtype=np.float32) / np.float32(f))).astype(np.float32)
        a = np.concatenate([r[:, None] * inv[None], c[:, None] * inv[None]], -1)
        return np.stack([np.cos(a), np.sin(a)]).astype(np.float32)
    return dict(onehot=onehot, bmask=bmask, valid=valid, band=band, cs128=angles(128), cs64=angles(64))


_INS = ["x", "w_in", "cmp_pos", "cmp_w1", "cmp_w2", "swa_sinks", "w_branch", "w_out", "w_mlp_in", "w_mlp_out",
        "norm_mix", "norm_mlp", "norm_final", "rel_bias", "c_2", "ctx_2", "c_ctx_2", "w_mod_2", "b_mod_2",
        "norm_g_2", "w_o_2", "final_g_2", "e_w_in_2", "a_lam_q1_2", "a_lam_k1_2", "a_lam_q2_2", "a_lam_k2_2",
        "a_sub_g_2", "b_sink_2", "o_w_in_2", "c_q_g_2", "c_k_g_2", "d_q_a_g_2", "d_kv_a_g_2", "d_w_q_b_2",
        "d_w_kv_b_2"]


def kernel(**inputs):
    import concourse.bacc as _bacc
    from concourse.bass_utils import run_bass_kernel_spmd as _run

    nc = _bacc.Bacc("TRN2", target_bir_lowering=False, num_devices=1)
    arrays, given, consts = {}, {}, {}
    for group_, names, values in (("in", _INS, inputs), ("const", None, constants())):
        for name in names or values:
            a = np.ascontiguousarray(values[name])
            arrays[f"{group_}_{name}"] = a
            ap = nc.dram_tensor(f"{group_}_{name}", a.shape, mybir.dt.from_np(a.dtype), kind="ExternalInput").ap()
            (given if group_ == "in" else consts)[name] = ap
    out = nc.dram_tensor("out", (1, SEQ, DM), F32, kind="ExternalOutput").ap()
    two_blocks(nc, given, consts, out)
    r = _run(nc, [arrays], core_ids=[0])
    return r.results[0]["out"]
```
